# Optimizing a Trainium2 kernel written in Bass

```python
import jax, jax.numpy as jnp
from jax import lax
import numpy as np

D_MODEL = 1024
BATCH = 1
SEQ = 256
DEPTH = 1

GRID_W = 64
CTX_LEN = 256
D_CONV = D_MODEL // 2
CONV_K = 3
D_SSM = D_MODEL // 2
SSM_GROUP = 16
N_GROUPS = D_SSM // SSM_GROUP
STATE = 64
N_DIR = 2
D_FF = -(-8 * D_MODEL // (3 * 256)) * 256
D_IN_PROJ = 3 * D_CONV + D_SSM + 2 * D_MODEL
SPLITS = [D_CONV, 2 * D_CONV, 3 * D_CONV, 3 * D_CONV + D_SSM, 3 * D_CONV + D_SSM + D_MODEL]
U_LO, U_HI = 3 * D_CONV, 3 * D_CONV + D_SSM
RMS_EPS = 1e-6
DT_MIN, DT_MAX = 1e-3, 1e-1

kernel_name = "hybrid_shortconv_s5_adaln_prefix_block"

def rmsnorm(x, g):
    xf = x.astype(jnp.float32)
    y = xf * lax.rsqrt(jnp.mean(xf * xf, axis=-1, keepdims=True) + RMS_EPS)
    return (y * g.astype(jnp.float32)).astype(x.dtype)

def modulate(h, shift, scale):
    return h * (1 + scale) + shift

def conv_centered(z, w):
    pad = CONV_K // 2
    n = z.shape[-2]
    zp = jnp.pad(z, [(0, 0)] * (z.ndim - 2) + [(pad, pad), (0, 0)])
    return sum(lax.slice_in_dim(zp, k, k + n, axis=z.ndim - 2) * w[k] for k in range(CONV_K))

def zoh(lam_re, lam_im, log_dt, b_re, b_im):
    lam_re = lam_re.astype(jnp.float32)
    lam_im = lam_im.astype(jnp.float32)
    dt = jnp.exp(log_dt.astype(jnp.float32))[:, None]
    mag = jnp.exp(lam_re * dt)
    a_re = mag * jnp.cos(lam_im * dt)
    a_im = mag * jnp.sin(lam_im * dt)
    nr, ni = a_re - 1.0, a_im
    den = lam_re * lam_re + lam_im * lam_im
    f_re = (nr * lam_re + ni * lam_im) / den
    f_im = (ni * lam_re - nr * lam_im) / den
    br, bi = b_re.astype(jnp.float32), b_im.astype(jnp.float32)
    bb_re = f_re[..., None] * br - f_im[..., None] * bi
    bb_im = f_re[..., None] * bi + f_im[..., None] * br
    return a_re, a_im, bb_re, bb_im

def _linrec_combine(e1, e2):
    a1r, a1i, b1r, b1i = e1
    a2r, a2i, b2r, b2i = e2
    return (a2r * a1r - a2i * a1i,
            a2r * a1i + a2i * a1r,
            a2r * b1r - a2i * b1i + b2r,
            a2r * b1i + a2i * b1r + b2i)

def ssm_states(u, lam_re, lam_im, log_dt, b_re, b_im, h0):
    bsz, n = u.shape[0], u.shape[1]
    ug = u.astype(jnp.float32).reshape(bsz, n, N_GROUPS, SSM_GROUP)
    states = []
    for d in range(N_DIR):
        reverse = d == 1
        a_re, a_im, bb_re, bb_im = zoh(lam_re[d], lam_im[d], log_dt[d], b_re[d], b_im[d])
        bu_re = jnp.einsum('bngh,gph->bngp', ug, bb_re)
        bu_im = jnp.einsum('bngh,gph->bngp', ug, bb_im)
        if h0 is not None:
            hr, hi = h0[d]
            first = n - 1 if reverse else 0
            bu_re = bu_re.at[:, first].add(a_re * hr - a_im * hi)
            bu_im = bu_im.at[:, first].add(a_re * hi + a_im * hr)
        ar = jnp.broadcast_to(a_re, bu_re.shape)
        ai = jnp.broadcast_to(a_im, bu_re.shape)
        _, _, s_re, s_im = lax.associative_scan(
            _linrec_combine, (ar, ai, bu_re, bu_im), reverse=reverse, axis=1)
        states.append((s_re, s_im))
    return states

def final_states(states):
    (fr, fi), (br, bi) = states
    return [(fr[:, -1], fi[:, -1]), (br[:, 0], bi[:, 0])]

def ssm_readout(states, u, c_re, c_im, d_skip):
    bsz, n = u.shape[0], u.shape[1]
    y = u.astype(jnp.float32) * d_skip.astype(jnp.float32)
    for d, (s_re, s_im) in enumerate(states):
        yd = (jnp.einsum('bngp,ghp->bngh', s_re, c_re[d].astype(jnp.float32))
              - jnp.einsum('bngp,ghp->bngh', s_im, c_im[d].astype(jnp.float32)))
        y = y + yd.reshape(bsz, n, D_SSM)
    return y.astype(u.dtype)

def mixer(h, lp, rows, h0):
    z = h @ lp['w_in'] + lp['b_in']
    g_b, g_c, x_in, u, gate_a, gate_b = jnp.split(z, SPLITS, axis=-1)
    v = g_c * x_in
    if rows is None:
        v = conv_centered(v, lp['conv_w'])
    else:
        bsz, n, ch = v.shape
        v = conv_centered(v.reshape(bsz, rows, GRID_W, ch), lp['conv_w']).reshape(bsz, n, ch)
    y_a = (g_b * v) @ lp['w_out_a']
    states = ssm_states(u, lp['lam_re'], lp['lam_im'], lp['log_dt'], lp['b_re'], lp['b_im'], h0)
    s = jax.nn.gelu(ssm_readout(states, u, lp['c_re'], lp['c_im'], lp['d_skip']))
    glu_v, glu_g = jnp.split(s @ lp['w_glu'] + lp['b_glu'], 2, axis=-1)
    y_b = glu_v * jax.nn.sigmoid(glu_g)
    merged = jax.nn.sigmoid(gate_a) * y_a + jax.nn.sigmoid(gate_b) * y_b
    return merged @ lp['w_o'], states

def swiglu(h, w_in, w_out):
    g, u = jnp.split(h @ w_in, 2, axis=-1)
    return (jax.nn.silu(g) * u) @ w_out

def setup_inputs(seed: int = 0) -> dict:
    key = jax.random.key(seed)
    ks = jax.random.split(key, 32)
    f32 = jnp.float32
    nrm = lambda k, shape, s: jax.random.normal(k, shape, f32) * s
    n_idx = jnp.arange(STATE, dtype=f32)
    lam_re = -0.5 + nrm(ks[10], (DEPTH, N_DIR, N_GROUPS, STATE), 0.01)
    lam_im = jnp.pi * n_idx + nrm(ks[11], (DEPTH, N_DIR, N_GROUPS, STATE), 0.01)
    log_dt = jax.random.uniform(ks[12], (DEPTH, N_DIR, N_GROUPS), f32,
                                np.log(DT_MIN).astype(np.float32), np.log(DT_MAX).astype(np.float32))
    return {
        "x": nrm(ks[0], (BATCH, SEQ, D_MODEL), 1.0),
        "c": nrm(ks[1], (BATCH, D_MODEL), 1.0),
        "ctx": nrm(ks[2], (BATCH, CTX_LEN, D_MODEL), 1.0),
        "c_ctx": nrm(ks[3], (D_MODEL,), 1.0),
        "w_mod": nrm(ks[4], (DEPTH, D_MODEL, 6 * D_MODEL), 0.5 * D_MODEL ** -0.5),
        "b_mod": nrm(ks[5], (DEPTH, 6 * D_MODEL), 0.01),
        "norm1_g": 1.0 + nrm(ks[6], (DEPTH, D_MODEL), 0.02),
        "norm2_g": 1.0 + nrm(ks[7], (DEPTH, D_MODEL), 0.02),
        "w_in": nrm(ks[8], (DEPTH, D_MODEL, D_IN_PROJ), D_MODEL ** -0.5),
        "b_in": nrm(ks[9], (DEPTH, D_IN_PROJ), 0.01),
        "conv_w": nrm(ks[13], (DEPTH, CONV_K, D_CONV), CONV_K ** -0.5),
        "w_out_a": nrm(ks[14], (DEPTH, D_CONV, D_MODEL), D_CONV ** -0.5),
        "lam_re": lam_re,
        "lam_im": lam_im,
        "log_dt": log_dt,
        "b_re": nrm(ks[15], (DEPTH, N_DIR, N_GROUPS, STATE, SSM_GROUP), (2 * SSM_GROUP) ** -0.5),
        "b_im": nrm(ks[16], (DEPTH, N_DIR, N_GROUPS, STATE, SSM_GROUP), (2 * SSM_GROUP) ** -0.5),
        "c_re": nrm(ks[17], (DEPTH, N_DIR, N_GROUPS, SSM_GROUP, STATE), (2 * STATE) ** -0.5),
        "c_im": nrm(ks[18], (DEPTH, N_DIR, N_GROUPS, SSM_GROUP, STATE), (2 * STATE) ** -0.5),
        "d_skip": nrm(ks[19], (DEPTH, D_SSM), 1.0),
        "w_glu": nrm(ks[20], (DEPTH, D_SSM, 2 * D_MODEL), D_SSM ** -0.5),
        "b_glu": nrm(ks[21], (DEPTH, 2 * D_MODEL), 0.01),
        "w_o": nrm(ks[22], (DEPTH, D_MODEL, D_MODEL), D_MODEL ** -0.5),
        "w_ff_in": nrm(ks[23], (DEPTH, D_MODEL, 2 * D_FF), D_MODEL ** -0.5),
        "w_ff_out": nrm(ks[24], (DEPTH, D_FF, D_MODEL), D_FF ** -0.5),
        "final_g": 1.0 + nrm(ks[25], (D_MODEL,), 0.02),
    }

def reference(x, c, ctx, c_ctx, w_mod, b_mod, norm1_g, norm2_g, w_in, b_in, conv_w, w_out_a,
              lam_re, lam_im, log_dt, b_re, b_im, c_re, c_im, d_skip, w_glu, b_glu, w_o,
              w_ff_in, w_ff_out, final_g):
    rows = x.shape[1] // GRID_W
    silu_c = jax.nn.silu(c)
    silu_cc = jax.nn.silu(c_ctx)
    for l in range(DEPTH):
        last = l == DEPTH - 1
        lp = {'w_in': w_in[l], 'b_in': b_in[l], 'conv_w': conv_w[l], 'w_out_a': w_out_a[l],
              'lam_re': lam_re[l], 'lam_im': lam_im[l], 'log_dt': log_dt[l],
              'b_re': b_re[l], 'b_im': b_im[l], 'c_re': c_re[l], 'c_im': c_im[l],
              'd_skip': d_skip[l], 'w_glu': w_glu[l], 'b_glu': b_glu[l], 'w_o': w_o[l]}
        sh1, sc1, g1, sh2, sc2, g2 = [m[:, None, :] for m in
                                      jnp.split(silu_c @ w_mod[l] + b_mod[l], 6, axis=-1)]
        n_ctx_mod = 2 if last else 6
        modc = jnp.split(silu_cc @ w_mod[l][:, :n_ctx_mod * D_MODEL]
                         + b_mod[l][:n_ctx_mod * D_MODEL], n_ctx_mod, axis=-1)
        hc = modulate(rmsnorm(ctx, norm1_g[l]), modc[0], modc[1])
        if last:
            u_ctx = hc @ w_in[l][:, U_LO:U_HI] + b_in[l][U_LO:U_HI]
            ctx_states = ssm_states(u_ctx, lp['lam_re'], lp['lam_im'], lp['log_dt'],
                                    lp['b_re'], lp['b_im'], None)
        else:
            out_c, ctx_states = mixer(hc, lp, None, None)
        h0 = final_states(ctx_states)
        h = modulate(rmsnorm(x, norm1_g[l]), sh1, sc1)
        out, _ = mixer(h, lp, rows, h0)
        x = x + g1 * out
        x = x + g2 * swiglu(modulate(rmsnorm(x, norm2_g[l]), sh2, sc2), w_ff_in[l], w_ff_out[l])
        if not last:
            ctx = ctx + modc[2] * out_c
            ctx = ctx + modc[5] * swiglu(modulate(rmsnorm(ctx, norm2_g[l]), modc[3], modc[4]),
                                         w_ff_in[l], w_ff_out[l])
    return rmsnorm(x, final_g)


_drawn_inputs = setup_inputs


def setup_inputs(seed=0):
    import zlib

    import numpy as np

    out = dict(_drawn_inputs(seed))
    spreads = {}
    factors = {'ctx': 64.0,
     'c_ctx': 64.0,
     'b_mod': 4.708,
     'norm1_g': 7.414,
     'norm2_g': 64.0,
     'b_in': 8.0,
     'lam_re': 64.0,
     'lam_im': 64.0,
     'log_dt': 64.0,
     'b_re': 64.0,
     'b_im': 64.0,
     'c_re': 64.0,
     'c_im': 64.0,
     'b_glu': 200.0,
     'final_g': 22.185,
     'd_skip': 8.0,
     'w_glu': 7.178}
    for name, (base, spread) in spreads.items():
        noise = np.random.default_rng([zlib.crc32(name.encode()), seed]).standard_normal(out[name].shape)
        drawn = base * np.exp(spread * noise) if base else spread * noise
        out[name] = __import__('jax').numpy.asarray(drawn.astype(out[name].dtype))
    for name, factor in factors.items():
        out[name] = (out[name] * factor).astype(out[name].dtype)
    return out
```

```python
from contextlib import ExitStack

import concourse.bass as bass
from concourse import mybir

ACT = mybir.ActivationFunctionType
ALU = mybir.AluOpType
F32 = mybir.dt.float32
F32R = mybir.dt.float32r

P = 128
D = 1024
KD = D // P
NT = 256
DC = D // 2
KC = DC // P
DFF = 2816
KF = DFF // P
GRID_W = 64
H = 16
NG = DC // H
NS = 64
DG = 2 * NG
CH = 8
NC = NT // CH
EPS = 1e-6
PI = 3.141592653589793
TWO_PI_HI, TWO_PI_MID = 6.28125, 0.0019350051879882812
TWO_PI_LO = 2 * PI - TWO_PI_HI - TWO_PI_MID
PI_BELOW = 3.1415925
ROUND = 1.5 * 2.0 ** 23

V_BMOD, V_BIN, V_BGLU, V_N1, V_N2, V_FG, V_CONV = 0, 48, 76, 92, 100, 108, 116
C_GB, C_GC, C_XIN, C_U, C_GA, C_GATEB = 0, DC, 2 * DC, 3 * DC, 4 * DC, 4 * DC + D

N_RAW = 3
UNIT = 2048
HALF = UNIT // 2
N_PIECE = 4

def build(nc, t, out, ctx):
    base = -(-nc.sbuf_base // 64) * 64

    def at(name, kb, shape, dt=F32):
        return nc.alloc_sbuf_tensor_at(name, shape, dt, offset=base + int(kb * 1024))

    raw = at("raw", 0, [P, N_RAW, UNIT])
    w_hi = at("w_hi", 24, [P, N_RAW, UNIT], F32R)
    w_lo = at("w_lo", 48, [P, N_RAW, UNIT], F32R)
    hT = at("hT", 24, [P, KD, CH, 2, NC])
    xnT = at("xnT", 40, [P, KD, 2 * NT])
    xtok = at("xtok", 56, [P, 4, D])
    b_half = at("b_half", 40, [P, 2, 512])
    b_T = at("b_T", 44, [P, 4, 512])
    gbv = at("gbv", 52, [P, KC, NT])
    mod_acc = at("mod_acc", 56, [P, 4 * D])
    rows_in = at("rows_in", 72, [P, P])
    crow_in = at("crow_in", 72.5, [16, P])
    c_pow = at("c_pow", 72, [P, DG, CH * H])
    xT = at("xT", 72, [P, KD, NT])
    xtok2 = at("xtok2", 80, [P, 2, D])
    x1T = at("x1T", 88, [P, KD, NT])
    x1g = at("x1g", 96, [P, KD, NT])
    diag = at("diag", 104, [P, 4, P])
    sq_junk = at("sq_junk", 106, [P, D])
    v_rows = at("v_rows", 104, [2 * NC, NG, CH, H])
    X = at("X", 104, [P, DG, 2 * NC])
    p_rev = at("p_rev", 116, [P, NG, NC])
    m_hi = at("m_hi", 104, [P, KD, NT], F32R)
    m_lo = at("m_lo", 112, [P, KD, NT], F32R)
    u_pack = at("u_pack", 120, [P, NG, 2 * NC])
    r_rows = at("r_rows", 128, [H, 8, 256])
    p_st = at("p_st", 128, [P, DG, NC])
    toep = at("toep", 136, [P, NG, CH * H])
    h2_hi = at("h2_hi", 136, [P, KD, NT], F32R)
    h2_lo = at("h2_lo", 144, [P, KD, NT], F32R)
    piece = at("piece", 152, [P, N_PIECE, D])
    par_b = at("par_b", 168, [P, 2, DG, H])
    par_c = at("par_c", 176, [P, 2, DG, H])
    ya = at("ya", 168, [P, KD, NT])
    sgb = at("sgb", 176, [P, KD, NT])
    a_hi = at("a_hi", 168, [P, 2, NT], F32R)
    a_lo = at("a_lo", 170, [P, 2, NT], F32R)
    silu_g = at("silu_g", 172, [P, 2, NT])
    gu = at("gu", 174, [P, 2, NT])
    e_re = at("e_re", 184, [P, 9, DG])
    e_im = at("e_im", 186.25, [P, 9, DG])
    tc = at("tc", 188.5, [P, 2, DG, CH])
    s_hi = at("s_hi", 184, [P, KC, NT], F32R)
    s_lo = at("s_lo", 188, [P, KC, NT], F32R)
    fin = at("fin", 184, [P, 2, D])
    sm = at("sm", 192.5, [P, 16, DG])
    tA = at("tA", 197, [P, 512])
    tB = at("tB", 199, [P, 512])
    s32 = at("s32", 197, [P, KC, NT])
    zrow = at("zrow", 178, [1, P + 512])
    mrg = at("mrg", 192.5, [P, 2, NT])
    yb = at("yb", 194.5, [P, 2, NT])
    sq = at("sq", 197, [P, 2, NT])
    bc = at("bc", 199, [P, 2, NT])
    gv = at("gv", 201, [P, 2, NT])
    cv = at("cv", 203, [P, 2, NT])
    y_rows = at("y_rows", 201, [P, CH, 8, H])
    sg = at("sg", 201, [P, 2, NT])
    end = [205.0]

    def small(name, cols, rows=P):
        end[0] += -(-cols // 8) * 8 / 256
        return at(name, end[0] - -(-cols // 8) * 8 / 256, [rows, cols])

    ident, ones, vecT = small("ident", P), small("ones", P), small("vecT", P)
    zeros, csil, bu, d_skip = small("zeros", 32), small("csil", 16), small("bu", NG), small("d_skip", NG, H)
    sgn, halfpi, epsc = small("sgn", 1), small("halfpi", 1), small("epsc", 1)
    ssum, srow, rstd = small("ssum", 4), small("srow", 4), small("rstd", 4)
    mod1, gs1, mod2, gs2 = small("mod1", 32), small("gs1", 16), small("mod2", 32), small("gs2", 8)
    d_diag = at("d_diag", 196.5, [H, 8, H])
    assert end[0] <= 207.7, end[0]

    bank = [ctx.enter_context(nc.psum_tensor(f"bank{i}", [P, 512], F32)) for i in range(8)]
    r_dram = nc.dram_tensor("r_scratch", (NG, H, 240), F32, kind="Internal").ap()

    def sem(name):
        return ctx.enter_context(nc.semaphore(name))

    rows_in_s, lam_s, par_c_s, par_b_s, x_s, ctx_s, pack_s, xtok2_s, out_s, r_out_s, toep_s = (sem(n) for n in (
        "rows_loaded", "lam_loaded", "par_c_loaded", "par_b_loaded", "x_loaded", "ctx_loaded", "packs_loaded",
        "xtok2_loaded", "out_stored", "r_rows_stored", "toep_loaded"))
    raw_full = [sem(f"raw_full{i}") for i in range(N_RAW)]
    piece_full = [sem(f"piece_full{i}") for i in range(N_PIECE)]
    piece2_full = [sem(f"piece2_full{i}") for i in range(N_PIECE)]
    S = {n: sem(n) for n in (
        "zeroed consts dt_ready lamdt_ready mag_ready trig_arg sin_done dve_step powers_ready "
        "rows_T csil_ready vec_ready sums_done sqrt_done diag_ready xn_mm xn_evac gs_ready h_ready "
        "piece_used_pe piece_used_dve acc_ready mod2_mm mod2_ready "
        "cpow_ready h_mm h_evac r_added u_mm u_rows u_T u_packed b_ready b_Tmm b_Tevac x_mm x_evac back_done rev_ready scan_done "
        "raw_used mm_done evac_act evac_dve ya_scaled y_mm y_evac s_T s_gelu s_hi_done s_ready "
        "hi_done lo_done sg_ready mrg_ready mul_done m_hi_done m_ready xT_mm xT_evac "
        "sq_ready x1g_ready ss_mm sqrt2_done t2_ready h2_hi_done h2_ready zrow_ready "
        "gate_mm up_mm silu_done prod_done a_hi_done act_ready fo_used x2_mm x2_ready sqf_ready xg_ready ssf_mm "
        "fin_T sqrt3_done rstd3_done fin_act fin_dve").split()}

    w_in, w_oa, w_glu, w_o, w_fi, w_fo = (t[n] for n in ("w_in", "w_out_a", "w_glu", "w_o", "w_ff_in", "w_ff_out"))

    def rows_of(w, col, n):
        return w[:, col:col + n].rearrange("(k p) n -> p k n", p=P)

    units = [(KD, [(0, 256, rows_of(w_in, C_U + 256 * q, 256))]) for q in range(2)]
    for q in range(2):
        units += [(KD, [(0, 256, rows_of(w_in, c + 256 * q, 256))]) for c in (C_GC, C_XIN, C_GB)]
    units += [(KC, [(0, 512, rows_of(w_oa, 512 * q, 512))]) for q in range(2)]
    units += [(KD, [(0, 256, rows_of(w_in, C_GA + 256 * q, 256))]) for q in range(8)]
    n_native = len(units)
    units += [(KC, [(256 * j, 256, rows_of(w_glu, c + 256 * q, 256)) for j, c in enumerate((D, 0))]) for q in range(4)]
    units += [(KD, [(0, 256, rows_of(w_o, 256 * q, 256))]) for q in range(4)]
    n_pre = len(units)
    n_turn = KF // 2
    U0_GC, U0_OA, U0_GATE, U0_GLU, U0_WO = 2, 8, 10, n_native, n_native + 4
    split0 = 2 * (n_pre - n_native)
    ffn_slot = [(n_pre + j) % N_RAW for j in range(3)]
    loads, raw_count = [0] * N_RAW, []
    for q, (_, parts) in enumerate(units):
        loads[q % N_RAW] += 16 * len(parts)
        raw_count.append(loads[q % N_RAW])
    ffn_raw0 = list(loads)

    def kview(ap, k):
        return ap.rearrange("p (k n) -> p k n", k=k)

    def half_of(buf, slot, half, k):
        n = UNIT // k // 2
        return kview(buf[:, slot, :], k)[:, :, half * n:half * n + n]

    conv_tiles = ["act", "act", "dve", "dve", "dve", "dve"] * 2
    evac_by = conv_tiles + ["act"] * 8 + ["act"] * 16 + ["act", "act", "dve", "dve"] * 4 + ["dve"] * 8
    T_OA, T_GATE, T_GLU, T_WO = 12, 20, 36, 52

    def evac_count(tile):
        by = evac_by[tile]
        return S["evac_" + by], evac_by[:tile + 1].count(by)

    def bias_of(col):
        c = V_BIN + (col // P if col < C_U else col // P - KC)
        return vecT[:, c:c + 1]

    def half_used(n):
        return T_GLU + 2 * n + 2 if n < 8 else T_WO + n - 8 + 1

    def cut_of(n):
        q = n_native + n // 2
        return units[q][0] if q < n_pre else (KD, KD, 2)[q - n_pre]

    def unit_used(q):
        if q < U0_GC:
            return S["u_mm"], q + 1
        if q < U0_OA:
            return S["mm_done"], 2 * (q - U0_GC) + 2
        if q < U0_GATE:
            return S["mm_done"], T_OA + 4 * (q - U0_OA) + 4
        return S["mm_done"], T_GATE + 2 * (q - U0_GATE) + 2

    block = ctx.enter_context(nc.Block())

    @block.sync
    def _(sp):
        sp.dma_start(crow_in[:, :], t["c_rows"]).then_inc(rows_in_s, 16)
        sp.dma_start(rows_in[:, :], t["vec_rows"]).then_inc(rows_in_s, 16)
        sp.dma_start(sm[:, 0:3, :], t["lam_pack"]).then_inc(lam_s, 16)
        sp.dma_start(xtok[:, 0:2, :], t["x"].rearrange("(a p) d -> p a d", p=P)).then_inc(x_s, 16)
        sp.dma_start(xtok[:, 2:4, :], t["ctx"].rearrange("(a p) d -> p a d", p=P)).then_inc(ctx_s, 16)
        sp.dma_start(par_c[:, :, :, :], t["c_pack"]).then_inc(par_c_s, 16)

        def load_unit(q):
            slot, (k, parts) = q % N_RAW, units[q]
            old = q - N_RAW
            if old >= 0 and old < n_native:
                sp.wait_ge(*unit_used(old))
            elif old >= 0:
                sp.wait_ge(S["lo_done"], 2 * (old - n_native) + 2)
            for c0, n, src in parts:
                sp.dma_start(kview(raw[:, slot, :], k)[:, :, c0:c0 + n], src).then_inc(raw_full[slot], 16)

        for n in range(16):
            if n >= N_PIECE:
                sp.wait_ge(S["piece_used_pe"], n - N_PIECE + 1)
            sp.dma_start(piece[:, n % N_PIECE, :], t["w_mod"][(n // 2) * P:(n // 2 + 1) * P, (n % 2) * D:(n % 2 + 1) * D]
                         ).then_inc(piece_full[n % N_PIECE], 16)
            if n == 1:
                sp.dma_start(par_b[:, :, :, :], t["b_pack"]).then_inc(par_b_s, 16)
                sp.dma_start(bu[:, :], t["bu_pack"]).then_inc(pack_s, 16)
                sp.dma_start(d_skip[:, :], t["d_pack"]).then_inc(pack_s, 16)
            if n == 11:
                load_unit(0)
        for q in range(1, n_pre):
            load_unit(q)
            if q == U0_OA:
                sp.wait_ge(r_out_s, 16 * 4)
                for j in range(CH):
                    sp.dma_start(toep[H * j:H * j + H, :, :],
                                 r_dram[:, :, (CH - 1 - j) * H:(CH - 1 - j) * H + CH * H].rearrange("g h n -> h g n")
                                 ).then_inc(toep_s, 16)
            if q == U0_GLU + 2:
                sp.wait_ge(S["y_mm"], 1)
                sp.dma_start(xtok2[:, :, :], t["x"].rearrange("(a p) d -> p a d", p=P)).then_inc(xtok2_s, 16)
        with sp.Fori(0, n_turn) as turn:
            for j in range(3):
                slot = ffn_slot[j]
                sp.wait_ge(S["lo_done"], turn * 6 + (split0 - 6 + 2 * j + 2))
                if j < 2:
                    src = w_fi[:, bass.ds(turn * 256 + j * DFF, 256)].rearrange("(k p) n -> p k n", p=P)
                    sp.dma_start(kview(raw[:, slot, :], KD), src).then_inc(raw_full[slot], 16)
                else:
                    src = w_fo[bass.ds(turn * 256, 256), :].rearrange("(k p) n -> p k n", p=P)
                    sp.dma_start(kview(raw[:, slot, :], 2), src).then_inc(raw_full[slot], 16)
        for tt in range(2):
            sp.wait_ge(S["fin_act"], tt + 1)
            sp.wait_ge(S["fin_dve"], tt + 1)
            sp.dma_start(out[tt * P:(tt + 1) * P, :], fin[:, tt, :]).then_inc(out_s, 16)
        sp.wait_ge(out_s, 32)

    @block.gpsimd
    def _(pool):
        g = nc.gpsimd
        g.memset(ident[:, :], 0.0).then_inc(S["zeroed"], 1)
        pool.wait_ge(S["zeroed"], 1)
        g.affine_select(out=ident[:, :], in_=ident[:, :], compare_op=ALU.not_equal, fill=1.0, base=0,
                        pattern=[[-1, P]], channel_multiplier=1).then_inc(S["consts"], 1)
        for i, (buf, rows, value) in enumerate(((ones, slice(0, P), 1.0), (zeros, slice(0, P), 0.0), (halfpi, slice(0, P), PI / 2),
                                 (epsc, slice(0, P), EPS), (sgn, slice(0, NS), 1.0), (sgn, slice(NS, P), -1.0))):
            pool.wait_ge(S["consts"], i + 1)
            g.memset(buf[rows, :], value).then_inc(S["consts"], 1)

        def mod_piece(m):
            n, k, c = 16 + m, m // 4, m % 4
            if m < N_PIECE:
                pool.wait_ge(S["piece_used_pe"], n - N_PIECE + 1)
            else:
                pool.wait_ge(S["piece_used_dve"], m - N_PIECE + 1)
            pool.dma_start(piece[:, n % N_PIECE, :], t["w_mod"][k * P:(k + 1) * P, (2 + c) * D:(3 + c) * D]
                           ).then_inc(piece2_full[n % N_PIECE], 16)

        for m in range(32):
            mod_piece(m)
        for f in range(KD):
            pool.wait_ge(S["evac_act"], evac_count(T_GATE + f)[1])
            g.tensor_tensor(ya[:, f, :], ya[:, f, :], gv[:, f % 2, :], ALU.mult).then_inc(S["ya_scaled"], 1)
        pool.wait_ge(S["evac_act"], evac_count(T_GATE + 15)[1])
        pool.wait_ge(S["ya_scaled"], KD)
        pool.wait_ge(S["scan_done"], 1)
        for f in range(KD):
            pool.wait_ge(*evac_count(T_GLU + 4 * (f // 2) + 2 + f % 2))
            if f >= 2:
                pool.wait_ge(S["m_ready"], f - 1)
            g.tensor_tensor(mrg[:, f % 2, :], yb[:, f % 2, :], sgb[:, f, :], ALU.mult).then_inc(S["mul_done"], 1)
            pool.wait_ge(S["mul_done"], f + 1)
            g.tensor_tensor(mrg[:, f % 2, :], mrg[:, f % 2, :], ya[:, f, :], ALU.add).then_inc(S["mrg_ready"], 1)
        pool.wait_ge(S["mrg_ready"], KD)
        g.memset(zrow[:, :], 0.0).then_inc(S["zrow_ready"], 1)

    n_const = 7
    LR, LI, LD, DT, MAG, SN, CS, DEN, NR, FR, FI, T0, T1, T2, T3, T4, T5, T6 = range(18)
    AR = [LR, LI, LD, DT, MAG]
    QI = [SN, CS, DEN, NR, FR]

    @block.scalar
    def _(act):
        A, copy = nc.scalar.activation, nc.scalar.copy

        act.wait_ge(lam_s, 16)
        A(sm[:, DT, :], sm[:, LD, :], ACT.Exp).then_inc(S["dt_ready"], 1)
        act.wait_ge(S["lamdt_ready"], 1)
        A(sm[:, MAG, :], sm[:, T0, :], ACT.Exp).then_inc(S["mag_ready"], 1)
        act.wait_ge(S["consts"], n_const)
        act.wait_ge(S["trig_arg"], 1)
        A(sm[:, SN, :], sm[:, T1, :], ACT.Sin).then_inc(S["sin_done"], 1)
        A(sm[:, CS, :], sm[:, T2, :], ACT.Sin, bias=halfpi[:, 0:1], scale=-1.0).then_inc(S["sin_done"], 1)
        act.wait_ge(S["rows_T"], 2)
        A(csil[:, :], bank[7][:, P:P + 16], ACT.Silu).then_inc(S["csil_ready"], 1)
        copy(vecT[:, :], bank[7][:, 0:P]).then_inc(S["vec_ready"], 1)
        act.wait_ge(x_s, 16)
        for tt in range(4):
            if tt == 2:
                act.wait_ge(ctx_s, 16)
            if tt:
                act.wait_ge(S["sums_done"], tt)
            A(sq_junk[:, :], xtok[:, tt, :], ACT.Square, accum_out=ssum[:, tt:tt + 1]).then_inc(S["sums_done"], 1)
        act.wait_ge(S["sums_done"], 4)
        A(srow[:, :], ssum[:, :], ACT.Sqrt, bias=epsc[:, 0:1], scale=1.0 / D).then_inc(S["sqrt_done"], 1)
        for k in range(KD):
            act.wait_ge(S["xn_mm"], k + 1)
            copy(xnT[:, k, :], bank[k % 4][:, :]).then_inc(S["xn_evac"], 1)

        def h_rows(c):
            act.wait_ge(S["h_mm"], c + 1)
            if c % 2 == 0 and c:
                act.wait_ge(r_out_s, 16 * (c // 2))
            for b in range(2):
                src = bank[5 + b][0:H, :].rearrange("h (g n) -> h g n", g=4)
                dst = r_rows[:, 4 * b:4 * b + 4, :]
                if c % 2 == 0:
                    copy(dst[:, :, 128:256], src).then_inc(S["h_evac"], 1)
                else:
                    copy(dst[:, :, 16:128], src[:, :, 0:112])
                    copy(dst[:, :, 0:16], src[:, :, 112:128]).then_inc(S["h_evac"], 1)
            if c % 2:
                act.wait_ge(S["r_added"], c // 2 + 1)
                act.dma_start(r_dram[8 * (c // 2):8 * (c // 2) + 8, :, :].rearrange("g h n -> h g n"),
                              r_rows[:, :, 16:256]).then_inc(r_out_s, 16)

        for c in range(4):
            h_rows(c)
        act.wait_ge(S["gs_ready"], 1)
        for k in range(KD):
            for s in range(2):
                A(hT[:, k, :, s, :].rearrange("p j c -> p c j"), xnT[:, k, s * NT:(s + 1) * NT], ACT.Identity, bias=mod1[:, 2 * k + s:2 * k + s + 1],
                  scale=gs1[:, 2 * k + s:2 * k + s + 1]).then_inc(S["h_ready"], 1)
        for c in range(4, 8):
            h_rows(c)
        for half in range(2):
            act.wait_ge(S["u_mm"], half + 1)
            for m in range(4):
                for jj in range(2):
                    copy(v_rows[:, 16 * half:16 * half + 16, 2 * m + jj, :],
                         bank[2 * half + m // 2][NS * jj:NS * jj + NS, 256 * (m % 2):256 * (m % 2) + 256]
                         .rearrange("c (g h) -> c g h", h=H)).then_inc(S["u_rows"], 1)

        def b_T_evac(n):
            act.wait_ge(S["b_Tmm"], n + 1)
            if n >= 4:
                act.wait_ge(S["x_mm"], n - 3)
            copy(b_T[:, n % 4, :], bank[5 + n % 2][:, :]).then_inc(S["b_Tevac"], 1)

        def x_evac(n):
            act.wait_ge(S["x_mm"], n + 1)
            copy(X[:, 4 * n:4 * n + 4, :], bank[(4, 7)[n % 2]][:, 0:256].rearrange("p (g c) -> p g c", g=4)
                 ).then_inc(S["x_evac"], 1)

        def ssm_pair(i):
            if i < 8:
                b_T_evac(2 * i)
                b_T_evac(2 * i + 1)
            if i >= 1:
                x_evac(2 * i - 2)
                x_evac(2 * i - 1)

        def tile_bank(tile):
            act.wait_ge(S["mm_done"], tile + 1)
            return bank[tile % 4][:, 0:NT]

        for tile in range(T_OA):
            if 2 <= tile <= 10:
                ssm_pair(tile - 2)
            if evac_by[tile] == "act":
                q, f = tile // 6, tile % 6
                if q:
                    act.wait_ge(*evac_count(4 + f))
                A(gv[:, f, :], tile_bank(tile), ACT.Identity, bias=bias_of(C_GC + 256 * q + P * f)).then_inc(S["evac_act"], 1)
        act.wait_ge(S["b_ready"], 16)
        for f in range(KD):
            copy(ya[:, f, :], tile_bank(T_OA + f)).then_inc(S["evac_act"], 1)
        act.wait_ge(*evac_count(T_OA - 1))
        for f in range(KD):
            if f >= 2:
                act.wait_ge(S["ya_scaled"], f - 1)
            A(gv[:, f % 2, :], tile_bank(T_GATE + f), ACT.Sigmoid, bias=bias_of(C_GA + P * f)).then_inc(S["evac_act"], 1)
        for f in range(KD):
            A(sgb[:, f, :], tile_bank(T_GATE + KD + f), ACT.Sigmoid, bias=bias_of(C_GATEB + P * f)).then_inc(S["evac_act"], 1)

        act.wait_ge(S["back_done"], 1)
        copy(p_rev[:, :, :], p_st[:, NG:, ::-1]).then_inc(S["rev_ready"], 1)

        def hi(n):
            q, half = n_native + n // 2, n % 2
            if q < n_pre:
                slot, k, need = q % N_RAW, units[q][0], raw_count[q]
            else:
                j = q - n_pre
                slot, k, need = ffn_slot[j], (KD, KD, 2)[j], ffn_raw0[ffn_slot[j]] + 16
            act.wait_ge(raw_full[slot], need)
            if n >= 6:
                act.wait_ge(S["mm_done"], half_used(n - 6 if cut_of(n - 6) == cut_of(n) else (n - 6) | 1))
            ffn_half(slot, half, k)

        def ffn_half(slot, half, k):
            if k > 2:
                src, dst = half_of(raw, slot, half, k), half_of(w_hi, slot, half, k)
            else:
                src, dst = raw[:, slot, half * HALF:(half + 1) * HALF], w_hi[:, slot, half * HALF:(half + 1) * HALF]
            copy(dst, src).then_inc(S["hi_done"], 1)

        for b in range(2):
            act.wait_ge(S["y_mm"], 1)
            act.wait_ge(S["ya_scaled"], KD)
            copy(y_rows[:, :, 4 * b:4 * b + 4, :].rearrange("p i g h -> p g i h"), bank[5 + b][:, :].rearrange("p (g i h) -> p g i h", g=4, i=CH)
                 ).then_inc(S["y_evac"], 1)
        act.wait_ge(S["mod2_mm"], 1)
        hi(0)
        act.wait_ge(S["s_T"], 1)
        for b in range(2):
            src = bank[(4, 7)[b]][:, :].rearrange("p (i g c) -> p g c i", i=4, g=KC)
            dst = s32[:, :, :].rearrange("p g (c i) -> p g c i", i=CH)[:, :, :, 4 * b:4 * b + 4]
            A(dst, src, ACT.Gelu_apprx_tanh).then_inc(S["s_gelu"], 1)
        act.wait_ge(S["s_gelu"], 2)
        copy(s_hi[:, :, :], s32[:, :, :]).then_inc(S["s_hi_done"], 1)
        for n in range(1, 6):
            hi(n)

        def m_hi_of(f):
            act.wait_ge(S["mrg_ready"], f + 1)
            copy(m_hi[:, f, :], mrg[:, f % 2, :]).then_inc(S["m_hi_done"], 1)

        for q in range(4):
            for f in range(2):
                if q:
                    act.wait_ge(*evac_count(T_GLU + 4 * q - 2 + f))
                b = V_BGLU + KD + 2 * q + f
                A(sg[:, f, :], tile_bank(T_GLU + 4 * q + f), ACT.Sigmoid, bias=vecT[:, b:b + 1]).then_inc(S["evac_act"], 1)
            hi(6 + 2 * q)
            if q:
                m_hi_of(2 * q - 2)
                m_hi_of(2 * q - 1)
            act.wait_ge(S["xT_mm"], q + 1)
            copy(xT[:, 2 * q:2 * q + 2, :], kview(bank[6 - q % 2][:, :], 2)).then_inc(S["xT_evac"], 1)
            hi(7 + 2 * q)
        m_hi_of(6)
        m_hi_of(7)
        for f in range(KD):
            act.wait_ge(S["evac_dve"], evac_count(T_WO + f)[1])
            if f >= 2:
                act.wait_ge(S["ss_mm"], f - 1)
            A(sq[:, f % 2, :], x1T[:, f, :], ACT.Square).then_inc(S["sq_ready"], 1)
            A(x1g[:, f, :], x1T[:, f, :], ACT.Copy, scale=gs2[:, f:f + 1]).then_inc(S["x1g_ready"], 1)
            if f < 7:
                hi(14 + f)
        act.wait_ge(S["ss_mm"], KD)
        A(bc[:, 0, :], bank[4][:, 0:NT], ACT.Sqrt, bias=epsc[:, 0:1], scale=1.0 / D).then_inc(S["sqrt2_done"], 1)
        for k in range(KD):
            act.wait_ge(S["t2_ready"], k + 1)
            A(h2_hi[:, k, :], x1g[:, k, :], ACT.Identity, bias=mod2[:, KD + k:KD + k + 1]).then_inc(S["h2_hi_done"], 1)
        hi(21)

        def silu(f, turn):
            act.wait_ge(S["gate_mm"], turn * 2 + (f + 1))
            act.wait_ge(S["prod_done"], turn * 2 + (f - 1))
            A(silu_g[:, f, :], bank[f][:, 0:NT], ACT.Silu).then_inc(S["silu_done"], 1)

        for f in range(2):
            act.wait_ge(S["gate_mm"], f + 1)
            act.wait_ge(S["mrg_ready"], KD)
            A(silu_g[:, f, :], bank[f][:, 0:NT], ACT.Silu).then_inc(S["silu_done"], 1)
        with act.Fori(1, n_turn) as turn:
            for j in range(3):
                for half in range(2):
                    if half == 0:
                        act.wait_ge(raw_full[ffn_slot[j]], turn * 16 + (ffn_raw0[ffn_slot[j]] + 16))
                    act.wait_ge(S[("gate_mm", "up_mm", "fo_used")[j]], turn * 2 + (half - 1))
                    ffn_half(ffn_slot[j], half, (KD, KD, 2)[j])
                    if j == 1:
                        silu(half, turn)
        for f in range(KD):
            act.wait_ge(S["x2_ready"], f + 1)
            if f >= 2:
                act.wait_ge(S["ssf_mm"], f - 1)
            A(sq[:, f % 2, :], x1T[:, f, :], ACT.Square).then_inc(S["sqf_ready"], 1)
        act.wait_ge(S["ssf_mm"], KD)
        A(srow[:, 0:2], bank[4][:, 0:2], ACT.Sqrt, bias=epsc[:, 0:1], scale=1.0 / D).then_inc(S["sqrt3_done"], 1)
        act.wait_ge(S["rstd3_done"], 1)
        act.wait_ge(S["fin_T"], KD)
        for tt in range(2):
            A(fin[:, tt, DC:D], bank[2 * tt + 1][:, :], ACT.Copy, scale=rstd[:, tt:tt + 1]).then_inc(S["fin_act"], 1)

    @block.vector
    def _(dve):
        v = nc.vector
        steps = [0]

        def step():
            steps[0] += 1
            return steps[0]

        def tt(o, a, b, op):
            return v.tensor_tensor(o, a, b, op)

        def stt(o, a, s, b, op0, op1):
            return v.scalar_tensor_tensor(out=o, in0=a, scalar=s, in1=b, op0=op0, op1=op1)

        def q(i):
            return sm[:, i, :]

        M, AD, SU = ALU.mult, ALU.add, ALU.subtract
        dve.wait_ge(S["dt_ready"], 1)
        tt(q(T0), q(LR), q(DT), M).then_inc(S["lamdt_ready"], 1)
        tt(q(T1), q(LI), q(DT), M).then_inc(S["dve_step"], 1)
        dve.wait_ge(S["dve_step"], step())
        v.tensor_scalar(q(T2), q(T1), 1.0 / (2 * PI), ROUND, M, AD).then_inc(S["dve_step"], 1)
        dve.wait_ge(S["dve_step"], step())
        v.tensor_scalar(q(T2), q(T2), ROUND, None, SU).then_inc(S["dve_step"], 1)
        dve.wait_ge(S["dve_step"], step())
        for part in (TWO_PI_HI, TWO_PI_MID, TWO_PI_LO):
            stt(q(T1), q(T2), -part, q(T1), M, AD).then_inc(S["dve_step"], 1)
            dve.wait_ge(S["dve_step"], step())
        v.tensor_scalar(q(T1), q(T1), PI_BELOW, -PI_BELOW, ALU.min, ALU.max).then_inc(S["dve_step"], 1)
        dve.wait_ge(S["dve_step"], step())
        stt(q(T2), q(T1), -1.0, q(T1), M, ALU.max).then_inc(S["trig_arg"], 1)
        tt(q(T3), q(LR), q(LR), M).then_inc(S["dve_step"], 1)
        dve.wait_ge(S["dve_step"], step())
        tt(q(T4), q(LI), q(LI), M).then_inc(S["dve_step"], 1)
        dve.wait_ge(S["dve_step"], step())
        tt(q(DEN), q(T3), q(T4), AD).then_inc(S["dve_step"], 1)
        dve.wait_ge(S["dve_step"], step())
        v.reciprocal(q(DEN), q(DEN)).then_inc(S["dve_step"], 1)
        dve.wait_ge(S["dve_step"], step())
        dve.wait_ge(S["mag_ready"], 1)
        dve.wait_ge(S["sin_done"], 2)
        dve.wait_ge(S["consts"], n_const)
        v.memset(e_re[:, 0, :], 1.0)
        v.memset(e_im[:, 0, :], 0.0)
        tt(e_re[:, 1, :], q(MAG), q(CS), M)
        tt(e_im[:, 1, :], q(MAG), q(SN), M).then_inc(S["dve_step"], 1)
        dve.wait_ge(S["dve_step"], step())
        v.tensor_scalar(q(NR), e_re[:, 1, :], -1.0, None, AD).then_inc(S["dve_step"], 1)
        dve.wait_ge(S["dve_step"], step())
        tt(q(T0), q(NR), q(LR), M)
        tt(q(T1), e_im[:, 1, :], q(LI), M)
        tt(q(T2), e_im[:, 1, :], q(LR), M)
        tt(q(T3), q(NR), q(LI), M).then_inc(S["dve_step"], 1)
        dve.wait_ge(S["dve_step"], step())
        tt(q(T0), q(T0), q(T1), AD)
        tt(q(T2), q(T2), q(T3), SU).then_inc(S["dve_step"], 1)
        dve.wait_ge(S["dve_step"], step())
        tt(q(FR), q(T0), q(DEN), M)
        tt(q(FI), q(T2), q(DEN), M).then_inc(S["dve_step"], 1)
        dve.wait_ge(S["dve_step"], step())

        def power(dst, n, by, src):
            def b(i):
                return e[i][:, by:by + 1, :].broadcast_to([P, n, DG])
            e = (e_re, e_im)
            s_re, s_im = e_re[:, src:src + n, :], e_im[:, src:src + n, :]
            t_a, t_b = (x[:, 0:n * DG].rearrange("p (n d) -> p n d", n=n) for x in (tA, tB))
            t_a2, t_b2 = (x[:, 256:256 + n * DG].rearrange("p (n d) -> p n d", n=n) for x in (tA, tB))
            tt(t_a, s_re, b(0), M)
            tt(t_b, s_im, b(1), M)
            tt(t_a2, s_re, b(1), M)
            tt(t_b2, s_im, b(0), M).then_inc(S["dve_step"], 1)
            dve.wait_ge(S["dve_step"], step())
            tt(e_re[:, dst:dst + n, :], t_a, t_b, SU)
            tt(e_im[:, dst:dst + n, :], t_a2, t_b2, AD).then_inc(S["dve_step"], 1)
            dve.wait_ge(S["dve_step"], step())

        power(2, 1, 1, 1)
        power(3, 2, 2, 1)
        power(5, 4, 4, 1)
        for d in range(2):
            dg = slice(NG * d, NG * d + NG)
            o = [tc[:, i, dg, :].rearrange("p g e -> p e g") for i in range(2)]
            src = [(x[:, 0:8, dg] if d == 0 else x[:, 7::-1, dg]) for x in (e_re, e_im)]
            f_re, f_im = (sm[:, i:i + 1, dg].broadcast_to([P, CH, NG]) for i in (FR, FI))
            t_a, t_b, = (x[:, 0:CH * NG].rearrange("p (n d) -> p n d", n=CH) for x in (tA, tB))
            t_a2, t_b2 = (x[:, 256:256 + CH * NG].rearrange("p (n d) -> p n d", n=CH) for x in (tA, tB))
            tt(t_a, src[0], f_re, M)
            tt(t_b, src[1], f_im, M)
            tt(t_a2, src[0], f_im, M)
            tt(t_b2, src[1], f_re, M).then_inc(S["dve_step"], 1)
            dve.wait_ge(S["dve_step"], step())
            tt(t_a, t_a, t_b, SU).then_inc(S["dve_step"], 1)
            dve.wait_ge(S["dve_step"], step())
            tt(t_a2, t_a2, t_b2, AD).then_inc(S["dve_step"], 1)
            dve.wait_ge(S["dve_step"], step())
            v.tensor_scalar(o[0], t_a, sgn[:, 0:1], None, M)
            v.tensor_scalar(o[1], t_a2, -1.0, None, M).then_inc(S["dve_step"], 1)
            dve.wait_ge(S["dve_step"], step())
        v.tensor_scalar(e_im[:, 1:9, :], e_im[:, 1:9, :], sgn[:, 0:1], -1.0, M, M).then_inc(S["dve_step"], 1)
        dve.wait_ge(S["dve_step"], step())

        def table(dst, par, dg, f0, f1, n_e):
            shape = [P, 4, n_e, H]
            t_a, t_b = (x[:, :].rearrange("p (g e h) -> p g e h", g=4, e=n_e) for x in (tA, tB))
            tt(t_a, par[:, 0, dg, None, :].broadcast_to(shape), f0[:, :, :, None].broadcast_to(shape), M)
            tt(t_b, par[:, 1, dg, None, :].broadcast_to(shape), f1[:, :, :, None].broadcast_to(shape), M).then_inc(S["dve_step"], 1)
            dve.wait_ge(S["dve_step"], step())
            return tt(dst, tA[:, :], tB[:, :], AD)

        dve.wait_ge(par_c_s, 16)
        dve.wait_ge(S["rows_T"], 2)

        def c_chunk(c):
            for hh in range(2):
                g0 = NG * (c % 2) + 8 * (c // 2) + 4 * hh
                dg = slice(g0, g0 + 4)
                table(c_pow[:, dg, :], par_c, dg, tc[:, 0, dg, :], tc[:, 1, dg, :], CH).then_inc(S["cpow_ready"], 1)
                dve.wait_ge(S["cpow_ready"], 2 * c + hh + 1)

        def r_add(i):
            dve.wait_ge(pack_s, 32)
            if i:
                dve.wait_ge(S["r_added"], i)
            tt(d_diag[:, :, :], ident[0:H, None, 0:H].broadcast_to([H, 8, H]),
               d_skip[:, 8 * i:8 * i + 8, None].broadcast_to([H, 8, H]), M).then_inc(S["dve_step"], 1)
            dve.wait_ge(S["dve_step"], step())
            dve.wait_ge(S["h_evac"], 4 * i + 4)
            tt(r_rows[:, :, 128:144], r_rows[:, :, 128:144], r_rows[:, :, 0:16], AD).then_inc(S["dve_step"], 1)
            dve.wait_ge(S["dve_step"], step())
            tt(r_rows[:, :, 128:144], r_rows[:, :, 128:144], d_diag[:, :, :], AD).then_inc(S["r_added"], 1)

        def b_chunk(n):
            dve.wait_ge(par_b_s, 16)
            if n < 2:
                dve.wait_ge(S["h_ready"], 2 * KD)
            if n >= 2:
                dve.wait_ge(S["b_Tmm"], n - 1)
            d = n // 8
            dg = slice(4 * n, 4 * n + 4)
            f = [(x[:, 8:0:-1, dg] if d == 0 else x[:, 1:9, dg]).rearrange("p e g -> p g e") for x in (e_re, e_im)]
            table(b_half[:, n % 2, :], par_b, dg, f[0], f[1], CH).then_inc(S["b_ready"], 1)
            dve.wait_ge(S["b_ready"], n + 1)

        def mod_acc_piece(m):
            n, k, c = 16 + m, m // 4, m % 4
            dve.wait_ge(piece2_full[n % N_PIECE], 16 * (m // N_PIECE + 1))
            a = mod_acc[:, c * D:(c + 1) * D]
            if k == 0:
                v.tensor_scalar(a, piece[:, n % N_PIECE, :], csil[:, 0:1], None, M).then_inc(S["piece_used_dve"], 1)
            else:
                dve.wait_ge(S["piece_used_dve"], m - 3)
                stt(a, piece[:, n % N_PIECE, :], csil[:, k:k + 1], a, M, AD).then_inc(S["piece_used_dve"], 1)

        dve.wait_ge(S["sqrt_done"], 1)
        v.reciprocal(rstd[:, :], srow[:, :]).then_inc(S["dve_step"], 1)
        dve.wait_ge(S["dve_step"], step())
        for i in range(4):
            v.tensor_scalar(diag[:, i, :], ident[:, :], rstd[:, i:i + 1], None, M).then_inc(S["diag_ready"], 1)
        for c in range(7):
            c_chunk(c)
            if c == 5:
                r_add(0)
        dve.wait_ge(S["piece_used_pe"], 16)
        dve.wait_ge(S["vec_ready"], 1)
        tt(mod1[:, :].rearrange("p (f s) -> p f s", s=2), bank[4][:, 0:32].rearrange("p (f s) -> p f s", s=2),
           vecT[:, V_BMOD:V_BMOD + 16, None].broadcast_to([P, 16, 2]), AD).then_inc(S["dve_step"], 1)
        dve.wait_ge(S["dve_step"], step())
        stt(gs1[:, :].rearrange("p (f s) -> p f s", s=2), mod1[:, 16:32].rearrange("p (f s) -> p f s", s=2), 1.0,
            vecT[:, V_N1:V_N1 + KD, None].broadcast_to([P, KD, 2]), AD, M).then_inc(S["gs_ready"], 1)
        dve.wait_ge(S["xn_evac"], KD)
        for m in range(4):
            mod_acc_piece(m)
        c_chunk(7)
        r_add(1)
        b_chunk(0)
        b_chunk(1)
        for m in range(4, 12):
            mod_acc_piece(m)
        r_add(2)
        for m in range(12, 16):
            mod_acc_piece(m)
        r_add(3)
        for r in range(4):
            dve.wait_ge(S["u_T"], r + 1)
            shape = [P, 8, 2 * NC]
            tt(u_pack[:, 8 * r:8 * r + 8, :], bank[(4, 7)[r % 2]][:, :].rearrange("p (g c) -> p g c", g=8),
               bu[:, 8 * r:8 * r + 8, None].broadcast_to(shape), AD).then_inc(S["u_packed"], 1)

        def tile_bank(tile):
            dve.wait_ge(S["mm_done"], tile + 1)
            return bank[tile % 4][:, 0:NT]

        def conv_tile(tile):
            qq, i = tile // 6, tile % 6
            f = i % 2
            if i < 4:
                dve.wait_ge(S["evac_act"], evac_count(6 * qq + f)[1])
                c0 = V_CONV + 2 * qq + f
                tap = [vecT[:, c0 + KC * j:c0 + KC * j + 1] for j in range(3)]
                stt(gv[:, f, :], tile_bank(tile), bias_of(C_XIN + 256 * qq + P * f), gv[:, f, :], AD, M
                    ).then_inc(S["evac_dve"], 1)
                dve.wait_ge(*evac_count(tile))
                v.tensor_scalar(cv[:, f, :], gv[:, f, :], tap[1], None, M).then_inc(S["dve_step"], 1)
                dve.wait_ge(S["dve_step"], step())
                rows = [x[:, f, :].rearrange("p (r c) -> p r c", c=GRID_W) for x in (gv, cv)]
                stt(rows[1][:, :, 1:], rows[0][:, :, :-1], tap[0], rows[1][:, :, 1:], M, AD).then_inc(S["dve_step"], 1)
                dve.wait_ge(S["dve_step"], step())
                stt(rows[1][:, :, :-1], rows[0][:, :, 1:], tap[2], rows[1][:, :, :-1], M, AD).then_inc(S["dve_step"], 1)
                dve.wait_ge(S["dve_step"], step())
            else:
                stt(gbv[:, 2 * qq + f, :], tile_bank(tile), bias_of(C_GB + 256 * qq + P * f), cv[:, f, :], AD, M
                    ).then_inc(S["evac_dve"], 1)

        for tile in range(2, T_OA):
            i = tile - 2
            if i < 7:
                b_chunk(2 * i + 2)
                b_chunk(2 * i + 3)
            if evac_by[tile] == "dve":
                conv_tile(tile)

        v.tensor_copy(q(AR[0]), e_re[:, 8, :]).then_inc(S["dve_step"], 1)
        dve.wait_ge(S["dve_step"], step())
        v.tensor_scalar(q(T0), e_im[:, 8, :], sgn[:, 0:1], -1.0, M, M).then_inc(S["dve_step"], 1)
        dve.wait_ge(S["dve_step"], step())
        for k in range(5):
            v.tensor_scalar(q(QI[k]), q(T0), sgn[:, 0:1], None, M).then_inc(S["dve_step"], 1)
            dve.wait_ge(S["dve_step"], step())
            if k < 4:
                tt(q(T1), q(AR[k]), q(AR[k]), M)
                tt(q(T2), q(T0), q(T0), M)
                tt(q(T3), q(AR[k]), q(T0), M).then_inc(S["dve_step"], 1)
                dve.wait_ge(S["dve_step"], step())
                tt(q(AR[k + 1]), q(T1), q(T2), SU)
                tt(q(T0), q(T3), q(T3), AD).then_inc(S["dve_step"], 1)
                dve.wait_ge(S["dve_step"], step())

        def advance(src, add, dst, k, g0, n_g, n):
            shape = [P, n_g, n]
            gs = slice(g0, g0 + n_g)
            t_a, t_b = (x[:, 0:n_g * n].rearrange("p (g n) -> p g n", g=n_g) for x in (tA, tB))
            tt(t_a, src, sm[:, AR[k], gs, None].broadcast_to(shape), M)
            lo, up = slice(0, NS), slice(NS, P)
            tt(t_b[lo], src[up], sm[up, QI[k], gs, None].broadcast_to([NS, n_g, n]), M)
            tt(t_b[up], src[lo], sm[lo, QI[k], gs, None].broadcast_to([NS, n_g, n]), M).then_inc(S["dve_step"], 1)
            dve.wait_ge(S["dve_step"], step())
            tt(t_a, t_a, t_b, AD).then_inc(S["dve_step"], 1)
            dve.wait_ge(S["dve_step"], step())
            return tt(dst, t_a, add, AD)

        dve.wait_ge(S["x_evac"], 16)
        m_next = 16
        for k in range(4):
            s = 1 << k
            n = NC // s
            n_g = min(DG, 512 // n)
            Xv = X[:, :, :].rearrange("p g (n s) -> p g n s", s=2 * s)
            for g0 in range(0, DG, n_g):
                right = Xv[:, g0:g0 + n_g, :, 2 * s - 1]
                advance(Xv[:, g0:g0 + n_g, :, s - 1], right, right, k, g0, n_g, n).then_inc(S["dve_step"], 1)
                dve.wait_ge(S["dve_step"], step())
                if m_next < 24:
                    mod_acc_piece(m_next)
                    m_next += 1
        last = X[:, :, 2 * NC - 1:2 * NC]
        dve.wait_ge(S["r_added"], 4)
        dve.wait_ge(r_out_s, 64)
        advance(X[:, :, NC + NC // 2 - 1:NC + NC // 2], last, p_st[:, :, 0:1], 4, 0, DG, 1).then_inc(S["dve_step"], 1)
        dve.wait_ge(S["dve_step"], step())
        for k in range(4, -1, -1):
            s = 1 << k
            n = NC // (2 * s)
            n_g = min(DG, 512 // n)
            Xv = X[:, :, 0:NC].rearrange("p g (n s) -> p g n s", s=2 * s)
            Pv = p_st[:, :, :].rearrange("p g (n s) -> p g n s", s=2 * s)
            for g0 in range(DG - n_g, -1, -n_g):
                gs = slice(g0, g0 + n_g)
                done = advance(Pv[:, gs, :, 0], Xv[:, gs, :, s - 1], Pv[:, gs, :, s], k, g0, n_g, n)
                if k == 0:
                    done.then_inc(S["back_done" if g0 else "scan_done"], 1)
                    if g0:
                        dve.wait_ge(S["back_done"], 1)
                else:
                    done.then_inc(S["dve_step"], 1)
                    dve.wait_ge(S["dve_step"], step())
        while m_next < 32:
            mod_acc_piece(m_next)
            m_next += 1

        def lo(n):
            qq, half = n_native + n // 2, n % 2
            dve.wait_ge(S["hi_done"], n + 1)
            if qq < n_pre:
                split_lo(qq % N_RAW, half, units[qq][0])
            else:
                split_lo(ffn_slot[qq - n_pre], half, (KD, KD, 2)[qq - n_pre])

        def split_lo(slot, half, k):
            if k > 2:
                a, h_, o = (half_of(x, slot, half, k) for x in (raw, w_hi, w_lo))
            else:
                a, h_, o = (x[:, slot, half * HALF:(half + 1) * HALF] for x in (raw, w_hi, w_lo))
            tt(o, a, h_.bitcast(F32), SU).then_inc(S["lo_done"], 1)

        dve.wait_ge(S["mod2_mm"], 1)
        tt(mod2[:, :], bank[5][:, 0:32], vecT[:, V_BMOD + 16:V_BMOD + 48], AD).then_inc(S["mod2_ready"], 1)
        dve.wait_ge(S["mod2_ready"], 1)
        stt(gs2[:, :], mod2[:, 2 * KD:3 * KD], 1.0, vecT[:, V_N2:V_N2 + KD], AD, M).then_inc(S["dve_step"], 1)
        dve.wait_ge(S["dve_step"], step())
        lo(0)
        dve.wait_ge(S["s_hi_done"], 1)
        tt(s_lo[:, :, :], s32[:, :, :], s_hi[:, :, :].bitcast(F32), SU).then_inc(S["s_ready"], 1)
        for n in range(1, 6):
            lo(n)

        def m_lo_of(f):
            dve.wait_ge(S["m_hi_done"], f + 1)
            tt(m_lo[:, f, :], mrg[:, f % 2, :], m_hi[:, f, :].bitcast(F32), SU).then_inc(S["m_ready"], 1)

        for qq in range(4):
            lo(6 + 2 * qq)
            for f in range(2):
                tile = T_GLU + 4 * qq + 2 + f
                dve.wait_ge(S["evac_act"], evac_count(tile - 2)[1])
                if qq:
                    dve.wait_ge(S["mul_done"], 2 * qq + f - 1)
                b = V_BGLU + 2 * qq + f
                if qq:
                    m_lo_of(2 * qq - 2 + f)
                stt(yb[:, f, :], tile_bank(tile), vecT[:, b:b + 1], sg[:, f, :], AD, M).then_inc(S["evac_dve"], 1)
            lo(7 + 2 * qq)
        m_lo_of(6)
        m_lo_of(7)
        dve.wait_ge(S["xT_evac"], 4)
        for f in range(KD):
            stt(x1T[:, f, :], tile_bank(T_WO + f), mod2[:, f:f + 1], xT[:, f, :], M, AD).then_inc(S["evac_dve"], 1)
            if f < 7:
                lo(14 + f)
        dve.wait_ge(S["sqrt2_done"], 1)
        v.reciprocal(bc[:, 1, :], bc[:, 0, :]).then_inc(S["dve_step"], 1)
        dve.wait_ge(S["dve_step"], step())

        def norm2(k):
            dve.wait_ge(S["x1g_ready"], k + 1)
            tt(x1g[:, k, :], x1g[:, k, :], bc[:, 1, :], M).then_inc(S["t2_ready"], 1)

        def h2_lo_of(k):
            dve.wait_ge(S["h2_hi_done"], k + 1)
            stt(h2_lo[:, k, :], x1g[:, k, :], mod2[:, KD + k:KD + k + 1], h2_hi[:, k, :].bitcast(F32), AD, SU
                ).then_inc(S["h2_ready"], 1)

        norm2(0)
        norm2(1)
        for k in range(KD):
            h2_lo_of(k)
            if k + 2 < KD:
                norm2(k + 2)
        lo(21)

        def act_tiles(turn, used):
            for f in range(2):
                dve.wait_ge(S["silu_done"], turn * 2 + (f + 1))
                dve.wait_ge(S["up_mm"], turn * 2 + (f + 1))
                tt(gu[:, f, :], bank[2 + f][:, 0:NT], silu_g[:, f, :], M).then_inc(S["prod_done"], 1)
            for f in range(2):
                if used is not None:
                    dve.wait_ge(S["fo_used"], used + (f + 1))
                dve.wait_ge(S["prod_done"], turn * 2 + (f + 1))
                v.tensor_copy(a_hi[:, f, :], gu[:, f, :]).then_inc(S["a_hi_done"], 1)
                dve.wait_ge(S["a_hi_done"], turn * 2 + (f + 1))
                tt(a_lo[:, f, :], gu[:, f, :], a_hi[:, f, :].bitcast(F32), SU).then_inc(S["act_ready"], 1)

        act_tiles(0, None)
        with dve.Fori(1, n_turn) as turn:
            for j in range(3):
                for half in range(2):
                    dve.wait_ge(S["hi_done"], turn * 6 + (split0 + 2 * j + half + 1))
                    split_lo(ffn_slot[j], half, (KD, KD, 2)[j])
            act_tiles(turn, turn * 2 - 2)
        for f in range(KD):
            dve.wait_ge(S["x2_mm"], 2 * (f // 2) + 2)
            stt(x1T[:, f, :], bank[4 + f // 2][:, (f % 2) * NT:(f % 2 + 1) * NT], mod2[:, 3 * KD + f:3 * KD + f + 1],
                x1T[:, f, :], M, AD).then_inc(S["x2_ready"], 1)
            dve.wait_ge(S["x2_ready"], f + 1)
            v.tensor_scalar(x1g[:, f, :], x1T[:, f, :], vecT[:, V_FG + f:V_FG + f + 1], None, M).then_inc(S["xg_ready"], 1)
        dve.wait_ge(S["sqrt3_done"], 1)
        v.reciprocal(rstd[:, 0:2], srow[:, 0:2]).then_inc(S["rstd3_done"], 1)
        dve.wait_ge(S["rstd3_done"], 1)
        dve.wait_ge(S["fin_T"], KD)
        for i in range(2):
            v.tensor_scalar(fin[:, i, 0:DC], bank[2 * i][:, :], rstd[:, i:i + 1], None, M).then_inc(S["fin_dve"], 1)

    @block.tensor
    def _(pe):
        mm = nc.tensor.matmul

        pe.wait_ge(S["consts"], n_const)
        pe.wait_ge(rows_in_s, 32)
        nc.tensor.transpose(bank[7][:, P:P + 16], crow_in[:, :], ident[0:16, 0:16]).then_inc(S["rows_T"], 1)
        nc.tensor.transpose(bank[7][:, 0:P], rows_in[:, :], ident[:, :]).then_inc(S["rows_T"], 1)
        mm(bank[4][:, 0:32], ident[:, :], zeros[:, :], start=True, stop=False, skip_group_check=True)

        def mod_cols(n):
            pe.wait_ge(piece_full[n % N_PIECE], 16 * (n // N_PIECE + 1))
            k, f0 = n // 2, KD * (n % 2)
            for f in range(KD):
                last = mm(bank[4][:, 2 * (f0 + f):2 * (f0 + f) + 2], piece[:, n % N_PIECE, f * P:(f + 1) * P],
                          csil[:, k:16:KD], start=False, stop=k == KD - 1, skip_group_check=True)
            last.then_inc(S["piece_used_pe"], 1)
            return last

        def h_cols(c):
            pe.wait_ge(S["cpow_ready"], 2 * c + 2)
            pe.wait_ge(par_b_s, 16)
            if c:
                pe.wait_ge(S["h_evac"], 2 * c)
            for g in range(8):
                dg = NG * (c % 2) + 8 * (c // 2) + g
                last = mm(bank[5 + g // 4][0:H, (g % 4) * P:(g % 4 + 1) * P], par_b[:, 0, dg, :], c_pow[:, dg, :],
                          start=True, stop=True)
            last.then_inc(S["h_mm"], 1)

        pe.wait_ge(S["csil_ready"], 1)
        mod_cols(0)
        mod_cols(1)
        pe.wait_ge(S["diag_ready"], 4)
        for k in range(KD):
            if k >= 4:
                pe.wait_ge(S["xn_evac"], k - 3)
            for tt in range(4):
                last = mm(bank[k % 4][:, tt * P:(tt + 1) * P], xtok[:, tt, k * P:(k + 1) * P], diag[:, tt, :],
                          start=True, stop=True)
            last.then_inc(S["xn_mm"], 1)
            if k % 2:
                mod_cols(2 + k // 2)
        for n in range(6, 16):
            mod_cols(n)
            if n in (8, 10, 12, 14):
                h_cols((n - 8) // 2)

        def raw_ready(q):
            pe.wait_ge(raw_full[q % N_RAW], raw_count[q])

        pe.wait_ge(S["xn_evac"], KD)
        for half in range(2):
            raw_ready(half)
            wu = kview(raw[:, half, :], KD)
            for k in range(KD):
                pe.wait_ge(S["h_ready"], 2 * k + 2)
                for m in range(4):
                    last = mm(bank[2 * half + m // 2][:, 256 * (m % 2):256 * (m % 2) + 256], hT[:, k, 2 * m:2 * m + 2, :, :].rearrange("p j s c -> p (j s c)"),
                              wu[:, k, :], start=k == 0 and m % 2 == 0, stop=k == KD - 1, skip_group_check=True)
            last.then_inc(S["u_mm"], 1)
            h_cols(4 + 2 * half)
            h_cols(5 + 2 * half)

        tile = [0]

        def open_tile():
            n = tile[0]
            tile[0] += 1
            if n < 4:
                pe.wait_ge(S["u_rows"], 8 if n < 2 else 16)
            else:
                pe.wait_ge(*evac_count(n - 4))
            return bank[n % 4][:, 0:NT]

        def native(q, f, k_n, rhs):
            raw_ready(q)
            wv, o = kview(raw[:, q % N_RAW, :], k_n), open_tile()
            for k in range(k_n):
                last = mm(o, wv[:, k, f * P:(f + 1) * P], rhs[:, k], start=k == 0, stop=k == k_n - 1)
            last.then_inc(S["mm_done"], 1)

        def ssm_pair(i):
            if i < 8:
                for n in (2 * i, 2 * i + 1):
                    pe.wait_ge(S["b_ready"], n + 1)
                    if n >= 2:
                        pe.wait_ge(S["b_Tevac"], n - 1)
                    for g in range(4):
                        last = nc.tensor.transpose(bank[5 + n % 2][:, g * P:(g + 1) * P], b_half[:, n % 2, g * P:(g + 1) * P],
                                                   ident[:, :])
                    last.then_inc(S["b_Tmm"], 1)
            if i >= 1:
                for n in (2 * i - 2, 2 * i - 1):
                    pe.wait_ge(S["b_Tevac"], n + 1)
                    if n >= 2:
                        pe.wait_ge(S["x_evac"], n - 1)
                    for g in range(4):
                        dg = 4 * n + g
                        cols = u_pack[:, dg % NG, :].rearrange("p (s c) -> p s c", s=2)
                        if dg >= NG:
                            cols = cols[:, :, ::-1]
                        last = mm(bank[(4, 7)[n % 2]][:, g * 64:(g + 1) * 64], b_T[:, n % 4, g * P:(g + 1) * P], cols,
                                  start=True, stop=True)
                    last.then_inc(S["x_mm"], 1)

        pe.wait_ge(S["h_evac"], 16)
        h_lat = hT[:, :, :, 0, :].rearrange("p k j c -> p k c j")
        for n in range(T_OA):
            native(U0_GC + n // 2, n % 2, KD, h_lat)
            if n == 1:
                pe.wait_ge(S["u_rows"], 16)
                for r in range(4):
                    if r >= 2:
                        pe.wait_ge(S["u_packed"], r - 1)
                    for g in range(8):
                        last = nc.tensor.transpose(bank[(4, 7)[r % 2]][:, g * 64:(g + 1) * 64],
                                                   v_rows[:, 8 * r + g, :, :].rearrange("c j h -> c (j h)"),
                                                   ident[0:64, 0:64])
                    last.then_inc(S["u_T"], 1)
                pe.wait_ge(S["u_packed"], 4)
            if 1 <= n <= 9:
                ssm_pair(n - 1)
        pe.wait_ge(*evac_count(T_OA - 1))
        for n in range(KD):
            native(U0_OA + n // 4, n % 4, KC, gbv)
        for n in range(2 * KD):
            native(U0_GATE + n // 2, n % 2, KD, h_lat)
        pe.wait_ge(S["scan_done"], 1)
        pe.wait_ge(S["rev_ready"], 1)
        pe.wait_ge(toep_s, 16 * CH)
        for g in range(NG):
            gq, gr = g // 8, g % 8
            o = bank[5 + gr // 4][NC * gq:NC * gq + NC, (gr % 4) * P:(gr % 4 + 1) * P]
            mm(o, u_pack[:, g, 0:NC], toep[:, g, :], start=True, stop=False)
            mm(o, p_st[:, g, :], c_pow[:, g, :], start=False, stop=False)
            last = mm(o, p_rev[:, g, :], c_pow[:, NG + g, :], start=False, stop=True)
        last.then_inc(S["y_mm"], 1)
        pe.wait_ge(S["y_evac"], 2)
        for i in range(CH):
            last = nc.tensor.transpose(bank[(4, 7)[i // 4]][:, (i % 4) * P:(i % 4 + 1) * P], y_rows[:, i, :, :].rearrange("p g h -> p (g h)"), ident[:, :])
        last.then_inc(S["s_T"], 1)

        pe.wait_ge(S["piece_used_dve"], 32)
        for c in range(32):
            last = mm(bank[5][:, c:c + 1], mod_acc[:, c * P:(c + 1) * P], ones[:, 0:1], start=True, stop=True)
        last.then_inc(S["mod2_mm"], 1)

        def three(o, wh, wl, xh, xl, first, final):
            mm(o, wh, xh, start=first, stop=False, skip_group_check=True)
            mm(o, wh, xl, start=False, stop=False, skip_group_check=True)
            return mm(o, wl, xh, start=False, stop=final, skip_group_check=True)

        def split_tile(slot, half, f, k_n, x_hi, x_lo):
            o = open_tile()
            wh, wl = (half_of(x, slot, half, k_n)[:, :, f * P:(f + 1) * P] for x in (w_hi, w_lo))
            for k in range(k_n):
                last = three(o, wh[:, k, :], wl[:, k, :], x_hi[:, k, :], x_lo[:, k, :], k == 0, k == k_n - 1)
            last.then_inc(S["mm_done"], 1)

        pe.wait_ge(S["s_ready"], 1)
        for q in range(4):
            for half in range(2):
                pe.wait_ge(S["lo_done"], 2 * q + half + 1)
                for f in range(2):
                    split_tile((n_native + q) % N_RAW, half, f, KC, s_hi, s_lo)
            if q == 0:
                pe.wait_ge(xtok2_s, 16)
            if q == 1:
                pe.wait_ge(S["mod2_ready"], 1)
            if q >= 2:
                pe.wait_ge(S["xT_evac"], q - 1)
            for k in range(2):
                for tt in range(2):
                    last = nc.tensor.transpose(bank[6 - q % 2][:, k * NT + tt * P:k * NT + (tt + 1) * P],
                                               xtok2[:, tt, (2 * q + k) * P:(2 * q + k + 1) * P], ident[:, :])
            last.then_inc(S["xT_mm"], 1)
        pe.wait_ge(S["m_ready"], KD)

        def sum_squares(f):
            pe.wait_ge(S["sq_ready"], f + 1)
            mm(bank[4][:, 0:NT], ones[:, :], sq[:, f % 2, :], start=f == 0, stop=f == KD - 1).then_inc(S["ss_mm"], 1)

        for f in range(KD):
            pe.wait_ge(S["lo_done"], 8 + f + 1)
            split_tile((n_native + 4 + f // 2) % N_RAW, f % 2, 0, KD, m_hi, m_lo)
            if f >= 2:
                sum_squares(f - 2)
        sum_squares(KD - 2)
        sum_squares(KD - 1)
        pe.wait_ge(S["sqrt2_done"], 1)
        pe.wait_ge(S["xT_evac"], 4)
        pe.wait_ge(S["zrow_ready"], 1)
        for b in range(4, 8):
            mm(bank[b][:, :], zrow[:, 0:P], zrow[:, P:], start=True, stop=False, skip_group_check=True)

        def ffn_up(k_ready, done):
            for j in range(2):
                for f in range(2):
                    done(j, f)
                    wh, wl = (half_of(x, ffn_slot[j], f, KD) for x in (w_hi, w_lo))
                    for k in range(KD):
                        if k_ready and j == f == 0:
                            pe.wait_ge(S["h2_ready"], k + 1)
                        last = three(bank[2 * j + f][:, 0:NT], wh[:, k, :], wl[:, k, :], h2_hi[:, k, :], h2_lo[:, k, :],
                                     k == 0, k == KD - 1)
                    last.then_inc(S[("gate_mm", "up_mm")[j]], 1)

        def out_parts(f, e):
            return (x[:, ffn_slot[2], f * HALF + e * P:f * HALF + (e + 1) * P] for x in (w_hi, w_lo))

        def acc(e):
            return bank[4 + e // 2][:, (e % 2) * NT:(e % 2 + 1) * NT]

        def first_waits(j, f):
            pe.wait_ge(S["lo_done"], split0 + 2 * j + f + 1)
            pe.wait_ge(*evac_count(T_WO + 4 + 2 * j + f))

        ffn_up(True, first_waits)
        with pe.Fori(1, n_turn) as turn:
            def waits(j, f):
                pe.wait_ge(S["lo_done"], turn * 6 + (split0 + 2 * j + f + 1))
                pe.wait_ge(S[("silu_done", "prod_done")[j]], turn * 2 + (f - 1))
            ffn_up(False, waits)
            for f in range(2):
                pe.wait_ge(S["act_ready"], turn * 2 + (f - 1))
                pe.wait_ge(S["lo_done"], turn * 6 + (split0 - 6 + 4 + f + 1))
                for e in range(KD):
                    wh, wl = out_parts(f, e)
                    last = three(acc(e), wh, wl, a_hi[:, f, :], a_lo[:, f, :], False, False)
                last.then_inc(S["fo_used"], 1)
        pe.wait_ge(S["act_ready"], 2 * n_turn)
        pe.wait_ge(S["lo_done"], split0 + 6 * n_turn)

        def fin_T(f):
            pe.wait_ge(S["xg_ready"], f + 1)
            for tt in range(2):
                last = nc.tensor.transpose(bank[2 * tt + f // 4][:, (f % 4) * P:(f % 4 + 1) * P],
                                           x1g[:, f, tt * P:(tt + 1) * P], ident[:, :])
            last.then_inc(S["fin_T"], 1)

        def fin_squares(f):
            pe.wait_ge(S["sqf_ready"], f + 1)
            if f == 0:
                pe.wait_ge(S["x2_ready"], 2)
            for tt in range(2):
                last = mm(bank[4][:, tt:tt + 1], sq[:, f % 2, tt * P:(tt + 1) * P], ones[:, 0:1],
                          start=f == 0 and tt == 0, stop=f == KD - 1, skip_group_check=True)
            last.then_inc(S["ssf_mm"], 1)

        for e in range(KD):
            for f in range(2):
                wh, wl = out_parts(f, e)
                last = three(acc(e), wh, wl, a_hi[:, f, :], a_lo[:, f, :], False, f == 1)
            last.then_inc(S["x2_mm"], 1)
            if e >= 3:
                fin_T(e - 3)
                fin_squares(e - 3)
        for f in range(KD - 3, KD):
            fin_T(f)
            fin_squares(f)


def kernel(**inputs):
    import numpy as np
    import concourse.bacc as bacc
    from concourse.bass_utils import run_bass_kernel_spmd

    a = {k: np.asarray(v) for k, v in inputs.items()}
    sg = {k: a[k][0] for k in ("w_mod", "w_in", "w_out_a", "w_glu", "w_o", "w_ff_in", "w_ff_out")}
    b_in = a["b_in"][0].reshape(-1, P)
    vec_rows = np.concatenate([a["b_mod"][0].reshape(-1, P), b_in[:C_U // P], b_in[C_U // P + KC:],
                               a["b_glu"][0].reshape(-1, P), a["norm1_g"][0].reshape(-1, P),
                               a["norm2_g"][0].reshape(-1, P), a["final_g"].reshape(-1, P),
                               a["conv_w"][0].reshape(-1, P)])

    def rows(z):
        z = z.reshape(DG, NS).T
        return np.concatenate([z, z])

    def b_rows(re, im):
        re, im = (z.reshape(DG, NS, H).transpose(1, 0, 2) for z in (re, im))
        return np.stack([np.concatenate([re, im]), np.concatenate([im, re])], axis=1)

    log_dt = np.repeat(a["log_dt"][0].reshape(1, DG), P, axis=0)
    ins = {
        "x": a["x"][0], "ctx": a["ctx"][0], **sg, "vec_rows": vec_rows,
        "c_rows": np.concatenate([a["c"].reshape(KD, P), a["c_ctx"].reshape(KD, P)]),
        "lam_pack": np.stack([rows(a["lam_re"][0]), rows(a["lam_im"][0]), log_dt], axis=1),
        "b_pack": b_rows(a["b_re"][0], a["b_im"][0]),
        "c_pack": b_rows(a["c_re"][0].transpose(0, 1, 3, 2), a["c_im"][0].transpose(0, 1, 3, 2)),
        "bu_pack": np.tile(a["b_in"][0][C_U:C_U + DC].reshape(NG, H).T, (CH, 1)),
        "d_pack": a["d_skip"][0].reshape(NG, H).T,
    }
    nc = bacc.Bacc("TRN2", target_bir_lowering=False, num_devices=1)
    arrays, t = {}, {}
    for name, z in ins.items():
        z = np.ascontiguousarray(z)
        arrays[f"in_{name}"] = z
        t[name] = nc.dram_tensor(f"in_{name}", z.shape, mybir.dt.from_np(z.dtype), kind="ExternalInput").ap()
    out = nc.dram_tensor("out", (NT, D), F32, kind="ExternalOutput").ap()
    with ExitStack() as ctx:
        build(nc, t, out, ctx)
    r = run_bass_kernel_spmd(nc, [arrays], core_ids=[0])
    return r.results[0]["out"].reshape(1, NT, D)
```

```python
from contextlib import ExitStack

import concourse.bass as bass
from concourse import mybir

ACT = mybir.ActivationFunctionType
ALU = mybir.AluOpType
F32 = mybir.dt.float32
F32R = mybir.dt.float32r

P = 128
D = 1024
KD = D // P
NT = 256
DC = D // 2
KC = DC // P
DFF = 2816
KF = DFF // P
GRID_W = 64
H = 16
NG = DC // H
NS = 64
DG = 2 * NG
CH = 8
NC = NT // CH
EPS = 1e-6
PI = 3.141592653589793
TWO_PI_HI, TWO_PI_MID = 6.28125, 0.0019350051879882812
TWO_PI_LO = 2 * PI - TWO_PI_HI - TWO_PI_MID
PI_BELOW = 3.1415925
ROUND = 1.5 * 2.0 ** 23

V_BMOD, V_BIN, V_BGLU, V_N1, V_N2, V_FG, V_CONV = 0, 48, 76, 92, 100, 108, 116
C_GB, C_GC, C_XIN, C_U, C_GA, C_GATEB = 0, DC, 2 * DC, 3 * DC, 4 * DC, 4 * DC + D

N_RAW = 3
UNIT = 2048
HALF = UNIT // 2
N_PIECE = 4

def build(nc, t, out, ctx):
    base = -(-nc.sbuf_base // 64) * 64

    def at(name, kb, shape, dt=F32):
        return nc.alloc_sbuf_tensor_at(name, shape, dt, offset=base + int(kb * 1024))

    raw = at("raw", 0, [P, N_RAW, UNIT])
    w_hi = [at(f"w_hi{i}", 24 + 16 * i, [P, UNIT], F32R) for i in range(N_RAW)]
    w_lo = [at(f"w_lo{i}", 32 + 16 * i, [P, UNIT], F32R) for i in range(N_RAW)]
    hT = at("hT", 56, [P, KD, CH, 2, NC])
    xnT = at("xnT", 40, [P, KD, 2 * NT])
    xtok = at("xtok", 56, [P, 4, D])
    b_half = at("b_half", 40, [P, 2, 512])
    b_T = at("b_T", 44, [P, 4, 512])
    gbv = at("gbv", 52, [P, KC, NT])
    mod_acc = at("mod_acc", 24, [P, 4 * D])
    rows_in = at("rows_in", 72, [P, P])
    crow_in = at("crow_in", 72.5, [16, P])
    c_pow = at("c_pow", 72, [P, DG, CH * H])
    xT = at("xT", 72, [P, KD, NT])
    xtok2 = at("xtok2", 80, [P, 2, D])
    x1T = at("x1T", 88, [P, KD, NT])
    x1g = at("x1g", 96, [P, KD, NT])
    diag = at("diag", 104, [P, 4, P])
    sq_junk = at("sq_junk", 106, [P, D])
    v_rows = at("v_rows", 104, [2 * NC, NG, CH, H])
    X = at("X", 104, [P, DG, 2 * NC])
    p_rev = at("p_rev", 116, [P, NG, NC])
    m_hi = at("m_hi", 104, [P, KD, NT], F32R)
    m_lo = at("m_lo", 112, [P, KD, NT], F32R)
    u_pack = at("u_pack", 120, [P, NG, 2 * NC])
    mod_rows = at("mod_rows", 120, [2, 2 * D])
    r_rows = at("r_rows", 128, [H, 2, 8, 256])
    p_st = at("p_st", 128, [P, DG, NC])
    toep = at("toep", 136, [P, NG, CH * H])
    h2_hi = at("h2_hi", 136, [P, KD, NT], F32R)
    h2_lo = at("h2_lo", 144, [P, KD, NT], F32R)
    piece = at("piece", 152, [P, N_PIECE, D])
    par_b = at("par_b", 168, [P, 2, DG, H])
    par_c = at("par_c", 176, [P, 2, DG, H])
    ya = at("ya", 168, [P, KD, NT])
    sgb = at("sgb", 176, [P, KD, NT])
    a_hi = at("a_hi", 168, [P, 2, NT], F32R)
    a_lo = at("a_lo", 170, [P, 2, NT], F32R)
    silu_g = at("silu_g", 172, [P, 2, NT])
    gu = at("gu", 174, [P, 2, NT])
    e_re = at("e_re", 184, [P, 9, DG])
    e_im = at("e_im", 186.25, [P, 9, DG])
    tc = at("tc", 188.5, [P, 2, DG, CH])
    s_hi = at("s_hi", 184, [P, KC, NT], F32R)
    s_lo = at("s_lo", 188, [P, KC, NT], F32R)
    fin = at("fin", 184, [P, 2, D])
    sm = at("sm", 192.5, [P, 16, DG])
    tA = at("tA", 197, [P, 512])
    tB = at("tB", 199, [P, 512])
    s32 = at("s32", 197, [P, KC, NT])
    zrow = at("zrow", 178, [1, P + 512])
    mrg = at("mrg", 192.5, [P, 2, NT])
    yb = at("yb", 194.5, [P, 2, NT])
    sq = at("sq", 197, [P, 2, NT])
    bc = at("bc", 199, [P, 2, NT])
    gv = at("gv", 201, [P, 2, NT])
    cv = at("cv", 203, [P, 2, NT])
    y_rows = at("y_rows", 201, [P, CH, 8, H])
    sg = at("sg", 201, [P, 2, NT])
    end = [205.0]

    def small(name, cols, rows=P):
        end[0] += -(-cols // 8) * 8 / 256
        return at(name, end[0] - -(-cols // 8) * 8 / 256, [rows, cols])

    ident, ones, vecT = small("ident", P), small("ones", P), small("vecT", P)
    csil, bu, d_skip = small("csil", 16), small("bu", NG), small("d_skip", NG, H)
    sgn, halfpi, epsc = small("sgn", 1), small("halfpi", 1), small("epsc", 1)
    ssum, srow, rstd = small("ssum", 4), small("srow", 4), small("rstd", 4)
    mod1, gs1, mod2, gs2 = small("mod1", 32), small("gs1", 16), small("mod2", 32), small("gs2", 8)
    d_diag = at("d_diag", 196.5, [H, 8, H])
    assert end[0] <= 207.7, end[0]

    bank = [ctx.enter_context(nc.psum_tensor(f"bank{i}", [P, 512], F32)) for i in range(8)]
    r_dram = nc.dram_tensor("r_scratch", (NG, H, 240), F32, kind="Internal").ap()

    def sem(name):
        return ctx.enter_context(nc.semaphore(name))

    rows_in_s, lam_s, par_c_s, par_b_s, x_s, ctx_s, pack_s, xtok2_s, out_s, toep_s = (sem(n) for n in (
        "rows_loaded", "lam_loaded", "par_c_loaded", "par_b_loaded", "x_loaded", "ctx_loaded", "packs_loaded",
        "xtok2_loaded", "out_stored", "toep_loaded"))
    r_out_s = [sem(f"r_rows_stored{i}") for i in range(2)]
    raw_full = [sem(f"raw_full{i}") for i in range(N_RAW)]
    piece_full = [sem(f"piece_full{i}") for i in range(N_PIECE)]
    piece2_full = [sem(f"piece2_full{i}") for i in range(N_PIECE)]
    S = {n: sem(n) for n in (
        "mod_rows_ready mod1_T zeroed consts dt_ready lamdt_ready mag_ready trig_arg sin_done dve_step powers_ready "
        "rows_T csil_ready vec_ready sums_done sqrt_done diag_ready xn_mm xn_evac gs_ready h_ready "
        "piece_used_pe piece_used_dve acc_ready mod2_mm mod2_ready "
        "cpow_ready h_mm h_evac r_added u_mm u_rows u_T u_packed b_ready b_Tmm b_Tevac x_mm x_evac back_done rev_ready scan_done "
        "raw_used mm_done evac_act evac_dve ya_scaled y_mm y_evac s_T s_gelu s_hi_done s_ready "
        "hi_done lo_done sg_ready mrg_ready mul_done m_hi_done m_ready xT_mm xT_evac "
        "sq_ready x1g_ready ss_mm sqrt2_done t2_ready h2_hi_done h2_ready zrow_ready "
        "gate_mm up_mm silu_done prod_done a_hi_done act_ready fo_used x2_mm x2_ready sqf_ready xg_ready ssf_mm "
        "fin_T sqrt3_done rstd3_done fin_act fin_dve").split()}

    w_in, w_oa, w_glu, w_o, w_fi, w_fo = (t[n] for n in ("w_in", "w_out_a", "w_glu", "w_o", "w_ff_in", "w_ff_out"))

    def rows_of(w, col, n):
        return w[:, col:col + n].rearrange("(k p) n -> p k n", p=P)

    units = [(KD, [(0, 256, rows_of(w_in, C_U + 256 * q, 256))]) for q in range(2)]
    for q in range(2):
        units += [(KD, [(0, 256, rows_of(w_in, c + 256 * q, 256))]) for c in (C_GC, C_XIN, C_GB)]
    units += [(KC, [(0, 512, rows_of(w_oa, 512 * q, 512))]) for q in range(2)]
    units += [(KD, [(0, 256, rows_of(w_in, C_GA + 256 * q, 256))]) for q in range(8)]
    n_native = len(units)
    units += [(KC, [(256 * j, 256, rows_of(w_glu, c + 256 * q, 256)) for j, c in enumerate((D, 0))]) for q in range(4)]
    units += [(KD, [(0, 256, rows_of(w_o, 256 * q, 256))]) for q in range(4)]
    n_pre = len(units)
    n_turn = KF // 2
    U0_GC, U0_OA, U0_GATE, U0_GLU, U0_WO = 2, 8, 10, n_native, n_native + 4
    split0 = 2 * (n_pre - n_native)
    split1 = split0 + 4
    ffn_slot = [(n_pre + j) % N_RAW for j in range(3)]
    loads, raw_count = [0] * N_RAW, []
    for q, (_, parts) in enumerate(units):
        loads[q % N_RAW] += 16 * len(parts)
        raw_count.append(loads[q % N_RAW])
    ffn_raw0 = list(loads)

    raw_slot = [raw[:, i, :] for i in range(N_RAW)]

    def kview(ap, k):
        return ap.rearrange("p (k n) -> p k n", k=k)

    def half_of(buf, slot, half, k):
        n = UNIT // k // 2
        return kview(buf[slot][:, :], k)[:, :, half * n:half * n + n]

    conv_tiles = ["act", "act", "dve", "dve", "dve", "dve"] * 2
    evac_by = conv_tiles + ["act"] * 8 + ["act"] * 16 + ["act", "act", "dve", "dve"] * 4 + ["dve"] * 8
    T_OA, T_GATE, T_GLU, T_WO = 12, 20, 36, 52
    Y_AT, S_AT = 10, 12

    def evac_count(tile):
        by = evac_by[tile]
        return S["evac_" + by], evac_by[:tile + 1].count(by)

    def bias_of(col):
        c = V_BIN + (col // P if col < C_U else col // P - KC)
        return vecT[:, c:c + 1]

    def half_used(n):
        return T_GLU + 2 * n + 2 if n < 8 else T_WO + n - 8 + 1

    def h_banks(c):
        return (4, 7) if c % 2 else (5, 6)

    def cut_of(n):
        q = n_native + n // 2
        return units[q][0] if q < n_pre else (KD, KD, 2)[q - n_pre]

    def unit_used(q):
        if q < U0_GC:
            return S["u_mm"], q + 1
        if q < U0_OA:
            return S["mm_done"], 2 * (q - U0_GC) + 2
        if q < U0_GATE:
            return S["mm_done"], T_OA + 4 * (q - U0_OA) + 4
        return S["mm_done"], T_GATE + 2 * (q - U0_GATE) + 2

    block = ctx.enter_context(nc.Block())

    @block.sync
    def _(sp):
        sp.dma_start(crow_in[:, :], t["c_rows"]).then_inc(rows_in_s, 16)
        sp.dma_start(rows_in[:, :], t["vec_rows"]).then_inc(rows_in_s, 16)
        sp.dma_start(sm[:, 0:3, :], t["lam_pack"]).then_inc(lam_s, 16)
        sp.dma_start(xtok[:, 0:2, :], t["x"].rearrange("(a p) d -> p a d", p=P)).then_inc(x_s, 16)
        sp.dma_start(xtok[:, 2:4, :], t["ctx"].rearrange("(a p) d -> p a d", p=P)).then_inc(ctx_s, 16)

        def load_unit(q):
            slot, (k, parts) = q % N_RAW, units[q]
            old = q - N_RAW
            if old >= 0 and old < n_native:
                sp.wait_ge(*unit_used(old))
            elif old >= 0:
                sp.wait_ge(S["lo_done"], 2 * (old - n_native) + 2)
            for c0, n, src in parts:
                sp.dma_start(kview(raw[:, slot, :], k)[:, :, c0:c0 + n], src).then_inc(raw_full[slot], 16)

        for n in range(16):
            if n >= N_PIECE:
                sp.wait_ge(S["piece_used_pe"], n - N_PIECE + 1)
            sp.dma_start(piece[:, n % N_PIECE, :], t["w_mod"][(n // 2) * P:(n // 2 + 1) * P, (n % 2) * D:(n % 2 + 1) * D]
                         ).then_inc(piece_full[n % N_PIECE], 16)
            if n == 1:
                sp.dma_start(par_c[:, :, :, :], t["c_pack"]).then_inc(par_c_s, 16)
            if n == 13:
                sp.dma_start(par_b[:, :, :, :], t["b_pack"]).then_inc(par_b_s, 16)
                sp.dma_start(bu[:, :], t["bu_pack"]).then_inc(pack_s, 16)
                sp.dma_start(d_skip[:, :], t["d_pack"]).then_inc(pack_s, 16)
            if n == 11:
                load_unit(0)
        for q in range(1, n_pre):
            load_unit(q)
            if q == U0_OA:
                sp.wait_ge(r_out_s[0], 32)
                sp.wait_ge(r_out_s[1], 32)
                for j in range(CH):
                    sp.dma_start(toep[H * j:H * j + H, :, :],
                                 r_dram[:, :, (CH - 1 - j) * H:(CH - 1 - j) * H + CH * H].rearrange("g h n -> h g n")
                                 ).then_inc(toep_s, 16)
            if q == U0_GLU + 2:
                sp.wait_ge(S["y_mm"], 1)
                sp.dma_start(xtok2[:, :, :], t["x"].rearrange("(a p) d -> p a d", p=P)).then_inc(xtok2_s, 16)
        def load_ffn(j, turn):
            slot = ffn_slot[j]
            if j < 2:
                src = w_fi[:, bass.ds(turn * 256 + j * DFF, 256)].rearrange("(k p) n -> p k n", p=P)
                sp.dma_start(kview(raw[:, slot, :], KD), src).then_inc(raw_full[slot], 16)
            else:
                src = w_fo[bass.ds(turn * 256, 256), :].rearrange("(k p) n -> p k n", p=P)
                sp.dma_start(kview(raw[:, slot, :], 2), src).then_inc(raw_full[slot], 16)

        for j in range(3):
            sp.wait_ge(S["lo_done"], split0 - 6 + 2 * j + 2)
            load_ffn(j, 0)
        for j in range(2):
            sp.wait_ge(S["lo_done"], split0 + 2 * j + 2)
            load_ffn(j, 1)
        with sp.Fori(1, n_turn - 1) as turn:
            for j in range(3):
                sp.wait_ge(S["lo_done"], turn * 6 + (split1 - 6 + 2 * j + 2))
                load_ffn(j, turn + 1 if j < 2 else turn)
        sp.wait_ge(S["lo_done"], split1 + 6 * (n_turn - 1))
        load_ffn(2, n_turn - 1)
        for tt in range(2):
            sp.wait_ge(S["fin_act"], tt + 1)
            sp.wait_ge(S["fin_dve"], tt + 1)
            sp.dma_start(out[tt * P:(tt + 1) * P, :], fin[:, tt, :]).then_inc(out_s, 16)
        sp.wait_ge(out_s, 32)

    @block.gpsimd
    def _(pool):
        g = nc.gpsimd
        g.memset(ident[:, :], 0.0).then_inc(S["zeroed"], 1)
        pool.wait_ge(S["zeroed"], 1)
        g.affine_select(out=ident[:, :], in_=ident[:, :], compare_op=ALU.not_equal, fill=1.0, base=0,
                        pattern=[[-1, P]], channel_multiplier=1).then_inc(S["consts"], 1)
        for i, (buf, rows, value) in enumerate(((ones, slice(0, P), 1.0), (halfpi, slice(0, P), PI / 2),
                                 (epsc, slice(0, P), EPS), (sgn, slice(0, NS), 1.0), (sgn, slice(NS, P), -1.0))):
            pool.wait_ge(S["consts"], i + 1)
            g.memset(buf[rows, :], value).then_inc(S["consts"], 1)

        def mod_piece(m):
            n, k, c = 16 + m, m // 4, m % 4
            if m < N_PIECE:
                pool.wait_ge(S["piece_used_pe"], n - N_PIECE + 1)
            else:
                pool.wait_ge(S["piece_used_dve"], m - N_PIECE + 1)
            pool.dma_start(piece[:, n % N_PIECE, :], t["w_mod"][k * P:(k + 1) * P, (2 + c) * D:(3 + c) * D]
                           ).then_inc(piece2_full[n % N_PIECE], 16)

        for m in range(32):
            mod_piece(m)
        for f in range(KD):
            pool.wait_ge(S["evac_act"], evac_count(T_GATE + f)[1])
            g.tensor_tensor(ya[:, f, :], ya[:, f, :], gv[:, f % 2, :], ALU.mult).then_inc(S["ya_scaled"], 1)
        pool.wait_ge(S["evac_act"], evac_count(T_GATE + 15)[1])
        pool.wait_ge(S["ya_scaled"], KD)
        pool.wait_ge(S["scan_done"], 1)
        for f in range(KD):
            pool.wait_ge(*evac_count(T_GLU + 4 * (f // 2) + 2 + f % 2))
            if f >= 2:
                pool.wait_ge(S["m_ready"], f - 1)
            g.tensor_tensor(mrg[:, f % 2, :], yb[:, f % 2, :], sgb[:, f, :], ALU.mult).then_inc(S["mul_done"], 1)
            pool.wait_ge(S["mul_done"], f + 1)
            g.tensor_tensor(mrg[:, f % 2, :], mrg[:, f % 2, :], ya[:, f, :], ALU.add).then_inc(S["mrg_ready"], 1)
        pool.wait_ge(S["mrg_ready"], KD)
        g.memset(zrow[:, :], 0.0).then_inc(S["zrow_ready"], 1)

    n_const = 6
    LR, LI, LD, DT, MAG, SN, CS, DEN, NR, FR, FI, T0, T1, T2, T3, T4, T5, T6 = range(18)
    AR = [LR, LI, LD, DT, MAG]
    QI = [SN, CS, DEN, NR, FR]

    @block.scalar
    def _(act):
        A, copy = nc.scalar.activation, nc.scalar.copy

        act.wait_ge(lam_s, 16)
        A(sm[:, DT, :], sm[:, LD, :], ACT.Exp).then_inc(S["dt_ready"], 1)
        act.wait_ge(S["lamdt_ready"], 1)
        A(sm[:, MAG, :], sm[:, T0, :], ACT.Exp).then_inc(S["mag_ready"], 1)
        act.wait_ge(S["consts"], n_const)
        act.wait_ge(S["trig_arg"], 1)
        A(sm[:, SN, :], sm[:, T1, :], ACT.Sin).then_inc(S["sin_done"], 1)
        A(sm[:, CS, :], sm[:, T2, :], ACT.Sin, bias=halfpi[:, 0:1], scale=-1.0).then_inc(S["sin_done"], 1)
        act.wait_ge(S["rows_T"], 2)
        A(csil[:, :], bank[7][:, P:P + 16], ACT.Silu).then_inc(S["csil_ready"], 1)
        copy(vecT[:, :], bank[7][:, 0:P]).then_inc(S["vec_ready"], 1)
        act.wait_ge(x_s, 16)
        for tt in range(4):
            if tt == 2:
                act.wait_ge(ctx_s, 16)
            if tt:
                act.wait_ge(S["sums_done"], tt)
            A(sq_junk[:, :], xtok[:, tt, :], ACT.Square, accum_out=ssum[:, tt:tt + 1]).then_inc(S["sums_done"], 1)
        act.wait_ge(S["sums_done"], 4)
        A(srow[:, :], ssum[:, :], ACT.Sqrt, bias=epsc[:, 0:1], scale=1.0 / D).then_inc(S["sqrt_done"], 1)
        for k in range(KD):
            act.wait_ge(S["xn_mm"], k + 1)
            copy(xnT[:, k, :], bank[k % 4][:, :]).then_inc(S["xn_evac"], 1)

        def h_rows(c):
            act.wait_ge(S["h_mm"], c + 1)
            if c % 2 == 0 and c >= 4:
                act.wait_ge(r_out_s[c // 2 % 2], 16)
            for b in range(2):
                src = bank[h_banks(c)[b]][0:H, :].rearrange("h (g n) -> h g n", g=4)
                dst = r_rows[:, c // 2 % 2, 4 * b:4 * b + 4, :]
                if c % 2 == 0:
                    copy(dst[:, :, 128:256], src).then_inc(S["h_evac"], 1)
                else:
                    copy(dst[:, :, 16:128], src[:, :, 0:112])
                    copy(dst[:, :, 0:16], src[:, :, 112:128]).then_inc(S["h_evac"], 1)
            if c % 2:
                act.wait_ge(S["r_added"], c // 2 + 1)
                act.dma_start(r_dram[8 * (c // 2):8 * (c // 2) + 8, :, :].rearrange("g h n -> h g n"),
                              r_rows[:, c // 2 % 2, :, 16:256]).then_inc(r_out_s[c // 2 % 2], 16)

        act.wait_ge(S["piece_used_pe"], 16)
        for b in range(2):
            copy(mod_rows[:, 512 * b:512 * (b + 1)], bank[4 + b][0:2, :]).then_inc(S["mod_rows_ready"], 1)
        act.wait_ge(S["gs_ready"], 1)
        act.wait_ge(S["xn_evac"], KD)
        for k in range(KD):
            for s in range(2):
                A(hT[:, k, :, s, :].rearrange("p j c -> p c j"), xnT[:, k, s * NT:(s + 1) * NT], ACT.Identity,
                  bias=mod1[:, 2 * k + s:2 * k + s + 1], scale=gs1[:, 2 * k + s:2 * k + s + 1]).then_inc(S["h_ready"], 1)
        h_rows(0)
        h_rows(1)
        for half in range(2):
            act.wait_ge(S["u_mm"], half + 1)
            for m in range(4):
                for jj in range(2):
                    copy(v_rows[:, 16 * half:16 * half + 16, 2 * m + jj, :],
                         bank[2 * half + m // 2][NS * jj:NS * jj + NS, 256 * (m % 2):256 * (m % 2) + 256]
                         .rearrange("c (g h) -> c g h", h=H)).then_inc(S["u_rows"], 1)
            for c in ((2, 3), (4, 5, 6, 7))[half]:
                h_rows(c)

        def b_T_evac(n):
            act.wait_ge(S["b_Tmm"], n + 1)
            if n >= 4:
                act.wait_ge(S["x_mm"], n - 3)
            copy(b_T[:, n % 4, :], bank[5 + n % 2][:, :]).then_inc(S["b_Tevac"], 1)

        def x_evac(n):
            act.wait_ge(S["x_mm"], n + 1)
            copy(X[:, 4 * n:4 * n + 4, :], bank[(4, 7)[n % 2]][:, 0:256].rearrange("p (g c) -> p g c", g=4)
                 ).then_inc(S["x_evac"], 1)

        def ssm_pair(i):
            if i < 8:
                b_T_evac(2 * i)
                b_T_evac(2 * i + 1)
            if i >= 1:
                x_evac(2 * i - 2)
                x_evac(2 * i - 1)

        def tile_bank(tile):
            act.wait_ge(S["mm_done"], tile + 1)
            return bank[tile % 4][:, 0:NT]

        for tile in range(T_OA):
            if 2 <= tile <= 10:
                ssm_pair(tile - 2)
            if evac_by[tile] == "act":
                q, f = tile // 6, tile % 6
                if q:
                    act.wait_ge(*evac_count(4 + f))
                A(gv[:, f, :], tile_bank(tile), ACT.Identity, bias=bias_of(C_GC + 256 * q + P * f)).then_inc(S["evac_act"], 1)
        act.wait_ge(S["b_ready"], 16)
        for f in range(KD):
            copy(ya[:, f, :], tile_bank(T_OA + f)).then_inc(S["evac_act"], 1)
        act.wait_ge(*evac_count(T_OA - 1))
        def gate_tile(f):
            if f >= KD:
                dst, c0 = sgb[:, f - KD, :], C_GATEB - D
            else:
                dst, c0 = gv[:, f % 2, :], C_GA
                if f >= 2:
                    act.wait_ge(S["ya_scaled"], f - 1)
            A(dst, tile_bank(T_GATE + f), ACT.Sigmoid, bias=bias_of(c0 + P * f)).then_inc(S["evac_act"], 1)

        def hi(n):
            q, half = n_native + n // 2, n % 2
            if q < n_pre:
                slot, k, need = q % N_RAW, units[q][0], raw_count[q]
            else:
                j = q - n_pre
                slot, k, need = ffn_slot[j], (KD, KD, 2)[j], ffn_raw0[ffn_slot[j]] + 16
            act.wait_ge(raw_full[slot], need)
            if n == 0:
                act.wait_ge(S["mod2_mm"], 1)
            if n == 2:
                act.wait_ge(S["mm_done"], T_GATE)
            if n == 4:
                act.wait_ge(S["mm_done"], T_GLU)
            if n >= 6:
                act.wait_ge(S["mm_done"], half_used(n - 6 if cut_of(n - 6) == cut_of(n) else (n - 6) | 1))
            ffn_half(slot, half, k)

        def ffn_half(slot, half, k):
            if k > 2:
                src, dst = half_of(raw_slot, slot, half, k), half_of(w_hi, slot, half, k)
            else:
                src, dst = (x[slot][:, half * HALF:(half + 1) * HALF] for x in (raw_slot, w_hi))
            copy(dst, src).then_inc(S["hi_done"], 1)

        for f in range(2 * KD):
            gate_tile(f)
            if f == Y_AT - 1:
                act.wait_ge(S["back_done"], 1)
                copy(p_rev[:, :, :], p_st[:, NG:, ::-1]).then_inc(S["rev_ready"], 1)
            if f == Y_AT:
                for b in range(2):
                    act.wait_ge(S["y_mm"], 1)
                    act.wait_ge(S["ya_scaled"], KD)
                    copy(y_rows[:, :, 4 * b:4 * b + 4, :].rearrange("p i g h -> p g i h"),
                         bank[5 + b][:, :].rearrange("p (g i h) -> p g i h", g=4, i=CH)).then_inc(S["y_evac"], 1)
            if f == S_AT:
                act.wait_ge(S["s_T"], 1)
                for b in range(2):
                    src = bank[(4, 7)[b]][:, :].rearrange("p (i g c) -> p g c i", i=4, g=KC)
                    dst = s32[:, :, :].rearrange("p g (c i) -> p g c i", i=CH)[:, :, :, 4 * b:4 * b + 4]
                    A(dst, src, ACT.Gelu_apprx_tanh).then_inc(S["s_gelu"], 1)
                act.wait_ge(S["s_gelu"], 2)
                copy(s_hi[:, :, :], s32[:, :, :]).then_inc(S["s_hi_done"], 1)
            if f >= 13:
                hi(f - 13)
        for n in range(3, 6):
            hi(n)

        def m_hi_of(f):
            act.wait_ge(S["mrg_ready"], f + 1)
            copy(m_hi[:, f, :], mrg[:, f % 2, :]).then_inc(S["m_hi_done"], 1)

        for q in range(4):
            for f in range(2):
                if q:
                    act.wait_ge(*evac_count(T_GLU + 4 * q - 2 + f))
                b = V_BGLU + KD + 2 * q + f
                A(sg[:, f, :], tile_bank(T_GLU + 4 * q + f), ACT.Sigmoid, bias=vecT[:, b:b + 1]).then_inc(S["evac_act"], 1)
            hi(6 + 2 * q)
            if q:
                m_hi_of(2 * q - 2)
                m_hi_of(2 * q - 1)
            act.wait_ge(S["xT_mm"], q + 1)
            copy(xT[:, 2 * q:2 * q + 2, :], kview(bank[6 - q % 2][:, :], 2)).then_inc(S["xT_evac"], 1)
            hi(7 + 2 * q)
        m_hi_of(6)
        m_hi_of(7)
        for f in range(KD):
            act.wait_ge(S["evac_dve"], evac_count(T_WO + f)[1])
            if f >= 2:
                act.wait_ge(S["ss_mm"], f - 1)
            A(sq[:, f % 2, :], x1T[:, f, :], ACT.Square).then_inc(S["sq_ready"], 1)
            A(x1g[:, f, :], x1T[:, f, :], ACT.Copy, scale=gs2[:, f:f + 1]).then_inc(S["x1g_ready"], 1)
            if f < 6:
                hi(14 + f)
        act.wait_ge(S["ss_mm"], KD)
        A(bc[:, 0, :], bank[4][:, 0:NT], ACT.Sqrt, bias=epsc[:, 0:1], scale=1.0 / D).then_inc(S["sqrt2_done"], 1)
        for k in range(KD):
            act.wait_ge(S["t2_ready"], k + 1)
            A(h2_hi[:, k, :], x1g[:, k, :], ACT.Identity, bias=mod2[:, KD + k:KD + k + 1]).then_inc(S["h2_hi_done"], 1)

        def act_turn(turn, first=False, last=False):
            for f in range(2):
                act.wait_ge(S["gate_mm"], turn * 2 + (f + 1))
                if first:
                    act.wait_ge(S["mrg_ready"], KD)
                else:
                    act.wait_ge(S["prod_done"], turn * 2 + (f - 1))
                A(silu_g[:, f, :], bank[f][:, 0:NT], ACT.Silu).then_inc(S["silu_done"], 1)
            for j in range(2 if last else 0, 3):
                slot = ffn_slot[j]
                act.wait_ge(raw_full[slot], turn * 16 + (ffn_raw0[slot] + (32 if j < 2 else 16)))
                for half in range(2):
                    if j < 2:
                        act.wait_ge(S[("gate_mm", "up_mm")[j]], turn * 2 + (half + 1))
                    elif first:
                        act.wait_ge(S["mm_done"], T_WO + KD)
                    else:
                        act.wait_ge(S["fo_used"], turn * 2 + (half - 1))
                    ffn_half(slot, half, (KD, KD, 2)[j])

        act_turn(0, first=True)
        with act.Fori(1, n_turn - 1) as turn:
            act_turn(turn)
        act_turn(n_turn - 1, last=True)
        for f in range(KD):
            act.wait_ge(S["x2_ready"], f + 1)
            if f >= 2:
                act.wait_ge(S["ssf_mm"], f - 1)
            A(sq[:, f % 2, :], x1T[:, f, :], ACT.Square).then_inc(S["sqf_ready"], 1)
        act.wait_ge(S["ssf_mm"], KD)
        A(srow[:, 0:2], bank[4][:, 0:2], ACT.Sqrt, bias=epsc[:, 0:1], scale=1.0 / D).then_inc(S["sqrt3_done"], 1)
        act.wait_ge(S["rstd3_done"], 1)
        act.wait_ge(S["fin_T"], KD)
        for tt in range(2):
            A(fin[:, tt, DC:D], bank[2 * tt + 1][:, :], ACT.Copy, scale=rstd[:, tt:tt + 1]).then_inc(S["fin_act"], 1)

    @block.vector
    def _(dve):
        v = nc.vector
        steps = [0]

        def step():
            steps[0] += 1
            return steps[0]

        def tt(o, a, b, op):
            return v.tensor_tensor(o, a, b, op)

        def stt(o, a, s, b, op0, op1):
            return v.scalar_tensor_tensor(out=o, in0=a, scalar=s, in1=b, op0=op0, op1=op1)

        def q(i):
            return sm[:, i, :]

        M, AD, SU = ALU.mult, ALU.add, ALU.subtract
        dve.wait_ge(S["dt_ready"], 1)
        tt(q(T0), q(LR), q(DT), M).then_inc(S["lamdt_ready"], 1)
        tt(q(T1), q(LI), q(DT), M).then_inc(S["dve_step"], 1)
        dve.wait_ge(S["dve_step"], step())
        v.tensor_scalar(q(T2), q(T1), 1.0 / (2 * PI), ROUND, M, AD).then_inc(S["dve_step"], 1)
        dve.wait_ge(S["dve_step"], step())
        v.tensor_scalar(q(T2), q(T2), ROUND, None, SU).then_inc(S["dve_step"], 1)
        dve.wait_ge(S["dve_step"], step())
        for part in (TWO_PI_HI, TWO_PI_MID, TWO_PI_LO):
            stt(q(T1), q(T2), -part, q(T1), M, AD).then_inc(S["dve_step"], 1)
            dve.wait_ge(S["dve_step"], step())
        v.tensor_scalar(q(T1), q(T1), PI_BELOW, -PI_BELOW, ALU.min, ALU.max).then_inc(S["dve_step"], 1)
        dve.wait_ge(S["dve_step"], step())
        stt(q(T2), q(T1), -1.0, q(T1), M, ALU.max).then_inc(S["trig_arg"], 1)
        tt(q(T3), q(LR), q(LR), M).then_inc(S["dve_step"], 1)
        dve.wait_ge(S["dve_step"], step())
        tt(q(T4), q(LI), q(LI), M).then_inc(S["dve_step"], 1)
        dve.wait_ge(S["dve_step"], step())
        tt(q(DEN), q(T3), q(T4), AD).then_inc(S["dve_step"], 1)
        dve.wait_ge(S["dve_step"], step())
        v.reciprocal(q(DEN), q(DEN)).then_inc(S["dve_step"], 1)
        dve.wait_ge(S["dve_step"], step())
        dve.wait_ge(S["mag_ready"], 1)
        dve.wait_ge(S["sin_done"], 2)
        dve.wait_ge(S["consts"], n_const)
        v.memset(e_re[:, 0, :], 1.0)
        v.memset(e_im[:, 0, :], 0.0)
        tt(e_re[:, 1, :], q(MAG), q(CS), M)
        tt(e_im[:, 1, :], q(MAG), q(SN), M).then_inc(S["dve_step"], 1)
        dve.wait_ge(S["dve_step"], step())
        v.tensor_scalar(q(NR), e_re[:, 1, :], -1.0, None, AD).then_inc(S["dve_step"], 1)
        dve.wait_ge(S["dve_step"], step())
        tt(q(T0), q(NR), q(LR), M)
        tt(q(T1), e_im[:, 1, :], q(LI), M)
        tt(q(T2), e_im[:, 1, :], q(LR), M)
        tt(q(T3), q(NR), q(LI), M).then_inc(S["dve_step"], 1)
        dve.wait_ge(S["dve_step"], step())
        tt(q(T0), q(T0), q(T1), AD)
        tt(q(T2), q(T2), q(T3), SU).then_inc(S["dve_step"], 1)
        dve.wait_ge(S["dve_step"], step())
        tt(q(FR), q(T0), q(DEN), M)
        tt(q(FI), q(T2), q(DEN), M).then_inc(S["dve_step"], 1)
        dve.wait_ge(S["dve_step"], step())

        def power(dst, n, by, src):
            def b(i):
                return e[i][:, by:by + 1, :].broadcast_to([P, n, DG])
            e = (e_re, e_im)
            s_re, s_im = e_re[:, src:src + n, :], e_im[:, src:src + n, :]
            t_a, t_b = (x[:, 0:n * DG].rearrange("p (n d) -> p n d", n=n) for x in (tA, tB))
            t_a2, t_b2 = (x[:, 256:256 + n * DG].rearrange("p (n d) -> p n d", n=n) for x in (tA, tB))
            tt(t_a, s_re, b(0), M)
            tt(t_b, s_im, b(1), M)
            tt(t_a2, s_re, b(1), M)
            tt(t_b2, s_im, b(0), M).then_inc(S["dve_step"], 1)
            dve.wait_ge(S["dve_step"], step())
            tt(e_re[:, dst:dst + n, :], t_a, t_b, SU)
            tt(e_im[:, dst:dst + n, :], t_a2, t_b2, AD).then_inc(S["dve_step"], 1)
            dve.wait_ge(S["dve_step"], step())

        power(2, 1, 1, 1)
        power(3, 2, 2, 1)
        power(5, 4, 4, 1)
        for d in range(2):
            dg = slice(NG * d, NG * d + NG)
            o = [tc[:, i, dg, :].rearrange("p g e -> p e g") for i in range(2)]
            src = [(x[:, 0:8, dg] if d == 0 else x[:, 7::-1, dg]) for x in (e_re, e_im)]
            f_re, f_im = (sm[:, i:i + 1, dg].broadcast_to([P, CH, NG]) for i in (FR, FI))
            t_a, t_b, = (x[:, 0:CH * NG].rearrange("p (n d) -> p n d", n=CH) for x in (tA, tB))
            t_a2, t_b2 = (x[:, 256:256 + CH * NG].rearrange("p (n d) -> p n d", n=CH) for x in (tA, tB))
            tt(t_a, src[0], f_re, M)
            tt(t_b, src[1], f_im, M)
            tt(t_a2, src[0], f_im, M)
            tt(t_b2, src[1], f_re, M).then_inc(S["dve_step"], 1)
            dve.wait_ge(S["dve_step"], step())
            tt(t_a, t_a, t_b, SU).then_inc(S["dve_step"], 1)
            dve.wait_ge(S["dve_step"], step())
            tt(t_a2, t_a2, t_b2, AD).then_inc(S["dve_step"], 1)
            dve.wait_ge(S["dve_step"], step())
            v.tensor_scalar(o[0], t_a, sgn[:, 0:1], None, M)
            v.tensor_scalar(o[1], t_a2, -1.0, None, M).then_inc(S["dve_step"], 1)
            dve.wait_ge(S["dve_step"], step())
        v.tensor_scalar(e_im[:, 1:9, :], e_im[:, 1:9, :], sgn[:, 0:1], -1.0, M, M).then_inc(S["dve_step"], 1)
        dve.wait_ge(S["dve_step"], step())

        def table(dst, par, dg, f0, f1, n_e):
            shape = [P, 4, n_e, H]
            t_a, t_b = (x[:, :].rearrange("p (g e h) -> p g e h", g=4, e=n_e) for x in (tA, tB))
            tt(t_a, par[:, 0, dg, None, :].broadcast_to(shape), f0[:, :, :, None].broadcast_to(shape), M)
            tt(t_b, par[:, 1, dg, None, :].broadcast_to(shape), f1[:, :, :, None].broadcast_to(shape), M).then_inc(S["dve_step"], 1)
            dve.wait_ge(S["dve_step"], step())
            return tt(dst, tA[:, :], tB[:, :], AD)

        dve.wait_ge(par_c_s, 16)
        dve.wait_ge(S["rows_T"], 2)

        def c_chunk(c):
            for hh in range(2):
                g0 = NG * (c % 2) + 8 * (c // 2) + 4 * hh
                dg = slice(g0, g0 + 4)
                table(c_pow[:, dg, :], par_c, dg, tc[:, 0, dg, :], tc[:, 1, dg, :], CH).then_inc(S["cpow_ready"], 1)
                dve.wait_ge(S["cpow_ready"], 2 * c + hh + 1)

        def r_add(i):
            dve.wait_ge(pack_s, 32)
            if i:
                dve.wait_ge(S["r_added"], i)
            tt(d_diag[:, :, :], ident[0:H, None, 0:H].broadcast_to([H, 8, H]),
               d_skip[:, 8 * i:8 * i + 8, None].broadcast_to([H, 8, H]), M).then_inc(S["dve_step"], 1)
            dve.wait_ge(S["dve_step"], step())
            dve.wait_ge(S["h_evac"], 4 * i + 4)
            tt(r_rows[:, i % 2, :, 128:144], r_rows[:, i % 2, :, 128:144], r_rows[:, i % 2, :, 0:16], AD).then_inc(S["dve_step"], 1)
            dve.wait_ge(S["dve_step"], step())
            tt(r_rows[:, i % 2, :, 128:144], r_rows[:, i % 2, :, 128:144], d_diag[:, :, :], AD).then_inc(S["r_added"], 1)

        def b_chunk(n):
            dve.wait_ge(par_b_s, 16)
            if n < 2:
                dve.wait_ge(S["h_ready"], 2 * KD)
            if n >= 2:
                dve.wait_ge(S["b_Tmm"], n - 1)
            d = n // 8
            dg = slice(4 * n, 4 * n + 4)
            f = [(x[:, 8:0:-1, dg] if d == 0 else x[:, 1:9, dg]).rearrange("p e g -> p g e") for x in (e_re, e_im)]
            table(b_half[:, n % 2, :], par_b, dg, f[0], f[1], CH).then_inc(S["b_ready"], 1)
            dve.wait_ge(S["b_ready"], n + 1)

        def mod_acc_piece(m):
            n, k, c = 16 + m, m // 4, m % 4
            dve.wait_ge(piece2_full[n % N_PIECE], 16 * (m // N_PIECE + 1))
            a = mod_acc[:, c * D:(c + 1) * D]
            if k == 0:
                v.tensor_scalar(a, piece[:, n % N_PIECE, :], csil[:, 0:1], None, M).then_inc(S["piece_used_dve"], 1)
            else:
                dve.wait_ge(S["piece_used_dve"], m - 3)
                stt(a, piece[:, n % N_PIECE, :], csil[:, k:k + 1], a, M, AD).then_inc(S["piece_used_dve"], 1)

        dve.wait_ge(S["sqrt_done"], 1)
        v.reciprocal(rstd[:, :], srow[:, :]).then_inc(S["dve_step"], 1)
        dve.wait_ge(S["dve_step"], step())
        for i in range(4):
            v.tensor_scalar(diag[:, i, :], ident[:, :], rstd[:, i:i + 1], None, M).then_inc(S["diag_ready"], 1)
        for c in range(8):
            c_chunk(c)
        dve.wait_ge(S["piece_used_pe"], 16)
        for b in range(2, 4):
            v.tensor_copy(mod_rows[:, 512 * b:512 * (b + 1)], bank[4 + b][0:2, :]).then_inc(S["mod_rows_ready"], 1)
        dve.wait_ge(S["mod1_T"], 1)
        dve.wait_ge(S["vec_ready"], 1)
        tt(mod1[:, :].rearrange("p (f s) -> p f s", s=2), bank[4][:, 0:32].rearrange("p (f s) -> p f s", s=2),
           vecT[:, V_BMOD:V_BMOD + 16, None].broadcast_to([P, 16, 2]), AD).then_inc(S["dve_step"], 1)
        dve.wait_ge(S["dve_step"], step())
        stt(gs1[:, :].rearrange("p (f s) -> p f s", s=2), mod1[:, 16:32].rearrange("p (f s) -> p f s", s=2), 1.0,
            vecT[:, V_N1:V_N1 + KD, None].broadcast_to([P, KD, 2]), AD, M).then_inc(S["gs_ready"], 1)
        for m in range(16):
            mod_acc_piece(m)
        r_add(0)
        b_chunk(0)
        b_chunk(1)
        for m in range(16, 20):
            mod_acc_piece(m)
        r_add(1)
        for m in range(20, 26):
            mod_acc_piece(m)
        r_add(2)
        for m in range(26, 32):
            mod_acc_piece(m)
        r_add(3)
        for r in range(4):
            dve.wait_ge(S["u_T"], r + 1)
            shape = [P, 8, 2 * NC]
            tt(u_pack[:, 8 * r:8 * r + 8, :], bank[(4, 7)[r % 2]][:, :].rearrange("p (g c) -> p g c", g=8),
               bu[:, 8 * r:8 * r + 8, None].broadcast_to(shape), AD).then_inc(S["u_packed"], 1)

        def tile_bank(tile):
            dve.wait_ge(S["mm_done"], tile + 1)
            return bank[tile % 4][:, 0:NT]

        def conv_tile(tile):
            qq, i = tile // 6, tile % 6
            f = i % 2
            if i < 4:
                dve.wait_ge(S["evac_act"], evac_count(6 * qq + f)[1])
                c0 = V_CONV + 2 * qq + f
                tap = [vecT[:, c0 + KC * j:c0 + KC * j + 1] for j in range(3)]
                stt(gv[:, f, :], tile_bank(tile), bias_of(C_XIN + 256 * qq + P * f), gv[:, f, :], AD, M
                    ).then_inc(S["evac_dve"], 1)
                dve.wait_ge(*evac_count(tile))
                v.tensor_scalar(cv[:, f, :], gv[:, f, :], tap[1], None, M).then_inc(S["dve_step"], 1)
                dve.wait_ge(S["dve_step"], step())
                rows = [x[:, f, :].rearrange("p (r c) -> p r c", c=GRID_W) for x in (gv, cv)]
                stt(rows[1][:, :, 1:], rows[0][:, :, :-1], tap[0], rows[1][:, :, 1:], M, AD).then_inc(S["dve_step"], 1)
                dve.wait_ge(S["dve_step"], step())
                stt(rows[1][:, :, :-1], rows[0][:, :, 1:], tap[2], rows[1][:, :, :-1], M, AD).then_inc(S["dve_step"], 1)
                dve.wait_ge(S["dve_step"], step())
            else:
                stt(gbv[:, 2 * qq + f, :], tile_bank(tile), bias_of(C_GB + 256 * qq + P * f), cv[:, f, :], AD, M
                    ).then_inc(S["evac_dve"], 1)

        for tile in range(2, T_OA):
            i = tile - 2
            if i < 7:
                b_chunk(2 * i + 2)
                b_chunk(2 * i + 3)
            if evac_by[tile] == "dve":
                conv_tile(tile)

        v.tensor_copy(q(AR[0]), e_re[:, 8, :]).then_inc(S["dve_step"], 1)
        dve.wait_ge(S["dve_step"], step())
        v.tensor_scalar(q(T0), e_im[:, 8, :], sgn[:, 0:1], -1.0, M, M).then_inc(S["dve_step"], 1)
        dve.wait_ge(S["dve_step"], step())
        for k in range(5):
            v.tensor_scalar(q(QI[k]), q(T0), sgn[:, 0:1], None, M).then_inc(S["dve_step"], 1)
            dve.wait_ge(S["dve_step"], step())
            if k < 4:
                tt(q(T1), q(AR[k]), q(AR[k]), M)
                tt(q(T2), q(T0), q(T0), M)
                tt(q(T3), q(AR[k]), q(T0), M).then_inc(S["dve_step"], 1)
                dve.wait_ge(S["dve_step"], step())
                tt(q(AR[k + 1]), q(T1), q(T2), SU)
                tt(q(T0), q(T3), q(T3), AD).then_inc(S["dve_step"], 1)
                dve.wait_ge(S["dve_step"], step())

        def advance(src, add, dst, k, g0, n_g, n):
            shape = [P, n_g, n]
            gs = slice(g0, g0 + n_g)
            t_a, t_b = (x[:, 0:n_g * n].rearrange("p (g n) -> p g n", g=n_g) for x in (tA, tB))
            tt(t_a, src, sm[:, AR[k], gs, None].broadcast_to(shape), M)
            lo, up = slice(0, NS), slice(NS, P)
            tt(t_b[lo], src[up], sm[up, QI[k], gs, None].broadcast_to([NS, n_g, n]), M)
            tt(t_b[up], src[lo], sm[lo, QI[k], gs, None].broadcast_to([NS, n_g, n]), M).then_inc(S["dve_step"], 1)
            dve.wait_ge(S["dve_step"], step())
            tt(t_a, t_a, t_b, AD).then_inc(S["dve_step"], 1)
            dve.wait_ge(S["dve_step"], step())
            return tt(dst, t_a, add, AD)

        dve.wait_ge(S["x_evac"], 16)
        for k in range(4):
            s = 1 << k
            n = NC // s
            n_g = min(DG, 512 // n)
            Xv = X[:, :, :].rearrange("p g (n s) -> p g n s", s=2 * s)
            for g0 in range(0, DG, n_g):
                right = Xv[:, g0:g0 + n_g, :, 2 * s - 1]
                advance(Xv[:, g0:g0 + n_g, :, s - 1], right, right, k, g0, n_g, n).then_inc(S["dve_step"], 1)
                dve.wait_ge(S["dve_step"], step())
        dve.wait_ge(S["mod2_mm"], 1)
        tt(mod2[:, :], bank[4][:, 256:288], vecT[:, V_BMOD + 16:V_BMOD + 48], AD).then_inc(S["mod2_ready"], 1)
        dve.wait_ge(S["mod2_ready"], 1)
        stt(gs2[:, :], mod2[:, 2 * KD:3 * KD], 1.0, vecT[:, V_N2:V_N2 + KD], AD, M).then_inc(S["dve_step"], 1)
        dve.wait_ge(S["dve_step"], step())
        last = X[:, :, 2 * NC - 1:2 * NC]
        dve.wait_ge(S["r_added"], 4)
        dve.wait_ge(r_out_s[0], 32)
        dve.wait_ge(r_out_s[1], 32)
        advance(X[:, :, NC + NC // 2 - 1:NC + NC // 2], last, p_st[:, :, 0:1], 4, 0, DG, 1).then_inc(S["dve_step"], 1)
        dve.wait_ge(S["dve_step"], step())
        for k in range(4, -1, -1):
            s = 1 << k
            n = NC // (2 * s)
            n_g = min(DG, 512 // n)
            Xv = X[:, :, 0:NC].rearrange("p g (n s) -> p g n s", s=2 * s)
            Pv = p_st[:, :, :].rearrange("p g (n s) -> p g n s", s=2 * s)
            for g0 in range(DG - n_g, -1, -n_g):
                gs = slice(g0, g0 + n_g)
                done = advance(Pv[:, gs, :, 0], Xv[:, gs, :, s - 1], Pv[:, gs, :, s], k, g0, n_g, n)
                if k == 0:
                    done.then_inc(S["back_done" if g0 else "scan_done"], 1)
                    if g0:
                        dve.wait_ge(S["back_done"], 1)
                else:
                    done.then_inc(S["dve_step"], 1)
                    dve.wait_ge(S["dve_step"], step())
        def lo(n):
            qq, half = n_native + n // 2, n % 2
            dve.wait_ge(S["hi_done"], n + 1)
            if qq < n_pre:
                split_lo(qq % N_RAW, half, units[qq][0])
            else:
                split_lo(ffn_slot[qq - n_pre], half, (KD, KD, 2)[qq - n_pre])

        def split_lo(slot, half, k):
            if k > 2:
                a, h_, o = (half_of(x, slot, half, k) for x in (raw_slot, w_hi, w_lo))
            else:
                a, h_, o = (x[slot][:, half * HALF:(half + 1) * HALF] for x in (raw_slot, w_hi, w_lo))
            tt(o, a, h_.bitcast(F32), SU).then_inc(S["lo_done"], 1)

        dve.wait_ge(S["s_hi_done"], 1)
        tt(s_lo[:, :, :], s32[:, :, :], s_hi[:, :, :].bitcast(F32), SU).then_inc(S["s_ready"], 1)
        for n in range(6):
            lo(n)

        def m_lo_of(f):
            dve.wait_ge(S["m_hi_done"], f + 1)
            tt(m_lo[:, f, :], mrg[:, f % 2, :], m_hi[:, f, :].bitcast(F32), SU).then_inc(S["m_ready"], 1)

        for qq in range(4):
            lo(6 + 2 * qq)
            for f in range(2):
                tile = T_GLU + 4 * qq + 2 + f
                dve.wait_ge(S["evac_act"], evac_count(tile - 2)[1])
                if qq:
                    dve.wait_ge(S["mul_done"], 2 * qq + f - 1)
                b = V_BGLU + 2 * qq + f
                if qq:
                    m_lo_of(2 * qq - 2 + f)
                stt(yb[:, f, :], tile_bank(tile), vecT[:, b:b + 1], sg[:, f, :], AD, M).then_inc(S["evac_dve"], 1)
            lo(7 + 2 * qq)
        m_lo_of(6)
        m_lo_of(7)
        dve.wait_ge(S["xT_evac"], 4)
        for f in range(KD):
            stt(x1T[:, f, :], tile_bank(T_WO + f), mod2[:, f:f + 1], xT[:, f, :], M, AD).then_inc(S["evac_dve"], 1)
            if f < 6:
                lo(14 + f)
        dve.wait_ge(S["sqrt2_done"], 1)
        v.reciprocal(bc[:, 1, :], bc[:, 0, :]).then_inc(S["dve_step"], 1)
        dve.wait_ge(S["dve_step"], step())

        def norm2(k):
            dve.wait_ge(S["x1g_ready"], k + 1)
            tt(x1g[:, k, :], x1g[:, k, :], bc[:, 1, :], M).then_inc(S["t2_ready"], 1)

        def h2_lo_of(k):
            dve.wait_ge(S["h2_hi_done"], k + 1)
            stt(h2_lo[:, k, :], x1g[:, k, :], mod2[:, KD + k:KD + k + 1], h2_hi[:, k, :].bitcast(F32), AD, SU
                ).then_inc(S["h2_ready"], 1)

        norm2(0)
        norm2(1)
        for k in range(KD):
            h2_lo_of(k)
            if k + 2 < KD:
                norm2(k + 2)

        def dve_turn(turn, first=False, last=False):
            def split(j):
                for half in range(2):
                    dve.wait_ge(S["hi_done"], turn * 6 + (split1 + 2 * j + half + 1 - (4 if last else 0)))
                    split_lo(ffn_slot[j], half, (KD, KD, 2)[j])

            if not last:
                split(0)
            for f in range(2):
                dve.wait_ge(S["silu_done"], turn * 2 + (f + 1))
                dve.wait_ge(S["up_mm"], turn * 2 + (f + 1))
                if not first:
                    dve.wait_ge(S["act_ready"], turn * 2 + (f - 1))
                tt(gu[:, f, :], bank[2 + f][:, 0:NT], silu_g[:, f, :], M).then_inc(S["prod_done"], 1)
            if not last:
                split(1)
            for f in range(2):
                if not first:
                    dve.wait_ge(S["fo_used"], turn * 2 + (f - 1))
                dve.wait_ge(S["prod_done"], turn * 2 + (f + 1))
                v.tensor_copy(a_hi[:, f, :], gu[:, f, :]).then_inc(S["a_hi_done"], 1)
                dve.wait_ge(S["a_hi_done"], turn * 2 + (f + 1))
                tt(a_lo[:, f, :], gu[:, f, :], a_hi[:, f, :].bitcast(F32), SU).then_inc(S["act_ready"], 1)
            split(2)

        dve_turn(0, first=True)
        with dve.Fori(1, n_turn - 1) as turn:
            dve_turn(turn)
        dve_turn(n_turn - 1, last=True)
        for f in range(KD):
            dve.wait_ge(S["x2_mm"], 2 * (f // 2) + 2)
            stt(x1T[:, f, :], bank[4 + f // 2][:, (f % 2) * NT:(f % 2 + 1) * NT], mod2[:, 3 * KD + f:3 * KD + f + 1],
                x1T[:, f, :], M, AD).then_inc(S["x2_ready"], 1)
            dve.wait_ge(S["x2_ready"], f + 1)
            v.tensor_scalar(x1g[:, f, :], x1T[:, f, :], vecT[:, V_FG + f:V_FG + f + 1], None, M).then_inc(S["xg_ready"], 1)
        dve.wait_ge(S["sqrt3_done"], 1)
        v.reciprocal(rstd[:, 0:2], srow[:, 0:2]).then_inc(S["rstd3_done"], 1)
        dve.wait_ge(S["rstd3_done"], 1)
        dve.wait_ge(S["fin_T"], KD)
        for i in range(2):
            v.tensor_scalar(fin[:, i, 0:DC], bank[2 * i][:, :], rstd[:, i:i + 1], None, M).then_inc(S["fin_dve"], 1)

    @block.tensor
    def _(pe):
        mm = nc.tensor.matmul

        pe.wait_ge(S["consts"], n_const)
        pe.wait_ge(rows_in_s, 32)
        nc.tensor.transpose(bank[7][:, P:P + 16], crow_in[:, :], ident[0:16, 0:16]).then_inc(S["rows_T"], 1)
        nc.tensor.transpose(bank[7][:, 0:P], rows_in[:, :], ident[:, :]).then_inc(S["rows_T"], 1)

        def mod_part(n):
            pe.wait_ge(piece_full[n % N_PIECE], 16 * (n // N_PIECE + 1))
            if n == 1:
                pe.wait_ge(S["vec_ready"], 1)
            k = n // 2
            for j in range(2):
                last = mm(bank[4 + 2 * (n % 2) + j][0:2, :], csil[:, k:16:KD], piece[:, n % N_PIECE, 512 * j:512 * (j + 1)],
                          start=k == 0, stop=k == KD - 1)
            last.then_inc(S["piece_used_pe"], 1)

        def h_cols(c):
            pe.wait_ge(S["cpow_ready"], 2 * c + 2)
            pe.wait_ge(par_b_s, 16)
            if c == 1:
                pe.wait_ge(S["gs_ready"], 1)
            if c >= 2:
                pe.wait_ge(S["h_evac"], 2 * c - 2)
            for g in range(8):
                dg = NG * (c % 2) + 8 * (c // 2) + g
                last = mm(bank[h_banks(c)[g // 4]][0:H, (g % 4) * P:(g % 4 + 1) * P], par_b[:, 0, dg, :], c_pow[:, dg, :],
                          start=True, stop=True)
            last.then_inc(S["h_mm"], 1)

        pe.wait_ge(S["csil_ready"], 1)
        mod_part(0)
        mod_part(1)
        pe.wait_ge(S["diag_ready"], 4)
        for k in range(KD):
            if k >= 4:
                pe.wait_ge(S["xn_evac"], k - 3)
            for tt in range(4):
                last = mm(bank[k % 4][:, tt * P:(tt + 1) * P], xtok[:, tt, k * P:(k + 1) * P], diag[:, tt, :],
                          start=True, stop=True)
            last.then_inc(S["xn_mm"], 1)
            if k % 2:
                mod_part(2 + k // 2)
        for n in range(6, 16):
            mod_part(n)
        pe.wait_ge(S["mod_rows_ready"], 4)
        for f in range(2 * KD):
            last = nc.tensor.transpose(bank[4][:, 2 * f:2 * f + 2], mod_rows[:, f * P:(f + 1) * P], ident[0:2, 0:2])
        last.then_inc(S["mod1_T"], 1)
        h_cols(0)

        def raw_ready(q):
            pe.wait_ge(raw_full[q % N_RAW], raw_count[q])

        pe.wait_ge(S["xn_evac"], KD)
        for half in range(2):
            raw_ready(half)
            wu = kview(raw[:, half, :], KD)
            for k in range(KD):
                pe.wait_ge(S["h_ready"], 2 * k + 2)
                for m in range(4):
                    last = mm(bank[2 * half + m // 2][:, 256 * (m % 2):256 * (m % 2) + 256], hT[:, k, 2 * m:2 * m + 2, :, :].rearrange("p j s c -> p (j s c)"),
                              wu[:, k, :], start=k == 0 and m % 2 == 0, stop=k == KD - 1, skip_group_check=True)
            last.then_inc(S["u_mm"], 1)
            for c in ((1, 2, 3), (4, 5, 6, 7))[half]:
                h_cols(c)

        tile = [0]

        def open_tile():
            n = tile[0]
            tile[0] += 1
            if n < 4:
                pe.wait_ge(S["u_rows"], 8 if n < 2 else 16)
            else:
                pe.wait_ge(*evac_count(n - 4))
            return bank[n % 4][:, 0:NT]

        def native(q, f, k_n, rhs):
            raw_ready(q)
            wv, o = kview(raw[:, q % N_RAW, :], k_n), open_tile()
            for k in range(k_n):
                last = mm(o, wv[:, k, f * P:(f + 1) * P], rhs[:, k], start=k == 0, stop=k == k_n - 1)
            last.then_inc(S["mm_done"], 1)

        def ssm_pair(i):
            if i < 8:
                for n in (2 * i, 2 * i + 1):
                    pe.wait_ge(S["b_ready"], n + 1)
                    if n >= 2:
                        pe.wait_ge(S["b_Tevac"], n - 1)
                    for g in range(4):
                        last = nc.tensor.transpose(bank[5 + n % 2][:, g * P:(g + 1) * P], b_half[:, n % 2, g * P:(g + 1) * P],
                                                   ident[:, :])
                    last.then_inc(S["b_Tmm"], 1)
            if i >= 1:
                for n in (2 * i - 2, 2 * i - 1):
                    pe.wait_ge(S["b_Tevac"], n + 1)
                    if n >= 2:
                        pe.wait_ge(S["x_evac"], n - 1)
                    if n % 2 == 0:
                        pe.wait_ge(S["piece_used_dve"], 32)
                        for c in range(2 * n, 2 * n + 4):
                            last = mm(bank[4][:, 256 + c:257 + c], mod_acc[:, c * P:(c + 1) * P], ones[:, 0:1],
                                      start=True, stop=True)
                        if n == 14:
                            last.then_inc(S["mod2_mm"], 1)
                    for g in range(4):
                        dg = 4 * n + g
                        cols = u_pack[:, dg % NG, :].rearrange("p (s c) -> p s c", s=2)
                        if dg >= NG:
                            cols = cols[:, :, ::-1]
                        last = mm(bank[(4, 7)[n % 2]][:, g * 64:(g + 1) * 64], b_T[:, n % 4, g * P:(g + 1) * P], cols,
                                  start=True, stop=True)
                    last.then_inc(S["x_mm"], 1)

        pe.wait_ge(S["h_evac"], 16)
        h_lat = hT[:, :, :, 0, :].rearrange("p k j c -> p k c j")
        for n in range(T_OA):
            native(U0_GC + n // 2, n % 2, KD, h_lat)
            if n == 1:
                pe.wait_ge(S["u_rows"], 16)
                for r in range(4):
                    if r >= 2:
                        pe.wait_ge(S["u_packed"], r - 1)
                    for g in range(8):
                        last = nc.tensor.transpose(bank[(4, 7)[r % 2]][:, g * 64:(g + 1) * 64],
                                                   v_rows[:, 8 * r + g, :, :].rearrange("c j h -> c (j h)"),
                                                   ident[0:64, 0:64])
                    last.then_inc(S["u_T"], 1)
                pe.wait_ge(S["u_packed"], 4)
            if 1 <= n <= 9:
                ssm_pair(n - 1)
        pe.wait_ge(*evac_count(T_OA - 1))
        for n in range(KD):
            native(U0_OA + n // 4, n % 4, KC, gbv)

        def ssm_output():
            pe.wait_ge(S["mod2_ready"], 1)
            pe.wait_ge(S["scan_done"], 1)
            pe.wait_ge(S["rev_ready"], 1)
            pe.wait_ge(toep_s, 16 * CH)
            for g in range(NG):
                gq, gr = g // 8, g % 8
                o = bank[5 + gr // 4][NC * gq:NC * gq + NC, (gr % 4) * P:(gr % 4 + 1) * P]
                mm(o, u_pack[:, g, 0:NC], toep[:, g, :], start=True, stop=False)
                mm(o, p_st[:, g, :], c_pow[:, g, :], start=False, stop=False)
                last = mm(o, p_rev[:, g, :], c_pow[:, NG + g, :], start=False, stop=True)
            last.then_inc(S["y_mm"], 1)

        def ssm_output_T():
            pe.wait_ge(S["y_evac"], 2)
            for i in range(CH):
                last = nc.tensor.transpose(bank[(4, 7)[i // 4]][:, (i % 4) * P:(i % 4 + 1) * P],
                                           y_rows[:, i, :, :].rearrange("p g h -> p (g h)"), ident[:, :])
            last.then_inc(S["s_T"], 1)

        for n in range(2 * KD):
            if n == Y_AT:
                ssm_output()
            if n == S_AT:
                ssm_output_T()
            native(U0_GATE + n // 2, n % 2, KD, h_lat)

        def three(o, wh, wl, xh, xl, first, final):
            mm(o, wh, xh, start=first, stop=False, skip_group_check=True)
            mm(o, wh, xl, start=False, stop=False, skip_group_check=True)
            return mm(o, wl, xh, start=False, stop=final, skip_group_check=True)

        def split_tile(slot, half, f, k_n, x_hi, x_lo):
            o = open_tile()
            wh, wl = (half_of(x, slot, half, k_n)[:, :, f * P:(f + 1) * P] for x in (w_hi, w_lo))
            for k in range(k_n):
                last = three(o, wh[:, k, :], wl[:, k, :], x_hi[:, k, :], x_lo[:, k, :], k == 0, k == k_n - 1)
            last.then_inc(S["mm_done"], 1)

        pe.wait_ge(S["s_ready"], 1)
        for q in range(4):
            for half in range(2):
                pe.wait_ge(S["lo_done"], 2 * q + half + 1)
                for f in range(2):
                    split_tile((n_native + q) % N_RAW, half, f, KC, s_hi, s_lo)
            if q == 0:
                pe.wait_ge(xtok2_s, 16)
            if q >= 2:
                pe.wait_ge(S["xT_evac"], q - 1)
            for k in range(2):
                for tt in range(2):
                    last = nc.tensor.transpose(bank[6 - q % 2][:, k * NT + tt * P:k * NT + (tt + 1) * P],
                                               xtok2[:, tt, (2 * q + k) * P:(2 * q + k + 1) * P], ident[:, :])
            last.then_inc(S["xT_mm"], 1)
        def sum_squares(f):
            pe.wait_ge(S["sq_ready"], f + 1)
            mm(bank[4][:, 0:NT], ones[:, :], sq[:, f % 2, :], start=f == 0, stop=f == KD - 1).then_inc(S["ss_mm"], 1)

        o4 = [open_tile() for f in range(4)]
        for k0, k1 in ((0, 6), (6, KD)):
            for f in range(4):
                pe.wait_ge(S["lo_done"], 8 + f + 1)
                wh, wl = (half_of(x, (n_native + 4 + f // 2) % N_RAW, f % 2, KD) for x in (w_hi, w_lo))
                for k in range(k0, k1):
                    if f == 0:
                        pe.wait_ge(S["m_ready"], k + 1)
                    last = three(o4[f], wh[:, k, :], wl[:, k, :], m_hi[:, k, :], m_lo[:, k, :], k == 0, k == KD - 1)
                if k1 == KD:
                    last.then_inc(S["mm_done"], 1)
        sum_squares(0)
        sum_squares(1)
        for f in range(4, KD):
            pe.wait_ge(S["lo_done"], 8 + f + 1)
            split_tile((n_native + 4 + f // 2) % N_RAW, f % 2, 0, KD, m_hi, m_lo)
            sum_squares(f - 2)
        sum_squares(KD - 2)
        sum_squares(KD - 1)
        pe.wait_ge(S["sqrt2_done"], 1)
        pe.wait_ge(S["xT_evac"], 4)
        pe.wait_ge(S["zrow_ready"], 1)
        for b in range(4, 8):
            mm(bank[b][:, :], zrow[:, 0:P], zrow[:, P:], start=True, stop=False, skip_group_check=True)

        def ffn_up(k_ready, done):
            for j in range(2):
                for f in range(2):
                    done(j, f)
                    wh, wl = (half_of(x, ffn_slot[j], f, KD) for x in (w_hi, w_lo))
                    for k in range(KD):
                        if k_ready and j == f == 0:
                            pe.wait_ge(S["h2_ready"], k + 1)
                        last = three(bank[2 * j + f][:, 0:NT], wh[:, k, :], wl[:, k, :], h2_hi[:, k, :], h2_lo[:, k, :],
                                     k == 0, k == KD - 1)
                    last.then_inc(S[("gate_mm", "up_mm")[j]], 1)

        def out_parts(f, e):
            return (x[ffn_slot[2]][:, f * HALF + e * P:f * HALF + (e + 1) * P] for x in (w_hi, w_lo))

        def acc(e):
            return bank[4 + e // 2][:, (e % 2) * NT:(e % 2 + 1) * NT]

        def first_waits(j, f):
            pe.wait_ge(S["lo_done"], split0 + 2 * j + f + 1)
            pe.wait_ge(*evac_count(T_WO + 4 + 2 * j + f))

        ffn_up(True, first_waits)
        with pe.Fori(1, n_turn) as turn:
            def waits(j, f):
                pe.wait_ge(S["lo_done"], turn * 6 + (split1 - 6 + 2 * j + f + 1))
                pe.wait_ge(S[("silu_done", "prod_done")[j]], turn * 2 + (f - 1))
            ffn_up(False, waits)
            for f in range(2):
                pe.wait_ge(S["act_ready"], turn * 2 + (f - 1))
                pe.wait_ge(S["lo_done"], turn * 6 + (split1 - 6 + 4 + f + 1))
                for e in range(KD):
                    wh, wl = out_parts(f, e)
                    last = three(acc(e), wh, wl, a_hi[:, f, :], a_lo[:, f, :], False, False)
                last.then_inc(S["fo_used"], 1)
        pe.wait_ge(S["act_ready"], 2 * n_turn)
        pe.wait_ge(S["lo_done"], split1 + 6 * (n_turn - 1) + 2)

        def fin_T(f):
            pe.wait_ge(S["xg_ready"], f + 1)
            for tt in range(2):
                last = nc.tensor.transpose(bank[2 * tt + f // 4][:, (f % 4) * P:(f % 4 + 1) * P],
                                           x1g[:, f, tt * P:(tt + 1) * P], ident[:, :])
            last.then_inc(S["fin_T"], 1)

        def fin_squares(f):
            pe.wait_ge(S["sqf_ready"], f + 1)
            if f == 0:
                pe.wait_ge(S["x2_ready"], 2)
            for tt in range(2):
                last = mm(bank[4][:, tt:tt + 1], sq[:, f % 2, tt * P:(tt + 1) * P], ones[:, 0:1],
                          start=f == 0 and tt == 0, stop=f == KD - 1, skip_group_check=True)
            last.then_inc(S["ssf_mm"], 1)

        for e in range(KD):
            for f in range(2):
                wh, wl = out_parts(f, e)
                last = three(acc(e), wh, wl, a_hi[:, f, :], a_lo[:, f, :], False, f == 1)
            last.then_inc(S["x2_mm"], 1)
            if e >= 3:
                fin_T(e - 3)
                fin_squares(e - 3)
        for f in range(KD - 3, KD):
            fin_T(f)
            fin_squares(f)


def kernel(**inputs):
    import numpy as np
    import concourse.bacc as bacc
    from concourse.bass_utils import run_bass_kernel_spmd

    a = {k: np.asarray(v) for k, v in inputs.items()}
    sg = {k: a[k][0] for k in ("w_mod", "w_in", "w_out_a", "w_glu", "w_o", "w_ff_in", "w_ff_out")}
    b_in = a["b_in"][0].reshape(-1, P)
    vec_rows = np.concatenate([a["b_mod"][0].reshape(-1, P), b_in[:C_U // P], b_in[C_U // P + KC:],
                               a["b_glu"][0].reshape(-1, P), a["norm1_g"][0].reshape(-1, P),
                               a["norm2_g"][0].reshape(-1, P), a["final_g"].reshape(-1, P),
                               a["conv_w"][0].reshape(-1, P)])

    def rows(z):
        z = z.reshape(DG, NS).T
        return np.concatenate([z, z])

    def b_rows(re, im):
        re, im = (z.reshape(DG, NS, H).transpose(1, 0, 2) for z in (re, im))
        return np.stack([np.concatenate([re, im]), np.concatenate([im, re])], axis=1)

    log_dt = np.repeat(a["log_dt"][0].reshape(1, DG), P, axis=0)
    ins = {
        "x": a["x"][0], "ctx": a["ctx"][0], **sg, "vec_rows": vec_rows,
        "c_rows": np.concatenate([a["c"].reshape(KD, P), a["c_ctx"].reshape(KD, P)]),
        "lam_pack": np.stack([rows(a["lam_re"][0]), rows(a["lam_im"][0]), log_dt], axis=1),
        "b_pack": b_rows(a["b_re"][0], a["b_im"][0]),
        "c_pack": b_rows(a["c_re"][0].transpose(0, 1, 3, 2), a["c_im"][0].transpose(0, 1, 3, 2)),
        "bu_pack": np.tile(a["b_in"][0][C_U:C_U + DC].reshape(NG, H).T, (CH, 1)),
        "d_pack": a["d_skip"][0].reshape(NG, H).T,
    }
    nc = bacc.Bacc("TRN2", target_bir_lowering=False, num_devices=1)
    arrays, t = {}, {}
    for name, z in ins.items():
        z = np.ascontiguousarray(z)
        arrays[f"in_{name}"] = z
        t[name] = nc.dram_tensor(f"in_{name}", z.shape, mybir.dt.from_np(z.dtype), kind="ExternalInput").ap()
    out = nc.dram_tensor("out", (NT, D), F32, kind="ExternalOutput").ap()
    with ExitStack() as ctx:
        build(nc, t, out, ctx)
    r = run_bass_kernel_spmd(nc, [arrays], core_ids=[0])
    return r.results[0]["out"].reshape(1, NT, D)
```

```python
from contextlib import ExitStack

import concourse.bass as bass
from concourse import mybir

ACT = mybir.ActivationFunctionType
ALU = mybir.AluOpType
F32 = mybir.dt.float32
F32R = mybir.dt.float32r

P = 128
D = 1024
KD = D // P
NT = 256
DC = D // 2
KC = DC // P
DFF = 2816
KF = DFF // P
GRID_W = 64
H = 16
NG = DC // H
NS = 64
DG = 2 * NG
CH = 8
NC = NT // CH
EPS = 1e-6
PI = 3.141592653589793
TWO_PI_HI, TWO_PI_MID = 6.28125, 0.0019350051879882812
TWO_PI_LO = 2 * PI - TWO_PI_HI - TWO_PI_MID
PI_BELOW = 3.1415925
ROUND = 1.5 * 2.0 ** 23

V_BMOD, V_BIN, V_BGLU, V_N1, V_N2, V_FG, V_CONV = 0, 48, 76, 92, 100, 108, 116
C_GB, C_GC, C_XIN, C_U, C_GA, C_GATEB = 0, DC, 2 * DC, 3 * DC, 4 * DC, 4 * DC + D

N_RAW = 3
UNIT = 2048
HALF = UNIT // 2
N_PIECE = 4

def build(nc, t, out, ctx):
    base = -(-nc.sbuf_base // 64) * 64

    def at(name, kb, shape, dt=F32):
        return nc.alloc_sbuf_tensor_at(name, shape, dt, offset=base + int(kb * 1024))

    raw = at("raw", 0, [P, N_RAW, UNIT])
    w_hi = [at(f"w_hi{i}", 24 + 16 * i, [P, UNIT], F32R) for i in range(N_RAW)]
    w_lo = [at(f"w_lo{i}", 32 + 16 * i, [P, UNIT], F32R) for i in range(N_RAW)]
    hT = at("hT", 24, [P, KD, CH, 2, NC])
    xnT = at("xnT", 40, [P, KD, 2 * NT])
    xtok = at("xtok", 24, [P, 4, D])
    b_half = at("b_half", 40, [P, 2, 512])
    b_T = at("b_T", 44, [P, 4, 512])
    gbv = at("gbv", 52, [P, KC, NT])
    mod_acc = at("mod_acc", 56, [P, 3 * D])
    rows_in = at("rows_in", 72, [P, P])
    crow_in = at("crow_in", 72.5, [16, P])
    c_pow = at("c_pow", 72, [P, DG, CH * H])
    xT = at("xT", 72, [P, KD, NT])
    xtok2 = at("xtok2", 80, [P, 2, D])
    x1T = at("x1T", 88, [P, KD, NT])
    x1g = at("x1g", 96, [P, KD, NT])
    sq_junk = at("sq_junk", 106, [P, D])
    v_rows = at("v_rows", 104, [2 * NC, NG, CH, H])
    X = at("X", 104, [P, DG, 2 * NC])
    p_rev = at("p_rev", 116, [P, NG, NC])
    m_hi = at("m_hi", 104, [P, KD, NT], F32R)
    m_lo = at("m_lo", 112, [P, KD, NT], F32R)
    u_pack = at("u_pack", 120, [P, NG, 2 * NC])
    mod_rows = at("mod_rows", 120, [2, 2 * D])
    r_rows = at("r_rows", 128, [H, 2, 8, 256])
    p_st = at("p_st", 128, [P, DG, NC])
    toep = at("toep", 136, [P, NG, CH * H])
    acc_g2 = at("acc_g2", 140, [P, D])
    h2_hi = at("h2_hi", 136, [P, KD, NT], F32R)
    h2_lo = at("h2_lo", 144, [P, KD, NT], F32R)
    piece = at("piece", 152, [P, N_PIECE, D])
    par_b = at("par_b", 168, [P, 2, DG, H])
    par_c = at("par_c", 176, [P, 2, DG, H])
    h_hi = at("h_hi", 152, [P, KD, NT], F32R)
    h_lo = at("h_lo", 160, [P, KD, NT], F32R)
    ya = at("ya", 168, [P, KD, NT])
    sgb = at("sgb", 176, [P, KD, NT])
    a_hi = at("a_hi", 168, [P, 4, NT], F32R)
    a_lo = at("a_lo", 172, [P, 4, NT], F32R)
    silu_g = at("silu_g", 176, [P, 2, NT])
    gu = at("gu", 178, [P, 2, NT])
    e_re = at("e_re", 184, [P, 9, DG])
    e_im = at("e_im", 186.25, [P, 9, DG])
    tc = at("tc", 188.5, [P, 2, DG, CH])
    s_hi = at("s_hi", 184, [P, KC, NT], F32R)
    s_lo = at("s_lo", 188, [P, KC, NT], F32R)
    fin = at("fin", 184, [P, 2, D])
    sm = at("sm", 192.5, [P, 16, DG])
    tA = at("tA", 197, [P, 512])
    tB = at("tB", 199, [P, 512])
    s32 = at("s32", 197, [P, KC, NT])
    zeros = at("zeros", 180, [1, 512])
    zrow = at("zrow", 182, [1, 512], F32R)
    mrg = at("mrg", 192.5, [P, 2, NT])
    yb = at("yb", 194.5, [P, 2, NT])
    sq = at("sq", 201, [P, 4, NT])
    bc = at("bc", 199, [P, 2, NT])
    gv = at("gv", 201, [P, 2, NT])
    cv = at("cv", 203, [P, 2, NT])
    y_rows = at("y_rows", 197, [P, CH, 8, H])
    sg = at("sg", 201, [P, 2, NT])
    end = [205.0]

    def small(name, cols, rows=P):
        end[0] += -(-cols // 8) * 8 / 256
        return at(name, end[0] - -(-cols // 8) * 8 / 256, [rows, cols])

    ident, ones, vecT = small("ident", P), small("ones", P), small("vecT", P)
    csil, bu, d_skip = small("csil", 16), small("bu", NG), small("d_skip", NG, H)
    warm, sgn, halfpi, epsc = small("warm", 1), small("sgn", 1), small("halfpi", 1), small("epsc", 1)
    ssum, srow, rstd = small("ssum", 4), small("srow", 4), small("rstd", 4)
    mod1, gs1, mod2, gs2 = small("mod1", 32), small("gs1", 16), small("mod2", 32), small("gs2", 8)
    d_diag = at("d_diag", 196.5, [H, 8, H])
    assert end[0] <= 207.7, end[0]

    bank = [ctx.enter_context(nc.psum_tensor(f"bank{i}", [P, 512], F32)) for i in range(8)]
    r_dram = nc.dram_tensor("r_scratch", (NG, H, 240), F32, kind="Internal").ap()

    def sem(name):
        return ctx.enter_context(nc.semaphore(name))

    rows_in_s, lam_s, par_c_s, par_b_s, x_s, ctx_s, pack_s, xtok2_s, out_s, toep_s = (sem(n) for n in (
        "rows_loaded", "lam_loaded", "par_c_loaded", "par_b_loaded", "x_loaded", "ctx_loaded", "packs_loaded",
        "xtok2_loaded", "out_stored", "toep_loaded"))
    r_out_s = [sem(f"r_rows_stored{i}") for i in range(2)]
    raw_full = [sem(f"raw_full{i}") for i in range(N_RAW)]
    piece_full = [sem(f"piece_full{i}") for i in range(N_PIECE)]
    piece2_full = [sem(f"piece2_full{i}") for i in range(N_PIECE)]
    S = {n: sem(n) for n in (
        "mod_rows_ready mod1_T zeroed consts dt_ready lamdt_ready mag_ready trig_arg sin_done dve_step powers_ready "
        "rows_T csil_ready vec_ready sums_done sqrt_done rstd_ready x_scaled h_hi_ready h_lo_ready xn_mm xn_evac gs_ready h_ready "
        "piece_used_pe piece_used_dve acc_ready mod2_mm mod2_ready g2_mm g2_ready "
        "cpow_ready h_mm h_evac r_added u_mm u_rows u_T u_packed b_ready b_Tmm b_Tevac x_mm x_evac back_done rev_ready scan_done "
        "raw_used mm_done evac_act evac_dve ya_scaled y_mm y_evac s_T s_gelu s_hi_done s_ready "
        "hi_done lo_done sg_ready mrg_ready mul_done m_hi_done m_ready xT_mm xT_evac "
        "sq_ready ss_mm sqrt2_done t2_ready h2_hi_done h2_ready zeros_ready zrow_ready "
        "gate_mm up_mm silu_done prod_done a_hi_done act_ready fo_used x2_mm x2_ready sqf_ready xg_ready ssf_mm "
        "fin_T sqrt3_done rstd3_done fin_act fin_dve").split()}

    w_in, w_oa, w_glu, w_o, w_fi, w_fo = (t[n] for n in ("w_in", "w_out_a", "w_glu", "w_o", "w_ff_in", "w_ff_out"))

    def rows_of(w, col, n):
        return w[:, col:col + n].rearrange("(k p) n -> p k n", p=P)

    units = [(KD, [(0, 256, rows_of(w_in, C_U + 256 * q, 256))]) for q in range(2)]
    for q in range(2):
        units += [(KD, [(0, 256, rows_of(w_in, c + 256 * q, 256))]) for c in (C_GC, C_XIN, C_GB)]
    units += [(KC, [(0, 512, rows_of(w_oa, 512 * q, 512))]) for q in range(2)]
    units += [(KD, [(0, 256, rows_of(w_in, C_GA + 256 * q, 256))]) for q in range(8)]
    n_native = len(units) - 5
    units += [(KC, [(256 * j, 256, rows_of(w_glu, c + 256 * q, 256)) for j, c in enumerate((D, 0))]) for q in range(4)]
    units += [(KD, [(0, 256, rows_of(w_o, 256 * q, 256))]) for q in range(4)]
    n_pre = len(units)
    n_turn = KF // 2
    U0_GC, U0_OA, U0_GATE, U0_GLU, U0_WO = 2, 8, 10, 18, 22
    F_SPLIT = 2 * (n_native - U0_GATE)
    G0 = 2 * KD - F_SPLIT
    split0 = 2 * (n_pre - n_native)
    split1 = split0 + 4
    ffn_slot = [(n_pre + j) % N_RAW for j in range(3)]
    loads, raw_count = [0] * N_RAW, []
    for q, (_, parts) in enumerate(units):
        loads[q % N_RAW] += 16 * len(parts)
        raw_count.append(loads[q % N_RAW])
    ffn_raw0 = list(loads)

    raw_slot = [raw[:, i, :] for i in range(N_RAW)]

    def kview(ap, k):
        return ap.rearrange("p (k n) -> p k n", k=k)

    def half_of(buf, slot, half, k):
        n = UNIT // k // 2
        return kview(buf[slot][:, :], k)[:, :, half * n:half * n + n]

    conv_tiles = ["act", "act", "dve", "dve", "dve", "dve"] * 2
    evac_by = conv_tiles + ["act"] * 8 + ["act"] * 16 + ["act", "act", "dve", "dve"] * 4 + ["dve"] * 8
    T_OA, T_GATE, T_GLU, T_WO = 12, 20, 36, 52
    Y_AT, S_AT = 6, 8

    def evac_count(tile):
        by = evac_by[tile]
        return S["evac_" + by], evac_by[:tile + 1].count(by)

    def bias_of(col):
        c = V_BIN + (col // P if col < C_U else col // P - KC)
        return vecT[:, c:c + 1]

    def half_used(n):
        if n < G0:
            return T_GATE + F_SPLIT + n + 1
        n -= G0
        return T_GLU + 2 * n + 2 if n < 8 else T_WO + n - 8 + 1

    def h_banks(c):
        return (4, 7) if c % 2 else (5, 6)

    def mod_rest(m):
        return (m // 3, m % 3) if m < 24 else (m - 24, 3)

    def cut_of(n):
        q = n_native + n // 2
        return units[q][0] if q < n_pre else (KD, KD, 2)[q - n_pre]

    def unit_used(q):
        if q < U0_GC:
            return S["u_mm"], q + 1
        if q < U0_OA:
            return S["mm_done"], 2 * (q - U0_GC) + 2
        if q < U0_GATE:
            return S["mm_done"], T_OA + 4 * (q - U0_OA) + 4
        return S["mm_done"], T_GATE + 2 * (q - U0_GATE) + 2

    block = ctx.enter_context(nc.Block())

    @block.sync
    def _(sp):
        sp.dma_start(crow_in[:, :], t["c_rows"]).then_inc(rows_in_s, 16)
        sp.dma_start(rows_in[:, :], t["vec_rows"]).then_inc(rows_in_s, 16)
        sp.dma_start(sm[:, 0:3, :], t["lam_pack"]).then_inc(lam_s, 16)

        def load_unit(q):
            slot, (k, parts) = q % N_RAW, units[q]
            old = q - N_RAW
            if old >= 0 and old < n_native:
                sp.wait_ge(*unit_used(old))
            elif old >= 0:
                sp.wait_ge(S["lo_done"], 2 * (old - n_native) + 2)
            for c0, n, src in parts:
                sp.dma_start(kview(raw[:, slot, :], k)[:, :, c0:c0 + n], src).then_inc(raw_full[slot], 16)

        for n in range(16):
            if n >= N_PIECE:
                sp.wait_ge(S["piece_used_pe"], n - N_PIECE + 1)
            sp.dma_start(piece[:, n % N_PIECE, :], t["w_mod"][(n // 2) * P:(n // 2 + 1) * P, (n % 2) * D:(n % 2 + 1) * D]
                         ).then_inc(piece_full[n % N_PIECE], 16)
            if n == 2:
                sp.dma_start(xtok[:, 0:2, :], t["x"].rearrange("(a p) d -> p a d", p=P)).then_inc(x_s, 16)
                sp.dma_start(xtok[:, 2:4, :], t["ctx"].rearrange("(a p) d -> p a d", p=P)).then_inc(ctx_s, 16)
            if n == 6:
                sp.dma_start(par_c[:, :, :, :], t["c_pack"]).then_inc(par_c_s, 16)
        sp.dma_start(par_b[:, :, :, :], t["b_pack"]).then_inc(par_b_s, 16)
        load_unit(0)
        sp.dma_start(bu[:, :], t["bu_pack"]).then_inc(pack_s, 16)
        sp.dma_start(d_skip[:, :], t["d_pack"]).then_inc(pack_s, 16)
        for q in range(1, n_pre):
            load_unit(q)
            if q == U0_OA:
                sp.wait_ge(r_out_s[0], 32)
                sp.wait_ge(r_out_s[1], 32)
                for j in range(CH):
                    sp.dma_start(toep[H * j:H * j + H, :, :],
                                 r_dram[:, :, (CH - 1 - j) * H:(CH - 1 - j) * H + CH * H].rearrange("g h n -> h g n")
                                 ).then_inc(toep_s, 16)
            if q == U0_GLU:
                sp.wait_ge(S["y_mm"], 1)
                sp.dma_start(xtok2[:, :, :], t["x"].rearrange("(a p) d -> p a d", p=P)).then_inc(xtok2_s, 16)
        def load_ffn(j, turn, slot):
            if j < 2:
                src = w_fi[:, bass.ds(turn * 256 + j * DFF, 256)].rearrange("(k p) n -> p k n", p=P)
                sp.dma_start(kview(raw[:, slot, :], KD), src).then_inc(raw_full[slot], 16)
            else:
                src = w_fo[bass.ds(turn * 256, 256), :].rearrange("(k p) n -> p k n", p=P)
                sp.dma_start(kview(raw[:, slot, :], 2), src).then_inc(raw_full[slot], 16)

        for j in range(3):
            sp.wait_ge(S["lo_done"], split0 - 6 + 2 * j + 2)
            load_ffn(j, 0, ffn_slot[j])
        for j in range(2):
            sp.wait_ge(S["lo_done"], split0 + 2 * j + 2)
            load_ffn(j, 1, ffn_slot[j])
        with sp.Fori(1, n_turn - 1) as turn:
            for j in range(3):
                sp.wait_ge(S["lo_done"], turn * 6 + (split1 - 6 + 2 * j + 2))
                load_ffn(j, turn + 1 if j < 2 else turn, ffn_slot[j])
        sp.wait_ge(S["lo_done"], split1 + 6 * (n_turn - 1) - 4)
        load_ffn(2, n_turn - 1, ffn_slot[0])
        for tt in range(2):
            sp.wait_ge(S["fin_act"], tt + 1)
            sp.wait_ge(S["fin_dve"], tt + 1)
            sp.dma_start(out[tt * P:(tt + 1) * P, :], fin[:, tt, :]).then_inc(out_s, 16)
        sp.wait_ge(out_s, 32)

    @block.gpsimd
    def _(pool):
        g = nc.gpsimd
        g.memset(ident[:, :], 0.0).then_inc(S["zeroed"], 1)
        pool.wait_ge(S["zeroed"], 1)
        g.affine_select(out=ident[:, :], in_=ident[:, :], compare_op=ALU.not_equal, fill=1.0, base=0,
                        pattern=[[-1, P]], channel_multiplier=1).then_inc(S["consts"], 1)
        for i, (buf, rows, value) in enumerate(((ones, slice(0, P), 1.0), (halfpi, slice(0, P), PI / 2),
                                 (epsc, slice(0, P), EPS), (sgn, slice(0, NS), 1.0), (sgn, slice(NS, P), -1.0))):
            pool.wait_ge(S["consts"], i + 1)
            g.memset(buf[rows, :], value).then_inc(S["consts"], 1)

        def mod_piece(m):
            n, (k, c) = 16 + m, mod_rest(m)
            if m < N_PIECE:
                pool.wait_ge(S["piece_used_pe"], n - N_PIECE + 1)
            elif 24 <= m < 24 + N_PIECE:
                pool.wait_ge(S["mm_done"], T_GLU)
            else:
                pool.wait_ge(S["piece_used_dve"], m - N_PIECE + 1)
            pool.dma_start(piece[:, n % N_PIECE, :], t["w_mod"][k * P:(k + 1) * P, (2 + c) * D:(3 + c) * D]
                           ).then_inc(piece2_full[n % N_PIECE], 16)

        for m in range(24):
            mod_piece(m)
        for f in range(KD):
            pool.wait_ge(S["evac_act"], evac_count(T_GATE + f)[1])
            g.tensor_tensor(ya[:, f, :], ya[:, f, :], gv[:, f % 2, :], ALU.mult).then_inc(S["ya_scaled"], 1)
        pool.wait_ge(S["evac_act"], evac_count(T_GATE + 15)[1])
        pool.wait_ge(S["ya_scaled"], KD)
        pool.wait_ge(S["scan_done"], 1)
        for m in range(24, 28):
            mod_piece(m)
        for f in range(KD):
            pool.wait_ge(*evac_count(T_GLU + 4 * (f // 2) + 2 + f % 2))
            if f >= 2:
                pool.wait_ge(S["m_ready"], f - 1)
            if f == 4 or f == 6:
                mod_piece(26 + f // 2)
            g.tensor_tensor(mrg[:, f % 2, :], yb[:, f % 2, :], sgb[:, f, :], ALU.mult).then_inc(S["mul_done"], 1)
            pool.wait_ge(S["mul_done"], f + 1)
            g.tensor_tensor(mrg[:, f % 2, :], mrg[:, f % 2, :], ya[:, f, :], ALU.add).then_inc(S["mrg_ready"], 1)
        mod_piece(30)
        mod_piece(31)
        pool.wait_ge(S["mrg_ready"], KD)
        g.memset(zeros[:, :], 0.0).then_inc(S["zeros_ready"], 1)

    n_const = 6
    LR, LI, LD, DT, MAG, SN, CS, DEN, NR, FR, FI, T0, T1, T2, T3, T4, T5, T6 = range(18)
    AR = [LR, LI, LD, DT, MAG]
    QI = [SN, CS, DEN, NR, FR]

    @block.scalar
    def _(act):
        A, copy = nc.scalar.activation, nc.scalar.copy

        act.wait_ge(lam_s, 16)
        A(sm[:, DT, :], sm[:, LD, :], ACT.Exp).then_inc(S["dt_ready"], 1)
        act.wait_ge(S["rows_T"], 2)
        A(csil[:, :], bank[7][:, P:P + 16], ACT.Silu).then_inc(S["csil_ready"], 1)
        copy(vecT[:, :], bank[7][:, 0:P]).then_inc(S["vec_ready"], 1)
        act.wait_ge(S["lamdt_ready"], 1)
        A(sm[:, MAG, :], sm[:, T0, :], ACT.Exp).then_inc(S["mag_ready"], 1)
        act.wait_ge(S["consts"], n_const)
        act.wait_ge(S["trig_arg"], 1)
        A(sm[:, SN, :], sm[:, T1, :], ACT.Sin).then_inc(S["sin_done"], 1)
        A(sm[:, CS, :], sm[:, T2, :], ACT.Sin, bias=halfpi[:, 0:1], scale=-1.0).then_inc(S["sin_done"], 1)
        act.wait_ge(x_s, 16)
        for tt in range(4):
            if tt == 2:
                act.wait_ge(ctx_s, 16)
            if tt:
                act.wait_ge(S["sums_done"], tt)
            A(sq_junk[:, :], xtok[:, tt, :], ACT.Square, accum_out=ssum[:, tt:tt + 1]).then_inc(S["sums_done"], 1)
        act.wait_ge(S["sums_done"], 4)
        A(srow[:, :], ssum[:, :], ACT.Sqrt, bias=epsc[:, 0:1], scale=1.0 / D).then_inc(S["sqrt_done"], 1)
        act.wait_ge(S["rstd_ready"], 1)
        for tt in range(4):
            A(xtok[:, tt, :], xtok[:, tt, :], ACT.Copy, scale=rstd[:, tt:tt + 1]).then_inc(S["x_scaled"], 1)
        for k in range(KD):
            act.wait_ge(S["xn_mm"], k + 1)
            copy(xnT[:, k, :], bank[k % 4][:, :]).then_inc(S["xn_evac"], 1)

        def h_rows(c):
            act.wait_ge(S["h_mm"], c + 1)
            if c % 2 == 0 and c >= 4:
                act.wait_ge(r_out_s[c // 2 % 2], 16)
            for b in range(2):
                src = bank[h_banks(c)[b]][0:H, :].rearrange("h (g n) -> h g n", g=4)
                dst = r_rows[:, c // 2 % 2, 4 * b:4 * b + 4, :]
                if c % 2 == 0:
                    copy(dst[:, :, 128:256], src).then_inc(S["h_evac"], 1)
                else:
                    copy(dst[:, :, 16:128], src[:, :, 0:112])
                    copy(dst[:, :, 0:16], src[:, :, 112:128]).then_inc(S["h_evac"], 1)
            if c % 2:
                act.wait_ge(S["r_added"], c // 2 + 1)
                act.dma_start(r_dram[8 * (c // 2):8 * (c // 2) + 8, :, :].rearrange("g h n -> h g n"),
                              r_rows[:, c // 2 % 2, :, 16:256]).then_inc(r_out_s[c // 2 % 2], 16)

        act.wait_ge(S["piece_used_pe"], 16)
        for b in range(2):
            copy(mod_rows[:, 512 * b:512 * (b + 1)], bank[4 + b][0:2, :]).then_inc(S["mod_rows_ready"], 1)
        act.wait_ge(S["gs_ready"], 1)
        act.wait_ge(S["xn_evac"], KD)
        for k in range(KD):
            for s in range(2):
                A(hT[:, k, :, s, :].rearrange("p j c -> p c j"), xnT[:, k, s * NT:(s + 1) * NT], ACT.Identity,
                  bias=mod1[:, 2 * k + s:2 * k + s + 1], scale=gs1[:, 2 * k + s:2 * k + s + 1]).then_inc(S["h_ready"], 1)
        h_rows(0)
        h_rows(1)
        for half in range(2):
            act.wait_ge(S["u_mm"], half + 1)
            for m in range(4):
                for jj in range(2):
                    copy(v_rows[:, 16 * half:16 * half + 16, 2 * m + jj, :],
                         bank[2 * half + m // 2][NS * jj:NS * jj + NS, 256 * (m % 2):256 * (m % 2) + 256]
                         .rearrange("c (g h) -> c g h", h=H)).then_inc(S["u_rows"], 1)
            for c in ((2, 3), (4, 5, 6, 7))[half]:
                h_rows(c)

        def b_T_evac(n):
            act.wait_ge(S["b_Tmm"], n + 1)
            if n >= 4:
                act.wait_ge(S["x_mm"], n - 3)
            copy(b_T[:, n % 4, :], bank[5 + n % 2][:, :]).then_inc(S["b_Tevac"], 1)

        def x_evac(n):
            act.wait_ge(S["x_mm"], n + 1)
            copy(X[:, 4 * n:4 * n + 4, :], bank[(4, 7)[n % 2]][:, 0:256].rearrange("p (g c) -> p g c", g=4)
                 ).then_inc(S["x_evac"], 1)

        def ssm_pair(i):
            if i < 8:
                b_T_evac(2 * i)
                b_T_evac(2 * i + 1)
            if i >= 1:
                x_evac(2 * i - 2)
                x_evac(2 * i - 1)

        def tile_bank(tile):
            act.wait_ge(S["mm_done"], tile + 1)
            return bank[tile % 4][:, 0:NT]

        for tile in range(T_OA):
            if 3 <= tile <= 11:
                ssm_pair(tile - 3)
            if evac_by[tile] == "act":
                q, f = tile // 6, tile % 6
                if q:
                    act.wait_ge(*evac_count(4 + f))
                A(gv[:, f, :], tile_bank(tile), ACT.Identity, bias=bias_of(C_GC + 256 * q + P * f)).then_inc(S["evac_act"], 1)
        act.wait_ge(S["b_ready"], 16)
        for f in range(KD):
            copy(ya[:, f, :], tile_bank(T_OA + f)).then_inc(S["evac_act"], 1)
        act.wait_ge(*evac_count(T_OA - 1))
        def gate_tile(f):
            if f >= KD:
                dst, c0 = sgb[:, f - KD, :], C_GATEB - D
            else:
                dst, c0 = gv[:, f % 2, :], C_GA
                if f >= 2:
                    act.wait_ge(S["ya_scaled"], f - 1)
            A(dst, tile_bank(T_GATE + f), ACT.Sigmoid, bias=bias_of(c0 + P * f)).then_inc(S["evac_act"], 1)

        def hi(n):
            q, half = n_native + n // 2, n % 2
            if q < n_pre:
                slot, k, need = q % N_RAW, units[q][0], raw_count[q]
            else:
                j = q - n_pre
                slot, k, need = ffn_slot[j], (KD, KD, 2)[j], ffn_raw0[ffn_slot[j]] + 16
            act.wait_ge(raw_full[slot], need)
            if n == 0:
                act.wait_ge(S["mm_done"], T_GATE)
            if n == 2:
                act.wait_ge(S["mod2_mm"], 1)
            if n == 4:
                act.wait_ge(S["mm_done"], T_GATE + F_SPLIT)
            if n >= 6:
                act.wait_ge(S["mm_done"], half_used(n - 6 if cut_of(n - 6) == cut_of(n) else (n - 6) | 1))
            ffn_half(slot, half, k)

        def ffn_half(slot, half, k):
            if k > 2:
                src, dst = half_of(raw_slot, slot, half, k), half_of(w_hi, slot, half, k)
            else:
                src, dst = (x[slot][:, half * HALF:(half + 1) * HALF] for x in (raw_slot, w_hi))
            copy(dst, src).then_inc(S["hi_done"], 1)

        for f in range(2 * KD):
            gate_tile(f)
            if f == 1:
                act.wait_ge(S["piece_used_dve"], 24)
                copy(h_hi[:, :, :].rearrange("p k (c j) -> p k c j", j=CH),
                     hT[:, :, :, 0, :].rearrange("p k j c -> p k c j")).then_inc(S["h_hi_ready"], 1)
            if f == Y_AT - 1:
                act.wait_ge(S["back_done"], 1)
                copy(p_rev[:, :, :], p_st[:, NG:, ::-1]).then_inc(S["rev_ready"], 1)
            if f == Y_AT:
                for b in range(2):
                    act.wait_ge(S["y_mm"], 1)
                    copy(y_rows[:, :, 4 * b:4 * b + 4, :].rearrange("p i g h -> p g i h"),
                         bank[5 + b][:, :].rearrange("p (g i h) -> p g i h", g=4, i=CH)).then_inc(S["y_evac"], 1)
            if f == S_AT:
                act.wait_ge(S["s_T"], 1)
                for b in range(2):
                    src = bank[(4, 7)[b]][:, :].rearrange("p (i g c) -> p g c i", i=4, g=KC)
                    dst = s32[:, :, :].rearrange("p g (c i) -> p g c i", i=CH)[:, :, :, 4 * b:4 * b + 4]
                    A(dst, src, ACT.Gelu_apprx_tanh).then_inc(S["s_gelu"], 1)
                act.wait_ge(S["s_gelu"], 2)
                copy(s_hi[:, :, :], s32[:, :, :]).then_inc(S["s_hi_done"], 1)
            if f >= 2:
                hi(f - 2)

        def m_hi_of(f):
            act.wait_ge(S["mrg_ready"], f + 1)
            copy(m_hi[:, f, :], mrg[:, f % 2, :]).then_inc(S["m_hi_done"], 1)

        act.wait_ge(S["ya_scaled"], KD)
        for q in range(4):
            for f in range(2):
                if q:
                    act.wait_ge(*evac_count(T_GLU + 4 * q - 2 + f))
                b = V_BGLU + KD + 2 * q + f
                A(sg[:, f, :], tile_bank(T_GLU + 4 * q + f), ACT.Sigmoid, bias=vecT[:, b:b + 1]).then_inc(S["evac_act"], 1)
            if q == 0:
                hi(G0 + 4)
                hi(G0 + 5)
            else:
                m_hi_of(2 * q - 2)
                m_hi_of(2 * q - 1)
            hi(G0 + 6 + 2 * q)
            act.wait_ge(S["xT_mm"], q + 1)
            copy(xT[:, 2 * q:2 * q + 2, :], kview(bank[6 - q % 2][:, :], 2)).then_inc(S["xT_evac"], 1)
            hi(G0 + 7 + 2 * q)
        m_hi_of(6)
        m_hi_of(7)
        A(warm[:, :], epsc[:, :], ACT.Sqrt)
        for f in range(KD):
            act.wait_ge(S["evac_dve"], evac_count(T_WO + f)[1])
            if f >= 4:
                act.wait_ge(S["ss_mm"], f - 3)
            A(sq[:, f % 4, :], x1T[:, f, :], ACT.Square).then_inc(S["sq_ready"], 1)
            if f == 2:
                act.wait_ge(S["zeros_ready"], 1)
                copy(zrow[:, :], zeros[:, :]).then_inc(S["zrow_ready"], 1)
            for n in {1: (14, 15), 3: (16, 17), 4: (18,), 5: (19,)}.get(f, ()):
                hi(G0 + n)
        act.wait_ge(S["ss_mm"], KD)
        A(bc[:, 0, :], bank[4][:, 0:NT], ACT.Sqrt, bias=epsc[:, 0:1], scale=1.0 / D).then_inc(S["sqrt2_done"], 1)
        for k in range(KD):
            act.wait_ge(S["t2_ready"], k + 1)
            A(h2_hi[:, k, :], x1g[:, k, :], ACT.Identity, bias=mod2[:, KD + k:KD + k + 1]).then_inc(S["h2_hi_done"], 1)

        def act_turn(turn, first=False, last=False):
            for f in range(2):
                act.wait_ge(S["gate_mm"], turn * 2 + (f + 1))
                if first:
                    act.wait_ge(S["mrg_ready"], KD)
                else:
                    act.wait_ge(S["prod_done"], turn * 2 + (f - 1))
                A(silu_g[:, f, :], bank[f][:, 0:NT], ACT.Silu).then_inc(S["silu_done"], 1)
            for j in range(2 if last else 0, 3):
                slot = ffn_slot[0 if last else j]
                act.wait_ge(raw_full[slot], turn * 16 + (ffn_raw0[slot] + (32 if j < 2 or last else 16)))
                for half in range(2):
                    if j < 2:
                        act.wait_ge(S[("gate_mm", "up_mm")[j]], turn * 2 + (half + 1))
                    elif last:
                        act.wait_ge(S["gate_mm"], turn * 2 + 2)
                    elif first:
                        act.wait_ge(S["mm_done"], T_WO + KD)
                    else:
                        act.wait_ge(S["fo_used"], turn * 2 + (half - 1))
                    ffn_half(slot, half, (KD, KD, 2)[j])

        act_turn(0, first=True)
        with act.Fori(1, n_turn - 1) as turn:
            act_turn(turn)
        act_turn(n_turn - 1, last=True)
        A(warm[:, :], epsc[:, :], ACT.Sqrt)
        for f in range(KD):
            act.wait_ge(S["x2_ready"], f + 1)
            if f >= 4:
                act.wait_ge(S["ssf_mm"], f - 3)
            A(sq[:, f % 4, :], x1T[:, f, :], ACT.Square).then_inc(S["sqf_ready"], 1)
        act.wait_ge(S["ssf_mm"], KD)
        A(srow[:, 0:2], bank[4][:, 0:2], ACT.Sqrt, bias=epsc[:, 0:1], scale=1.0 / D).then_inc(S["sqrt3_done"], 1)
        act.wait_ge(S["rstd3_done"], 1)
        act.wait_ge(S["fin_T"], KD)
        for tt in range(2):
            A(fin[:, tt, DC:D], bank[2 * tt + 1][:, :], ACT.Copy, scale=rstd[:, tt:tt + 1]).then_inc(S["fin_act"], 1)

    @block.vector
    def _(dve):
        v = nc.vector
        steps = [0]

        def step():
            steps[0] += 1
            return steps[0]

        def tt(o, a, b, op):
            return v.tensor_tensor(o, a, b, op)

        def stt(o, a, s, b, op0, op1):
            return v.scalar_tensor_tensor(out=o, in0=a, scalar=s, in1=b, op0=op0, op1=op1)

        def q(i):
            return sm[:, i, :]

        M, AD, SU = ALU.mult, ALU.add, ALU.subtract
        dve.wait_ge(S["dt_ready"], 1)
        tt(q(T0), q(LR), q(DT), M).then_inc(S["lamdt_ready"], 1)
        tt(q(T1), q(LI), q(DT), M).then_inc(S["dve_step"], 1)
        dve.wait_ge(S["dve_step"], step())
        v.tensor_scalar(q(T2), q(T1), 1.0 / (2 * PI), ROUND, M, AD).then_inc(S["dve_step"], 1)
        dve.wait_ge(S["dve_step"], step())
        v.tensor_scalar(q(T2), q(T2), ROUND, None, SU).then_inc(S["dve_step"], 1)
        dve.wait_ge(S["dve_step"], step())
        for part in (TWO_PI_HI, TWO_PI_MID, TWO_PI_LO):
            stt(q(T1), q(T2), -part, q(T1), M, AD).then_inc(S["dve_step"], 1)
            dve.wait_ge(S["dve_step"], step())
        v.tensor_scalar(q(T1), q(T1), PI_BELOW, -PI_BELOW, ALU.min, ALU.max).then_inc(S["dve_step"], 1)
        dve.wait_ge(S["dve_step"], step())
        stt(q(T2), q(T1), -1.0, q(T1), M, ALU.max).then_inc(S["trig_arg"], 1)
        tt(q(T3), q(LR), q(LR), M).then_inc(S["dve_step"], 1)
        dve.wait_ge(S["dve_step"], step())
        tt(q(T4), q(LI), q(LI), M).then_inc(S["dve_step"], 1)
        dve.wait_ge(S["dve_step"], step())
        tt(q(DEN), q(T3), q(T4), AD).then_inc(S["dve_step"], 1)
        dve.wait_ge(S["dve_step"], step())
        v.reciprocal(q(DEN), q(DEN)).then_inc(S["dve_step"], 1)
        dve.wait_ge(S["dve_step"], step())
        dve.wait_ge(S["mag_ready"], 1)
        dve.wait_ge(S["sin_done"], 2)
        dve.wait_ge(S["consts"], n_const)
        v.memset(e_re[:, 0, :], 1.0)
        v.memset(e_im[:, 0, :], 0.0)
        tt(e_re[:, 1, :], q(MAG), q(CS), M)
        tt(e_im[:, 1, :], q(MAG), q(SN), M).then_inc(S["dve_step"], 1)
        dve.wait_ge(S["dve_step"], step())
        v.tensor_scalar(q(NR), e_re[:, 1, :], -1.0, None, AD).then_inc(S["dve_step"], 1)
        dve.wait_ge(S["dve_step"], step())
        tt(q(T0), q(NR), q(LR), M)
        tt(q(T1), e_im[:, 1, :], q(LI), M)
        tt(q(T2), e_im[:, 1, :], q(LR), M)
        tt(q(T3), q(NR), q(LI), M).then_inc(S["dve_step"], 1)
        dve.wait_ge(S["dve_step"], step())
        tt(q(T0), q(T0), q(T1), AD)
        tt(q(T2), q(T2), q(T3), SU).then_inc(S["dve_step"], 1)
        dve.wait_ge(S["dve_step"], step())
        tt(q(FR), q(T0), q(DEN), M)
        tt(q(FI), q(T2), q(DEN), M).then_inc(S["dve_step"], 1)
        dve.wait_ge(S["dve_step"], step())

        def power(dst, n, by, src):
            def b(i):
                return e[i][:, by:by + 1, :].broadcast_to([P, n, DG])
            e = (e_re, e_im)
            s_re, s_im = e_re[:, src:src + n, :], e_im[:, src:src + n, :]
            t_a, t_b = (x[:, 0:n * DG].rearrange("p (n d) -> p n d", n=n) for x in (tA, tB))
            t_a2, t_b2 = (x[:, 256:256 + n * DG].rearrange("p (n d) -> p n d", n=n) for x in (tA, tB))
            tt(t_a, s_re, b(0), M)
            tt(t_b, s_im, b(1), M)
            tt(t_a2, s_re, b(1), M)
            tt(t_b2, s_im, b(0), M).then_inc(S["dve_step"], 1)
            dve.wait_ge(S["dve_step"], step())
            tt(e_re[:, dst:dst + n, :], t_a, t_b, SU)
            tt(e_im[:, dst:dst + n, :], t_a2, t_b2, AD).then_inc(S["dve_step"], 1)
            dve.wait_ge(S["dve_step"], step())

        power(2, 1, 1, 1)
        power(3, 2, 2, 1)
        power(5, 4, 4, 1)
        dve.wait_ge(S["sqrt_done"], 1)
        v.reciprocal(rstd[:, :], srow[:, :]).then_inc(S["rstd_ready"], 1)
        for d in range(2):
            dg = slice(NG * d, NG * d + NG)
            o = [tc[:, i, dg, :].rearrange("p g e -> p e g") for i in range(2)]
            src = [(x[:, 0:8, dg] if d == 0 else x[:, 7::-1, dg]) for x in (e_re, e_im)]
            f_re, f_im = (sm[:, i:i + 1, dg].broadcast_to([P, CH, NG]) for i in (FR, FI))
            t_a, t_b, = (x[:, 0:CH * NG].rearrange("p (n d) -> p n d", n=CH) for x in (tA, tB))
            t_a2, t_b2 = (x[:, 256:256 + CH * NG].rearrange("p (n d) -> p n d", n=CH) for x in (tA, tB))
            tt(t_a, src[0], f_re, M)
            tt(t_b, src[1], f_im, M)
            tt(t_a2, src[0], f_im, M)
            tt(t_b2, src[1], f_re, M).then_inc(S["dve_step"], 1)
            dve.wait_ge(S["dve_step"], step())
            tt(t_a, t_a, t_b, SU).then_inc(S["dve_step"], 1)
            dve.wait_ge(S["dve_step"], step())
            tt(t_a2, t_a2, t_b2, AD).then_inc(S["dve_step"], 1)
            dve.wait_ge(S["dve_step"], step())
            v.tensor_scalar(o[0], t_a, sgn[:, 0:1], None, M)
            v.tensor_scalar(o[1], t_a2, -1.0, None, M).then_inc(S["dve_step"], 1)
            dve.wait_ge(S["dve_step"], step())
        v.tensor_scalar(e_im[:, 1:9, :], e_im[:, 1:9, :], sgn[:, 0:1], -1.0, M, M).then_inc(S["dve_step"], 1)
        dve.wait_ge(S["dve_step"], step())

        def table(dst, par, dg, f0, f1, n_e):
            shape = [P, 4, n_e, H]
            t_a, t_b = (x[:, :].rearrange("p (g e h) -> p g e h", g=4, e=n_e) for x in (tA, tB))
            tt(t_a, par[:, 0, dg, None, :].broadcast_to(shape), f0[:, :, :, None].broadcast_to(shape), M)
            tt(t_b, par[:, 1, dg, None, :].broadcast_to(shape), f1[:, :, :, None].broadcast_to(shape), M).then_inc(S["dve_step"], 1)
            dve.wait_ge(S["dve_step"], step())
            return tt(dst, tA[:, :], tB[:, :], AD)

        dve.wait_ge(par_c_s, 16)
        dve.wait_ge(S["rows_T"], 2)

        def c_half(n):
            c, hh = n // 2, n % 2
            g0 = NG * (c % 2) + 8 * (c // 2) + 4 * hh
            dg = slice(g0, g0 + 4)
            table(c_pow[:, dg, :], par_c, dg, tc[:, 0, dg, :], tc[:, 1, dg, :], CH).then_inc(S["cpow_ready"], 1)
            dve.wait_ge(S["cpow_ready"], n + 1)

        def r_add(i):
            dve.wait_ge(pack_s, 32)
            if i:
                dve.wait_ge(S["r_added"], i)
            tt(d_diag[:, :, :], ident[0:H, None, 0:H].broadcast_to([H, 8, H]),
               d_skip[:, 8 * i:8 * i + 8, None].broadcast_to([H, 8, H]), M).then_inc(S["dve_step"], 1)
            dve.wait_ge(S["dve_step"], step())
            dve.wait_ge(S["h_evac"], 4 * i + 4)
            tt(r_rows[:, i % 2, :, 128:144], r_rows[:, i % 2, :, 128:144], r_rows[:, i % 2, :, 0:16], AD).then_inc(S["dve_step"], 1)
            dve.wait_ge(S["dve_step"], step())
            tt(r_rows[:, i % 2, :, 128:144], r_rows[:, i % 2, :, 128:144], d_diag[:, :, :], AD).then_inc(S["r_added"], 1)

        def b_chunk(n):
            dve.wait_ge(par_b_s, 16)
            if n < 2:
                dve.wait_ge(S["h_ready"], 2 * KD)
            if n >= 2:
                dve.wait_ge(S["b_Tmm"], n - 1)
            d = n // 8
            dg = slice(4 * n, 4 * n + 4)
            f = [(x[:, 8:0:-1, dg] if d == 0 else x[:, 1:9, dg]).rearrange("p e g -> p g e") for x in (e_re, e_im)]
            table(b_half[:, n % 2, :], par_b, dg, f[0], f[1], CH).then_inc(S["b_ready"], 1)
            dve.wait_ge(S["b_ready"], n + 1)

        def mod_acc_piece(m):
            n, (k, c) = 16 + m, mod_rest(m)
            dve.wait_ge(piece2_full[n % N_PIECE], 16 * (m // N_PIECE + 1))
            a = mod_acc[:, c * D:(c + 1) * D] if c < 3 else acc_g2[:, :]
            if k == 0:
                v.tensor_scalar(a, piece[:, n % N_PIECE, :], csil[:, 0:1], None, M).then_inc(S["piece_used_dve"], 1)
            else:
                dve.wait_ge(S["piece_used_dve"], m - 2 if c < 3 else m)
                stt(a, piece[:, n % N_PIECE, :], csil[:, k:k + 1], a, M, AD).then_inc(S["piece_used_dve"], 1)

        for n in range(9):
            c_half(n)
        dve.wait_ge(S["piece_used_pe"], 16)
        for b in range(2, 4):
            v.tensor_copy(mod_rows[:, 512 * b:512 * (b + 1)], bank[4 + b][0:2, :]).then_inc(S["mod_rows_ready"], 1)
        dve.wait_ge(S["mod1_T"], 1)
        dve.wait_ge(S["vec_ready"], 1)
        tt(mod1[:, :].rearrange("p (f s) -> p f s", s=2), bank[4][:, 0:32].rearrange("p (f s) -> p f s", s=2),
           vecT[:, V_BMOD:V_BMOD + 16, None].broadcast_to([P, 16, 2]), AD).then_inc(S["dve_step"], 1)
        dve.wait_ge(S["dve_step"], step())
        stt(gs1[:, :].rearrange("p (f s) -> p f s", s=2), mod1[:, 16:32].rearrange("p (f s) -> p f s", s=2), 1.0,
            vecT[:, V_N1:V_N1 + KD, None].broadcast_to([P, KD, 2]), AD, M).then_inc(S["gs_ready"], 1)
        for n in range(9, 12):
            c_half(n)
        for m in range(4):
            mod_acc_piece(m)
        for m in range(4, 8):
            mod_acc_piece(m)
        c_half(12)
        c_half(13)
        r_add(0)
        for m in range(8, 12):
            mod_acc_piece(m)
        c_half(14)
        c_half(15)
        r_add(1)
        b_chunk(0)
        b_chunk(1)
        for m in range(12, 16):
            mod_acc_piece(m)
        r_add(2)
        for m in range(16, 20):
            mod_acc_piece(m)
        r_add(3)
        mod_acc_piece(20)
        for r in range(4):
            dve.wait_ge(S["u_T"], r + 1)
            shape = [P, 8, 2 * NC]
            tt(u_pack[:, 8 * r:8 * r + 8, :], bank[(4, 7)[r % 2]][:, :].rearrange("p (g c) -> p g c", g=8),
               bu[:, 8 * r:8 * r + 8, None].broadcast_to(shape), AD).then_inc(S["u_packed"], 1)

        def tile_bank(tile):
            dve.wait_ge(S["mm_done"], tile + 1)
            return bank[tile % 4][:, 0:NT]

        def conv_tile(tile):
            qq, i = tile // 6, tile % 6
            f = i % 2
            if i < 4:
                dve.wait_ge(S["evac_act"], evac_count(6 * qq + f)[1])
                c0 = V_CONV + 2 * qq + f
                tap = [vecT[:, c0 + KC * j:c0 + KC * j + 1] for j in range(3)]
                stt(gv[:, f, :], tile_bank(tile), bias_of(C_XIN + 256 * qq + P * f), gv[:, f, :], AD, M
                    ).then_inc(S["evac_dve"], 1)
                dve.wait_ge(*evac_count(tile))
                v.tensor_scalar(cv[:, f, :], gv[:, f, :], tap[1], None, M).then_inc(S["dve_step"], 1)
                dve.wait_ge(S["dve_step"], step())
                rows = [x[:, f, :].rearrange("p (r c) -> p r c", c=GRID_W) for x in (gv, cv)]
                stt(rows[1][:, :, 1:], rows[0][:, :, :-1], tap[0], rows[1][:, :, 1:], M, AD).then_inc(S["dve_step"], 1)
                dve.wait_ge(S["dve_step"], step())
                stt(rows[1][:, :, :-1], rows[0][:, :, 1:], tap[2], rows[1][:, :, :-1], M, AD).then_inc(S["dve_step"], 1)
                dve.wait_ge(S["dve_step"], step())
            else:
                stt(gbv[:, 2 * qq + f, :], tile_bank(tile), bias_of(C_GB + 256 * qq + P * f), cv[:, f, :], AD, M
                    ).then_inc(S["evac_dve"], 1)

        def scan_coefficients():
            v.tensor_copy(q(AR[0]), e_re[:, 8, :]).then_inc(S["dve_step"], 1)
            dve.wait_ge(S["dve_step"], step())
            v.tensor_scalar(q(T0), e_im[:, 8, :], sgn[:, 0:1], -1.0, M, M).then_inc(S["dve_step"], 1)
            dve.wait_ge(S["dve_step"], step())
            for k in range(5):
                v.tensor_scalar(q(QI[k]), q(T0), sgn[:, 0:1], None, M).then_inc(S["dve_step"], 1)
                dve.wait_ge(S["dve_step"], step())
                if k < 4:
                    tt(q(T1), q(AR[k]), q(AR[k]), M)
                    tt(q(T2), q(T0), q(T0), M)
                    tt(q(T3), q(AR[k]), q(T0), M).then_inc(S["dve_step"], 1)
                    dve.wait_ge(S["dve_step"], step())
                    tt(q(AR[k + 1]), q(T1), q(T2), SU)
                    tt(q(T0), q(T3), q(T3), AD).then_inc(S["dve_step"], 1)
                    dve.wait_ge(S["dve_step"], step())

        def advance(src, add, dst, k, g0, n_g, n):
            shape = [P, n_g, n]
            gs = slice(g0, g0 + n_g)
            t_a, t_b = (x[:, 0:n_g * n].rearrange("p (g n) -> p g n", g=n_g) for x in (tA, tB))
            tt(t_a, src, sm[:, AR[k], gs, None].broadcast_to(shape), M)
            lo, up = slice(0, NS), slice(NS, P)
            tt(t_b[lo], src[up], sm[up, QI[k], gs, None].broadcast_to([NS, n_g, n]), M)
            tt(t_b[up], src[lo], sm[lo, QI[k], gs, None].broadcast_to([NS, n_g, n]), M).then_inc(S["dve_step"], 1)
            dve.wait_ge(S["dve_step"], step())
            tt(t_a, t_a, t_b, AD).then_inc(S["dve_step"], 1)
            dve.wait_ge(S["dve_step"], step())
            return tt(dst, t_a, add, AD)

        def up(k, g0):
            s = 1 << k
            n = NC // s
            n_g = min(DG, 512 // n)
            Xv = X[:, :, :].rearrange("p g (n s) -> p g n s", s=2 * s)
            right = Xv[:, g0:g0 + n_g, :, 2 * s - 1]
            advance(Xv[:, g0:g0 + n_g, :, s - 1], right, right, k, g0, n_g, n).then_inc(S["dve_step"], 1)
            dve.wait_ge(S["dve_step"], step())
            return g0 + n_g

        for tile in range(2, T_OA):
            i = tile - 3
            if 0 <= i < 7:
                b_chunk(2 * i + 2)
                b_chunk(2 * i + 3)
            if evac_by[tile] == "dve":
                conv_tile(tile)
            if tile == 6:
                for m in range(21, 24):
                    mod_acc_piece(m)
            if tile == 10:
                scan_coefficients()
        for g0 in (0, 16, 32):
            dve.wait_ge(S["x_evac"], g0 // 4 + 4)
            up(0, g0)

        dve.wait_ge(S["x_evac"], 16)
        up(0, 48)
        for k in range(1, 4):
            g0 = 0
            while g0 < DG:
                g0 = up(k, g0)
        last = X[:, :, 2 * NC - 1:2 * NC]
        dve.wait_ge(S["r_added"], 4)
        dve.wait_ge(r_out_s[0], 32)
        dve.wait_ge(r_out_s[1], 32)
        advance(X[:, :, NC + NC // 2 - 1:NC + NC // 2], last, p_st[:, :, 0:1], 4, 0, DG, 1).then_inc(S["dve_step"], 1)
        dve.wait_ge(S["dve_step"], step())
        for k in range(4, -1, -1):
            s = 1 << k
            n = NC // (2 * s)
            n_g = min(DG, 512 // n)
            Xv = X[:, :, 0:NC].rearrange("p g (n s) -> p g n s", s=2 * s)
            Pv = p_st[:, :, :].rearrange("p g (n s) -> p g n s", s=2 * s)
            for g0 in range(DG - n_g, -1, -n_g):
                gs = slice(g0, g0 + n_g)
                done = advance(Pv[:, gs, :, 0], Xv[:, gs, :, s - 1], Pv[:, gs, :, s], k, g0, n_g, n)
                if k == 0:
                    done.then_inc(S["back_done" if g0 else "scan_done"], 1)
                    if g0:
                        dve.wait_ge(S["back_done"], 1)
                else:
                    done.then_inc(S["dve_step"], 1)
                    dve.wait_ge(S["dve_step"], step())
        def lo(n):
            qq, half = n_native + n // 2, n % 2
            dve.wait_ge(S["hi_done"], n + 1)
            if qq < n_pre:
                split_lo(qq % N_RAW, half, units[qq][0])
            else:
                split_lo(ffn_slot[qq - n_pre], half, (KD, KD, 2)[qq - n_pre])

        def split_lo(slot, half, k):
            if k > 2:
                a, h_, o = (half_of(x, slot, half, k) for x in (raw_slot, w_hi, w_lo))
            else:
                a, h_, o = (x[slot][:, half * HALF:(half + 1) * HALF] for x in (raw_slot, w_hi, w_lo))
            tt(o, a, h_.bitcast(F32), SU).then_inc(S["lo_done"], 1)

        dve.wait_ge(S["mod2_mm"], 1)
        tt(mod2[:, 0:24], bank[4][:, 0:24], vecT[:, V_BMOD + 16:V_BMOD + 40], AD).then_inc(S["mod2_ready"], 1)
        dve.wait_ge(S["mod2_ready"], 1)
        stt(gs2[:, :], mod2[:, 2 * KD:3 * KD], 1.0, vecT[:, V_N2:V_N2 + KD], AD, M).then_inc(S["dve_step"], 1)
        dve.wait_ge(S["dve_step"], step())
        dve.wait_ge(S["h_hi_ready"], 1)
        tt(h_lo[:, :, :].rearrange("p k (c j) -> p k c j", j=CH), hT[:, :, :, 0, :].rearrange("p k j c -> p k c j"),
           h_hi[:, :, :].bitcast(F32).rearrange("p k (c j) -> p k c j", j=CH), SU).then_inc(S["h_lo_ready"], 1)
        for n in range(8):
            lo(n)
        dve.wait_ge(S["s_hi_done"], 1)
        tt(s_lo[:, :, :], s32[:, :, :], s_hi[:, :, :].bitcast(F32), SU).then_inc(S["s_ready"], 1)
        for n in range(8, G0 + 4):
            lo(n)

        def m_lo_of(f):
            dve.wait_ge(S["m_hi_done"], f + 1)
            tt(m_lo[:, f, :], mrg[:, f % 2, :], m_hi[:, f, :].bitcast(F32), SU).then_inc(S["m_ready"], 1)

        for qq in range(4):
            if qq == 0:
                lo(G0 + 4)
                lo(G0 + 5)
            else:
                m_lo_of(2 * qq - 2)
                m_lo_of(2 * qq - 1)
            for f in range(2):
                tile = T_GLU + 4 * qq + 2 + f
                dve.wait_ge(S["evac_act"], evac_count(tile - 2)[1])
                if qq:
                    dve.wait_ge(S["mul_done"], 2 * qq + f - 1)
                b = V_BGLU + 2 * qq + f
                stt(yb[:, f, :], tile_bank(tile), vecT[:, b:b + 1], sg[:, f, :], AD, M).then_inc(S["evac_dve"], 1)
            lo(G0 + 6 + 2 * qq)
            lo(G0 + 7 + 2 * qq)
            mod_acc_piece(24 + qq)
        m_lo_of(6)
        m_lo_of(7)
        dve.wait_ge(S["xT_evac"], 4)
        for m in range(28, 31):
            mod_acc_piece(m)
        for f in range(KD):
            stt(x1T[:, f, :], tile_bank(T_WO + f), mod2[:, f:f + 1], xT[:, f, :], M, AD).then_inc(S["evac_dve"], 1)
            for n in {3: (14, 15, 16, 17), 4: (18,), 5: (19,)}.get(f, ()):
                lo(G0 + n)
            if f == 3:
                mod_acc_piece(31)
            if f == 6:
                dve.wait_ge(S["g2_mm"], 1)
                tt(mod2[:, 24:32], bank[5][:, 0:8], vecT[:, V_BMOD + 40:V_BMOD + 48], AD).then_inc(S["g2_ready"], 1)
        dve.wait_ge(S["sqrt2_done"], 1)
        v.reciprocal(bc[:, 1, :], bc[:, 0, :]).then_inc(S["dve_step"], 1)
        dve.wait_ge(S["dve_step"], step())

        def norm2(k):
            stt(x1g[:, k, :], x1T[:, k, :], gs2[:, k:k + 1], bc[:, 1, :], M, M).then_inc(S["t2_ready"], 1)

        def h2_lo_of(k):
            dve.wait_ge(S["h2_hi_done"], k + 1)
            stt(h2_lo[:, k, :], x1g[:, k, :], mod2[:, KD + k:KD + k + 1], h2_hi[:, k, :].bitcast(F32), AD, SU
                ).then_inc(S["h2_ready"], 1)

        norm2(0)
        norm2(1)
        for k in range(KD):
            h2_lo_of(k)
            if k + 2 < KD:
                norm2(k + 2)

        def dve_turn(turn, first=False, last=False):
            def split(j):
                for half in range(2):
                    dve.wait_ge(S["hi_done"], turn * 6 + (split1 + 2 * j + half + 1 - (4 if last else 0)))
                    split_lo(ffn_slot[0 if last else j], half, (KD, KD, 2)[j])

            s0 = 2 if last else 0
            split(2 if last else 0)
            for f in range(2):
                dve.wait_ge(S["silu_done"], turn * 2 + (f + 1))
                dve.wait_ge(S["up_mm"], turn * 2 + (f + 1))
                if not first:
                    dve.wait_ge(S["act_ready"], turn * 2 + (f - 1))
                tt(gu[:, f, :], bank[2 + f][:, 0:NT], silu_g[:, f, :], M).then_inc(S["prod_done"], 1)
            if not last:
                split(1)
            for f in range(2):
                if not first and not last:
                    dve.wait_ge(S["fo_used"], turn * 2 + (f - 1))
                dve.wait_ge(S["prod_done"], turn * 2 + (f + 1))
                v.tensor_copy(a_hi[:, s0 + f, :], gu[:, f, :]).then_inc(S["a_hi_done"], 1)
                dve.wait_ge(S["a_hi_done"], turn * 2 + (f + 1))
                tt(a_lo[:, s0 + f, :], gu[:, f, :], a_hi[:, s0 + f, :].bitcast(F32), SU).then_inc(S["act_ready"], 1)
            if not last:
                split(2)

        dve_turn(0, first=True)
        with dve.Fori(1, n_turn - 1) as turn:
            dve_turn(turn)
        dve_turn(n_turn - 1, last=True)
        for f in range(KD):
            dve.wait_ge(S["x2_mm"], 2 * (f // 2) + 2)
            stt(x1T[:, f, :], bank[4 + f // 2][:, (f % 2) * NT:(f % 2 + 1) * NT], mod2[:, 3 * KD + f:3 * KD + f + 1],
                x1T[:, f, :], M, AD).then_inc(S["x2_ready"], 1)
            dve.wait_ge(S["x2_ready"], f + 1)
            v.tensor_scalar(x1g[:, f, :], x1T[:, f, :], vecT[:, V_FG + f:V_FG + f + 1], None, M).then_inc(S["xg_ready"], 1)
        dve.wait_ge(S["sqrt3_done"], 1)
        v.reciprocal(rstd[:, 0:2], srow[:, 0:2]).then_inc(S["rstd3_done"], 1)
        dve.wait_ge(S["rstd3_done"], 1)
        dve.wait_ge(S["fin_T"], KD)
        for i in range(2):
            v.tensor_scalar(fin[:, i, 0:DC], bank[2 * i][:, :], rstd[:, i:i + 1], None, M).then_inc(S["fin_dve"], 1)

    @block.tensor
    def _(pe):
        mm = nc.tensor.matmul

        pe.wait_ge(S["consts"], n_const)
        pe.wait_ge(rows_in_s, 32)
        nc.tensor.transpose(bank[7][:, P:P + 16], crow_in[:, :], ident[0:16, 0:16]).then_inc(S["rows_T"], 1)
        nc.tensor.transpose(bank[7][:, 0:P], rows_in[:, :], ident[:, :]).then_inc(S["rows_T"], 1)

        def mod_part(n):
            pe.wait_ge(piece_full[n % N_PIECE], 16 * (n // N_PIECE + 1))
            if n == 1:
                pe.wait_ge(S["vec_ready"], 1)
            k = n // 2
            for j in range(2):
                last = mm(bank[4 + 2 * (n % 2) + j][0:2, :], csil[:, k:16:KD], piece[:, n % N_PIECE, 512 * j:512 * (j + 1)],
                          start=k == 0, stop=k == KD - 1)
            last.then_inc(S["piece_used_pe"], 1)

        def h_cols(c):
            pe.wait_ge(S["cpow_ready"], 2 * c + 2)
            pe.wait_ge(par_b_s, 16)
            if c == 1:
                pe.wait_ge(S["gs_ready"], 1)
            if c >= 2:
                pe.wait_ge(S["h_evac"], 2 * c - 2)
            for g in range(8):
                dg = NG * (c % 2) + 8 * (c // 2) + g
                last = mm(bank[h_banks(c)[g // 4]][0:H, (g % 4) * P:(g % 4 + 1) * P], par_b[:, 0, dg, :], c_pow[:, dg, :],
                          start=True, stop=True)
            last.then_inc(S["h_mm"], 1)

        pe.wait_ge(S["csil_ready"], 1)
        for n in range(6):
            mod_part(n)
        pe.wait_ge(S["x_scaled"], 4)
        for k in range(KD):
            if k >= 4:
                pe.wait_ge(S["xn_evac"], k - 3)
            for tt in range(4):
                last = nc.tensor.transpose(bank[k % 4][:, tt * P:(tt + 1) * P], xtok[:, tt, k * P:(k + 1) * P], ident[:, :])
            last.then_inc(S["xn_mm"], 1)
            if k % 2:
                mod_part(6 + k // 2)
        for n in range(10, 16):
            mod_part(n)
        pe.wait_ge(S["mod_rows_ready"], 4)
        for f in range(2 * KD):
            last = nc.tensor.transpose(bank[4][:, 2 * f:2 * f + 2], mod_rows[:, f * P:(f + 1) * P], ident[0:2, 0:2])
        last.then_inc(S["mod1_T"], 1)
        h_cols(0)

        def raw_ready(q):
            pe.wait_ge(raw_full[q % N_RAW], raw_count[q])

        pe.wait_ge(S["xn_evac"], KD)
        for half in range(2):
            raw_ready(half)
            wu = kview(raw[:, half, :], KD)
            for k in range(KD):
                pe.wait_ge(S["h_ready"], 2 * k + 2)
                for m in range(4):
                    last = mm(bank[2 * half + m // 2][:, 256 * (m % 2):256 * (m % 2) + 256], hT[:, k, 2 * m:2 * m + 2, :, :].rearrange("p j s c -> p (j s c)"),
                              wu[:, k, :], start=k == 0 and m % 2 == 0, stop=k == KD - 1, skip_group_check=True)
            last.then_inc(S["u_mm"], 1)
            if half == 0:
                for c in range(1, 4):
                    h_cols(c)

        tile = [0]

        def open_tile():
            n = tile[0]
            tile[0] += 1
            if n < 4:
                pe.wait_ge(S["u_rows"], 8 if n < 2 else 16)
            else:
                pe.wait_ge(*evac_count(n - 4))
            return bank[n % 4][:, 0:NT]

        def native(q, f, k_n, rhs):
            raw_ready(q)
            wv, o = kview(raw[:, q % N_RAW, :], k_n), open_tile()
            for k in range(k_n):
                last = mm(o, wv[:, k, f * P:(f + 1) * P], rhs[:, k], start=k == 0, stop=k == k_n - 1)
            last.then_inc(S["mm_done"], 1)

        def ssm_pair(i):
            if i < 8:
                for n in (2 * i, 2 * i + 1):
                    pe.wait_ge(S["b_ready"], n + 1)
                    if n >= 2:
                        pe.wait_ge(S["b_Tevac"], n - 1)
                    for g in range(4):
                        last = nc.tensor.transpose(bank[5 + n % 2][:, g * P:(g + 1) * P], b_half[:, n % 2, g * P:(g + 1) * P],
                                                   ident[:, :])
                    last.then_inc(S["b_Tmm"], 1)
            if i >= 1:
                for n in (2 * i - 2, 2 * i - 1):
                    pe.wait_ge(S["b_Tevac"], n + 1)
                    if n >= 2:
                        pe.wait_ge(S["x_evac"], n - 1)
                    for g in range(4):
                        dg = 4 * n + g
                        cols = u_pack[:, dg % NG, :].rearrange("p (s c) -> p s c", s=2)
                        if dg >= NG:
                            cols = cols[:, :, ::-1]
                        last = mm(bank[(4, 7)[n % 2]][:, g * 64:(g + 1) * 64], b_T[:, n % 4, g * P:(g + 1) * P], cols,
                                  start=True, stop=True)
                    last.then_inc(S["x_mm"], 1)

        h_lat = hT[:, :, :, 0, :].rearrange("p k j c -> p k c j")
        for n in range(T_OA):
            native(U0_GC + n // 2, n % 2, KD, h_lat)
            if n < 2:
                h_cols(4 + 2 * n)
                h_cols(5 + 2 * n)
            if n == 2:
                pe.wait_ge(S["h_evac"], 16)
                pe.wait_ge(S["u_rows"], 16)
                for r in range(4):
                    if r >= 2:
                        pe.wait_ge(S["u_packed"], r - 1)
                    for g in range(8):
                        last = nc.tensor.transpose(bank[(4, 7)[r % 2]][:, g * 64:(g + 1) * 64],
                                                   v_rows[:, 8 * r + g, :, :].rearrange("c j h -> c (j h)"),
                                                   ident[0:64, 0:64])
                    last.then_inc(S["u_T"], 1)
                pe.wait_ge(S["u_packed"], 4)
            if 2 <= n <= 10:
                ssm_pair(n - 2)
        pe.wait_ge(*evac_count(T_OA - 1))
        for n in range(KD):
            native(U0_OA + n // 4, n % 4, KC, gbv)
            if n == 4:
                pe.wait_ge(S["piece_used_dve"], 24)
                pe.wait_ge(S["x_evac"], 16)
            for c in range(6 * n - 24, 6 * n - 18) if n >= 4 else ():
                last = mm(bank[4][:, c:c + 1], mod_acc[:, c * P:(c + 1) * P], ones[:, 0:1], start=True, stop=True)
        last.then_inc(S["mod2_mm"], 1)

        def ssm_output():
            pe.wait_ge(S["mod2_ready"], 1)
            pe.wait_ge(S["scan_done"], 1)
            pe.wait_ge(S["rev_ready"], 1)
            pe.wait_ge(toep_s, 16 * CH)
            for g in range(NG):
                gq, gr = g // 8, g % 8
                o = bank[5 + gr // 4][NC * gq:NC * gq + NC, (gr % 4) * P:(gr % 4 + 1) * P]
                mm(o, u_pack[:, g, 0:NC], toep[:, g, :], start=True, stop=False)
                mm(o, p_st[:, g, :], c_pow[:, g, :], start=False, stop=False)
                last = mm(o, p_rev[:, g, :], c_pow[:, NG + g, :], start=False, stop=True)
            last.then_inc(S["y_mm"], 1)

        def ssm_output_T():
            pe.wait_ge(S["y_evac"], 2)
            for i in range(CH):
                last = nc.tensor.transpose(bank[(4, 7)[i // 4]][:, (i % 4) * P:(i % 4 + 1) * P],
                                           y_rows[:, i, :, :].rearrange("p g h -> p (g h)"), ident[:, :])
            last.then_inc(S["s_T"], 1)

        def three(o, wh, wl, xh, xl, first, final):
            mm(o, wh, xh, start=first, stop=False, skip_group_check=True)
            mm(o, wh, xl, start=False, stop=False, skip_group_check=True)
            return mm(o, wl, xh, start=False, stop=final, skip_group_check=True)

        def split_tile(slot, half, f, k_n, x_hi, x_lo):
            o = open_tile()
            wh, wl = (half_of(x, slot, half, k_n)[:, :, f * P:(f + 1) * P] for x in (w_hi, w_lo))
            for k in range(k_n):
                last = three(o, wh[:, k, :], wl[:, k, :], x_hi[:, k, :], x_lo[:, k, :], k == 0, k == k_n - 1)
            last.then_inc(S["mm_done"], 1)

        for n in range(2 * KD):
            if n == Y_AT:
                ssm_output()
            if n == S_AT:
                ssm_output_T()
            if n < F_SPLIT:
                native(U0_GATE + n // 2, n % 2, KD, h_lat)
                continue
            pe.wait_ge(S["h_lo_ready"], 1)
            pe.wait_ge(S["lo_done"], n - F_SPLIT + 1)
            split_tile((U0_GATE + n // 2) % N_RAW, n % 2, 0, KD, h_hi, h_lo)

        pe.wait_ge(S["s_ready"], 1)
        for q in range(4):
            for half in range(2):
                pe.wait_ge(S["lo_done"], G0 + 2 * q + half + 1)
                for f in range(2):
                    split_tile((U0_GLU + q) % N_RAW, half, f, KC, s_hi, s_lo)
            if q == 0:
                pe.wait_ge(xtok2_s, 16)
            if q >= 2:
                pe.wait_ge(S["xT_evac"], q - 1)
            for k in range(2):
                for tt in range(2):
                    last = nc.tensor.transpose(bank[6 - q % 2][:, k * NT + tt * P:k * NT + (tt + 1) * P],
                                               xtok2[:, tt, (2 * q + k) * P:(2 * q + k + 1) * P], ident[:, :])
            last.then_inc(S["xT_mm"], 1)
        def sum_squares(f):
            pe.wait_ge(S["sq_ready"], f + 1)
            mm(bank[4][:, 0:NT], ones[:, :], sq[:, f % 4, :], start=f == 0, stop=f == KD - 1).then_inc(S["ss_mm"], 1)

        o4 = [open_tile() for f in range(4)]
        for k0, k1 in ((0, 6), (6, KD)):
            for f in range(4):
                pe.wait_ge(S["lo_done"], G0 + 8 + f + 1)
                wh, wl = (half_of(x, (U0_WO + f // 2) % N_RAW, f % 2, KD) for x in (w_hi, w_lo))
                for k in range(k0, k1):
                    if f == 0:
                        pe.wait_ge(S["m_ready"], k + 1)
                    last = three(o4[f], wh[:, k, :], wl[:, k, :], m_hi[:, k, :], m_lo[:, k, :], k == 0, k == KD - 1)
                if k1 == KD:
                    last.then_inc(S["mm_done"], 1)
        for f in range(4, KD):
            pe.wait_ge(S["lo_done"], G0 + 8 + f + 1)
            split_tile((U0_WO + f // 2) % N_RAW, f % 2, 0, KD, m_hi, m_lo)
            for f2 in ((0, 1), (2, 3), (4,), (5,))[f - 4]:
                sum_squares(f2)
            if f == 6:
                pe.wait_ge(S["piece_used_dve"], 32)
                pe.wait_ge(S["xT_evac"], 4)
                for c in range(KD):
                    last = mm(bank[5][:, c:c + 1], acc_g2[:, c * P:(c + 1) * P], ones[:, 0:1], start=True, stop=True)
                last.then_inc(S["g2_mm"], 1)
        sum_squares(KD - 2)
        sum_squares(KD - 1)
        pe.wait_ge(S["zrow_ready"], 1)
        pe.wait_ge(S["g2_ready"], 1)
        for b in (5, 6, 7, 4):
            if b == 4:
                pe.wait_ge(S["sqrt2_done"], 1)
            mm(bank[b][:, :], zrow[:, 0:P], zrow[:, :], start=True, stop=False, skip_group_check=True)

        def ffn_part(j, f, k):
            wh, wl = (half_of(x, ffn_slot[j], f, KD) for x in (w_hi, w_lo))
            return three(bank[2 * j + f][:, 0:NT], wh[:, k, :], wl[:, k, :], h2_hi[:, k, :], h2_lo[:, k, :],
                         k == 0, k == KD - 1)

        def out_parts(f, e, slot):
            return (x[slot][:, f * HALF + e * P:f * HALF + (e + 1) * P] for x in (w_hi, w_lo))

        def acc(e):
            return bank[4 + e // 2][:, (e % 2) * NT:(e % 2 + 1) * NT]

        for j in range(2):
            for k in range(KD):
                pe.wait_ge(S["h2_ready"], k + 1)
                for f in range(2):
                    if k == 0:
                        pe.wait_ge(S["lo_done"], split0 + 2 * j + f + 1)
                        pe.wait_ge(*evac_count(T_WO + 4 + 2 * j + f))
                    last = ffn_part(j, f, k)
                    if k == KD - 1:
                        last.then_inc(S[("gate_mm", "up_mm")[j]], 1)
        with pe.Fori(1, n_turn) as turn:
            for j in range(2):
                for f in range(2):
                    pe.wait_ge(S["lo_done"], turn * 6 + (split1 - 6 + 2 * j + f + 1))
                    pe.wait_ge(S[("silu_done", "prod_done")[j]], turn * 2 + (f - 1))
                    for k in range(KD):
                        last = ffn_part(j, f, k)
                    last.then_inc(S[("gate_mm", "up_mm")[j]], 1)
            for f in range(2):
                pe.wait_ge(S["act_ready"], turn * 2 + (f - 1))
                pe.wait_ge(S["lo_done"], turn * 6 + (split1 - 6 + 4 + f + 1))
                for e in range(KD):
                    wh, wl = out_parts(f, e, ffn_slot[2])
                    last = three(acc(e), wh, wl, a_hi[:, f, :], a_lo[:, f, :], False, False)
                last.then_inc(S["fo_used"], 1)
        pe.wait_ge(S["act_ready"], 2 * n_turn)
        pe.wait_ge(S["lo_done"], split1 + 6 * (n_turn - 1) + 2)

        def fin_T(f):
            pe.wait_ge(S["xg_ready"], f + 1)
            for tt in range(2):
                last = nc.tensor.transpose(bank[2 * tt + f // 4][:, (f % 4) * P:(f % 4 + 1) * P],
                                           x1g[:, f, tt * P:(tt + 1) * P], ident[:, :])
            last.then_inc(S["fin_T"], 1)

        def fin_squares(f):
            pe.wait_ge(S["sqf_ready"], f + 1)
            if f == 0:
                pe.wait_ge(S["x2_ready"], 2)
            for tt in range(2):
                last = mm(bank[4][:, tt:tt + 1], sq[:, f % 4, tt * P:(tt + 1) * P], ones[:, 0:1],
                          start=f == 0 and tt == 0, stop=f == KD - 1, skip_group_check=True)
            last.then_inc(S["ssf_mm"], 1)

        for e in range(KD):
            for f in range(2):
                wh, wl = out_parts(f, e, ffn_slot[0])
                last = three(acc(e), wh, wl, a_hi[:, 2 + f, :], a_lo[:, 2 + f, :], False, f == 1)
            last.then_inc(S["x2_mm"], 1)
            if e >= 3:
                fin_T(e - 3)
                fin_squares(e - 3)
        for f in range(KD - 3, KD):
            fin_T(f)
            fin_squares(f)


def kernel(**inputs):
    import numpy as np
    import concourse.bacc as bacc
    from concourse.bass_utils import run_bass_kernel_spmd

    a = {k: np.asarray(v) for k, v in inputs.items()}
    sg = {k: a[k][0] for k in ("w_mod", "w_in", "w_out_a", "w_glu", "w_o", "w_ff_in", "w_ff_out")}
    b_in = a["b_in"][0].reshape(-1, P)
    vec_rows = np.concatenate([a["b_mod"][0].reshape(-1, P), b_in[:C_U // P], b_in[C_U // P + KC:],
                               a["b_glu"][0].reshape(-1, P), a["norm1_g"][0].reshape(-1, P),
                               a["norm2_g"][0].reshape(-1, P), a["final_g"].reshape(-1, P),
                               a["conv_w"][0].reshape(-1, P)])

    def rows(z):
        z = z.reshape(DG, NS).T
        return np.concatenate([z, z])

    def b_rows(re, im):
        re, im = (z.reshape(DG, NS, H).transpose(1, 0, 2) for z in (re, im))
        return np.stack([np.concatenate([re, im]), np.concatenate([im, re])], axis=1)

    log_dt = np.repeat(a["log_dt"][0].reshape(1, DG), P, axis=0)
    ins = {
        "x": a["x"][0], "ctx": a["ctx"][0], **sg, "vec_rows": vec_rows,
        "c_rows": np.concatenate([a["c"].reshape(KD, P), a["c_ctx"].reshape(KD, P)]),
        "lam_pack": np.stack([rows(a["lam_re"][0]), rows(a["lam_im"][0]), log_dt], axis=1),
        "b_pack": b_rows(a["b_re"][0], a["b_im"][0]),
        "c_pack": b_rows(a["c_re"][0].transpose(0, 1, 3, 2), a["c_im"][0].transpose(0, 1, 3, 2)),
        "bu_pack": np.tile(a["b_in"][0][C_U:C_U + DC].reshape(NG, H).T, (CH, 1)),
        "d_pack": a["d_skip"][0].reshape(NG, H).T,
    }
    nc = bacc.Bacc("TRN2", target_bir_lowering=False, num_devices=1)
    arrays, t = {}, {}
    for name, z in ins.items():
        z = np.ascontiguousarray(z)
        arrays[f"in_{name}"] = z
        t[name] = nc.dram_tensor(f"in_{name}", z.shape, mybir.dt.from_np(z.dtype), kind="ExternalInput").ap()
    out = nc.dram_tensor("out", (NT, D), F32, kind="ExternalOutput").ap()
    with ExitStack() as ctx:
        build(nc, t, out, ctx)
    r = run_bass_kernel_spmd(nc, [arrays], core_ids=[0])
    return r.results[0]["out"].reshape(1, NT, D)
```
